# Optimizing a Trainium2 kernel written in Bass

```python
import jax, jax.numpy as jnp
from jax import lax
import numpy as np

D_MODEL = 1024
BATCH = 1
SEQ = 512
DEPTH = 2

NORM_EPS = 1e-6
ATT_GROUPS = ((128, 1), (512, 4), (2048, 16))
N_ATT_GROUPS = 3
ATT_SLOTS = 4
ATT_HEAD_DIM = 64
ATT_WIDTH = ATT_SLOTS * ATT_HEAD_DIM
ATT_BLOCK = 128
ALIBI_MAX_EXP = 8.0
DN_HEADS = 4
DN_HEAD_DIM = 128
DN_WIDTH = DN_HEADS * DN_HEAD_DIM
DN_CONV = 4
DN_CHUNK = 64
S5_GROUP = 16
S5_GROUPS = 16
S5_WIDTH = S5_GROUPS * S5_GROUP
S5_STATE = 64
PEER_HEADS = 8
PEER_KEYS = 128
PEER_EXPERTS = PEER_KEYS * PEER_KEYS
PEER_TOPK = 16
PEER_KEY_DIM = 128
PEER_BLOCK = 128
PLE_DIM = 256

SPLIT_SIZES = (N_ATT_GROUPS * ATT_WIDTH, ATT_WIDTH, ATT_WIDTH, 3 * DN_WIDTH, DN_WIDTH, DN_HEADS, DN_HEADS, S5_WIDTH, 3 * D_MODEL)
IN_COLS = sum(SPLIT_SIZES)
SPLIT_IDX = tuple(int(c) for c in np.cumsum(SPLIT_SIZES)[:-1])

kernel_name = 'hybrid_dilated_deltanet_s5_peer_block'

def rms_norm(x, gain):
    xf = x.astype(jnp.float32)
    y = xf * lax.rsqrt(jnp.mean(xf * xf, axis=-1, keepdims=True) + NORM_EPS)
    return (y * gain.astype(jnp.float32)).astype(x.dtype)

def l2_normalize(x):
    return x * lax.rsqrt(jnp.sum(x * x, axis=-1, keepdims=True) + NORM_EPS)

def alibi_slopes():
    n = N_ATT_GROUPS * ATT_SLOTS
    s = 2.0 ** (-ALIBI_MAX_EXP * np.arange(1, n + 1) / n)
    return jnp.asarray(s.reshape(N_ATT_GROUPS, ATT_SLOTS), dtype=jnp.float32)

def dilated_window_attention(q, k, v, slopes, dilation, span):
    b, h, seq, dh = q.shape
    sub = seq // dilation
    nb = -(-sub // ATT_BLOCK)
    pad = nb * ATT_BLOCK - sub

    def to_blocks(t):
        t = t.reshape(b, h, sub, dilation, dh).transpose(0, 1, 3, 2, 4)
        t = jnp.pad(t, ((0, 0), (0, 0), (0, 0), (0, pad), (0, 0)))
        return t.reshape(b, h, dilation, nb, ATT_BLOCK, dh)

    def with_prev(t):
        prev = jnp.pad(t, ((0, 0), (0, 0), (0, 0), (1, 0), (0, 0), (0, 0)))[:, :, :, :-1]
        return jnp.concatenate([prev, t], axis=4)

    qb = to_blocks(q)
    kc = with_prev(to_blocks(k))
    vc = with_prev(to_blocks(v))
    s = jnp.einsum('bhrnqd,bhrnkd->bhrnqk', qb, kc)
    qpos = jnp.arange(ATT_BLOCK)[:, None]
    kpos = jnp.arange(2 * ATT_BLOCK)[None, :]
    rel = qpos + ATT_BLOCK - kpos
    blk = jnp.arange(nb)[:, None, None]
    valid = (rel >= 0) & (rel <= span) & (blk * ATT_BLOCK + kpos >= ATT_BLOCK)
    bias = -slopes[:, None, None, None, None] * (rel * dilation).astype(jnp.float32)
    s = jnp.where(valid, s + bias, -jnp.inf)
    m = jnp.max(s, axis=-1, keepdims=True)
    e = jnp.exp(s - m)
    den = jnp.sum(e, axis=-1, keepdims=True)
    o = jnp.einsum('bhrnqk,bhrnkd->bhrnqd', e, vc) / den
    lse = (m + jnp.log(den))[..., 0]
    o = o.reshape(b, h, dilation, nb * ATT_BLOCK, dh)[:, :, :, :sub].transpose(0, 1, 3, 2, 4).reshape(b, h, seq, dh)
    lse = lse.reshape(b, h, dilation, nb * ATT_BLOCK)[..., :sub].transpose(0, 1, 3, 2).reshape(b, h, seq)
    return o, lse

def dilated_attention_mixer(qa, ka, va, q_gain, k_gain):
    b, seq, _ = qa.shape
    q = rms_norm(qa.reshape(b, seq, N_ATT_GROUPS, ATT_SLOTS, ATT_HEAD_DIM), q_gain).astype(jnp.float32)
    q = (q * ATT_HEAD_DIM ** -0.5).transpose(2, 0, 3, 1, 4)
    k = rms_norm(ka.reshape(b, seq, ATT_SLOTS, ATT_HEAD_DIM), k_gain).astype(jnp.float32).transpose(0, 2, 1, 3)
    v = va.reshape(b, seq, ATT_SLOTS, ATT_HEAD_DIM).astype(jnp.float32).transpose(0, 2, 1, 3)
    slopes = alibi_slopes()
    outs, lses = [], []
    for g, (window, dilation) in enumerate(ATT_GROUPS):
        o, lse = dilated_window_attention(q[g], k, v, slopes[g], dilation, window // dilation)
        outs.append(o)
        lses.append(lse)
    wts = jax.nn.softmax(jnp.stack(lses), axis=0)
    o = jnp.sum(wts[..., None] * jnp.stack(outs), axis=0)
    return o.transpose(0, 2, 1, 3).reshape(b, seq, ATT_WIDTH).astype(qa.dtype)

def causal_depthwise_conv(x, w):
    ch = x.shape[-1]
    return lax.conv_general_dilated(x, w[:, None, :].astype(x.dtype), window_strides=(1,), padding=((DN_CONV - 1, 0),), dimension_numbers=('NWC', 'WIO', 'NWC'), feature_group_count=ch)

def chunked_gated_delta_rule(q, k, v, beta, g):
    b, h, seq, dk = q.shape
    dv = v.shape[-1]
    c = DN_CHUNK
    n = seq // c
    q = (q * dk ** -0.5).reshape(b, h, n, c, dk)
    k = k.reshape(b, h, n, c, dk)
    v = v.reshape(b, h, n, c, dv)
    beta = beta.reshape(b, h, n, c)
    g = jnp.cumsum(g.reshape(b, h, n, c), axis=-1)
    incl = jnp.tril(jnp.ones((c, c), dtype=bool))
    strict = jnp.tril(jnp.ones((c, c), dtype=bool), k=-1)
    decay = jnp.exp(jnp.where(incl, g[..., :, None] - g[..., None, :], -jnp.inf))
    k_beta = k * beta[..., None]
    lower = jnp.where(strict, jnp.einsum('bhnid,bhnjd->bhnij', k_beta, k) * decay, 0.0)
    eye = jnp.eye(c, dtype=q.dtype)
    t_inv = lax.linalg.triangular_solve(lower + eye, jnp.broadcast_to(eye, lower.shape), left_side=True, lower=True, unit_diagonal=True)
    u = jnp.einsum('bhnij,bhnje->bhnie', t_inv, v * beta[..., None])
    w = jnp.einsum('bhnij,bhnjd->bhnid', t_inv, k_beta * jnp.exp(g)[..., None])
    attn = jnp.where(incl, jnp.einsum('bhnid,bhnjd->bhnij', q, k) * decay, 0.0)
    q_dec = q * jnp.exp(g)[..., None]
    k_dec = k * jnp.exp(g[..., -1:] - g)[..., None]
    g_last = jnp.exp(g[..., -1])

    def step(state, inp):
        u_c, w_c, q_c, k_c, a_c, gl = inp
        v_new = u_c - jnp.einsum('bhcd,bhde->bhce', w_c, state)
        o_c = jnp.einsum('bhcd,bhde->bhce', q_c, state) + jnp.einsum('bhij,bhje->bhie', a_c, v_new)
        state = state * gl[..., None, None] + jnp.einsum('bhcd,bhce->bhde', k_c, v_new)
        return state, o_c

    xs = tuple(jnp.moveaxis(t, 2, 0) for t in (u, w, q_dec, k_dec, attn, g_last))
    state0 = jnp.zeros((b, h, dk, dv), q.dtype)
    _, o = lax.scan(step, state0, xs)
    return jnp.moveaxis(o, 0, 2).reshape(b, h, seq, dv)

def gated_deltanet_mixer(qkv, z, beta_logit, a_in, conv_w, a_log, dt_bias, out_gain):
    b, seq, _ = qkv.shape
    qkv = jax.nn.silu(causal_depthwise_conv(qkv, conv_w)).astype(jnp.float32)

    def heads(t):
        return t.reshape(b, seq, DN_HEADS, DN_HEAD_DIM).transpose(0, 2, 1, 3)

    q, k, v = (heads(t) for t in jnp.split(qkv, 3, axis=-1))
    q, k = l2_normalize(q), l2_normalize(k)
    beta = jax.nn.sigmoid(beta_logit.astype(jnp.float32)).transpose(0, 2, 1)
    g = -(jnp.exp(a_log.astype(jnp.float32)) * jax.nn.softplus(a_in.astype(jnp.float32) + dt_bias.astype(jnp.float32))).transpose(0, 2, 1)
    o = chunked_gated_delta_rule(q, k, v, beta, g).transpose(0, 2, 1, 3)
    zf = z.astype(jnp.float32).reshape(b, seq, DN_HEADS, DN_HEAD_DIM)
    o = rms_norm(o, out_gain) * jax.nn.silu(zf)
    return o.reshape(b, seq, DN_WIDTH).astype(z.dtype)

def s5_mixer(u, a_re, a_im, log_dt, b_re, b_im, c_re, c_im, d_skip):
    bsz, seq, _ = u.shape
    uf = u.astype(jnp.float32).reshape(bsz, seq, S5_GROUPS, S5_GROUP)
    dt = jnp.exp(log_dt.astype(jnp.float32))[:, None]
    lr, li = a_re.astype(jnp.float32), a_im.astype(jnp.float32)
    mag = jnp.exp(lr * dt)
    ab_r, ab_i = mag * jnp.cos(li * dt), mag * jnp.sin(li * dt)
    den = lr * lr + li * li
    nr, ni = ab_r - 1.0, ab_i
    cr, ci = (nr * lr + ni * li) / den, (ni * lr - nr * li) / den
    br, bi = b_re.astype(jnp.float32), b_im.astype(jnp.float32)
    bb_r = cr[..., None] * br - ci[..., None] * bi
    bb_i = cr[..., None] * bi + ci[..., None] * br
    bu_r = jnp.einsum('blgp,gnp->blgn', uf, bb_r)
    bu_i = jnp.einsum('blgp,gnp->blgn', uf, bb_i)
    a_r = jnp.broadcast_to(ab_r, (seq, S5_GROUPS, S5_STATE))
    a_i = jnp.broadcast_to(ab_i, (seq, S5_GROUPS, S5_STATE))

    def combine(e1, e2):
        a1r, a1i, b1r, b1i = e1
        a2r, a2i, b2r, b2i = e2
        return (a2r * a1r - a2i * a1i, a2r * a1i + a2i * a1r, a2r * b1r - a2i * b1i + b2r, a2r * b1i + a2i * b1r + b2i)

    def scan_one(sr, si):
        _, _, xr, xi = lax.associative_scan(combine, (a_r, a_i, sr, si), axis=0)
        return xr, xi

    xr, xi = jax.vmap(scan_one)(bu_r, bu_i)
    y = (jnp.einsum('blgn,gpn->blgp', xr, c_re.astype(jnp.float32)) - jnp.einsum('blgn,gpn->blgp', xi, c_im.astype(jnp.float32)) + d_skip.astype(jnp.float32) * uf)
    return y.reshape(bsz, seq, S5_WIDTH).astype(u.dtype)

def peer_ffn(xf, w_query, keys1, keys2, expert_u, expert_v):
    tokens, d = xf.shape

    def block(xt):
        qry = (xt @ w_query).reshape(PEER_BLOCK, PEER_HEADS, 2, PEER_KEY_DIM)
        s1 = jnp.einsum('thd,kd->thk', qry[:, :, 0], keys1)
        s2 = jnp.einsum('thd,kd->thk', qry[:, :, 1], keys2)
        v1, i1 = lax.top_k(s1, PEER_TOPK)
        v2, i2 = lax.top_k(s2, PEER_TOPK)
        cand_s = (v1[..., :, None] + v2[..., None, :]).reshape(PEER_BLOCK, PEER_HEADS, PEER_TOPK * PEER_TOPK)
        cand_i = (i1[..., :, None] * PEER_KEYS + i2[..., None, :]).reshape(PEER_BLOCK, PEER_HEADS, PEER_TOPK * PEER_TOPK)
        top_s, pos = lax.top_k(cand_s, PEER_TOPK)
        idx = jnp.take_along_axis(cand_i, pos, axis=-1)
        gate = jax.nn.softmax(top_s.astype(jnp.float32), axis=-1).astype(xt.dtype)
        act = jax.nn.gelu(jnp.einsum('td,thkd->thk', xt, expert_u[idx]))
        return jnp.einsum('thk,thkd->td', gate * act, expert_v[idx])

    out = lax.map(block, xf.reshape(tokens // PEER_BLOCK, PEER_BLOCK, d))
    return out.reshape(tokens, d)

def hybrid_layer(x, pe, norm_mix, w_in, att_q_gain, att_k_gain, w_a_out, dn_conv, dn_a_log, dn_dt_bias, dn_out_gain, w_b_out, s5_a_re, s5_a_im, s5_log_dt, s5_b_re, s5_b_im, s5_c_re, s5_c_im, s5_d, w_c_val, w_c_gate, w_out, norm_ffn, peer_w_query, peer_keys1, peer_keys2, peer_u, peer_v, ple_w, ple_norm, ple_w_gate):
    b, seq, d = x.shape
    h = rms_norm(x, norm_mix)
    qa, ka, va, qkv_b, z_b, beta_b, alpha_b, u_c, gates = jnp.split(h @ w_in, SPLIT_IDX, axis=-1)
    y_a = dilated_attention_mixer(qa, ka, va, att_q_gain, att_k_gain) @ w_a_out
    y_b = gated_deltanet_mixer(qkv_b, z_b, beta_b, alpha_b, dn_conv, dn_a_log, dn_dt_bias, dn_out_gain) @ w_b_out
    s = jax.nn.gelu(s5_mixer(u_c, s5_a_re, s5_a_im, s5_log_dt, s5_b_re, s5_b_im, s5_c_re, s5_c_im, s5_d))
    y_c = (s @ w_c_val) * jax.nn.sigmoid(s @ w_c_gate)
    g_a, g_b, g_c = jnp.split(jax.nn.sigmoid(gates), 3, axis=-1)
    x = x + (g_a * y_a + g_b * y_b + g_c * y_c) @ w_out
    hf = rms_norm(x, norm_ffn).reshape(b * seq, d)
    x = x + peer_ffn(hf, peer_w_query, peer_keys1, peer_keys2, peer_u, peer_v).reshape(b, seq, d)
    x = x + jax.nn.sigmoid(rms_norm(x, ple_norm) @ ple_w_gate) * (pe @ ple_w)
    return x

def setup_inputs(seed: int = 0) -> dict:
    key = jax.random.key(seed)
    keys = iter(jax.random.split(key, 40))
    f32 = jnp.float32
    nl = DEPTH

    def normal(shape, scale):
        return jax.random.normal(next(keys), shape, f32) * scale

    def uniform(shape, lo, hi):
        return jax.random.uniform(next(keys), shape, f32, lo, hi)

    def gain(shape):
        return 1.0 + normal(shape, 0.02)

    log_dt_lo, log_dt_hi = float(np.log(1e-3)), float(np.log(1e-1))
    dn_dt = jnp.exp(uniform((nl, DN_HEADS), log_dt_lo, log_dt_hi))
    return {
        'x': normal((BATCH, SEQ, D_MODEL), 1.0),
        'p': normal((DEPTH, BATCH, SEQ, PLE_DIM), 1.0),
        'norm_mix': gain((nl, D_MODEL)),
        'w_in': normal((nl, D_MODEL, IN_COLS), D_MODEL ** -0.5),
        'att_q_gain': gain((nl, ATT_HEAD_DIM)),
        'att_k_gain': gain((nl, ATT_HEAD_DIM)),
        'w_a_out': normal((nl, ATT_WIDTH, D_MODEL), ATT_WIDTH ** -0.5),
        'dn_conv': normal((nl, DN_CONV, 3 * DN_WIDTH), DN_CONV ** -0.5),
        'dn_a_log': jnp.log(uniform((nl, DN_HEADS), 1.0, 16.0)),
        'dn_dt_bias': dn_dt + jnp.log(-jnp.expm1(-dn_dt)),
        'dn_out_gain': gain((nl, DN_HEAD_DIM)),
        'w_b_out': normal((nl, DN_WIDTH, D_MODEL), DN_WIDTH ** -0.5),
        's5_a_re': -0.5 + normal((nl, S5_GROUPS, S5_STATE), 0.01),
        's5_a_im': jnp.pi * jnp.arange(S5_STATE, dtype=f32) + normal((nl, S5_GROUPS, S5_STATE), 0.01),
        's5_log_dt': uniform((nl, S5_GROUPS), log_dt_lo, log_dt_hi),
        's5_b_re': normal((nl, S5_GROUPS, S5_STATE, S5_GROUP), (2 * S5_GROUP) ** -0.5),
        's5_b_im': normal((nl, S5_GROUPS, S5_STATE, S5_GROUP), (2 * S5_GROUP) ** -0.5),
        's5_c_re': normal((nl, S5_GROUPS, S5_GROUP, S5_STATE), S5_STATE ** -0.5),
        's5_c_im': normal((nl, S5_GROUPS, S5_GROUP, S5_STATE), S5_STATE ** -0.5),
        's5_d': normal((nl, S5_GROUPS, S5_GROUP), 1.0),
        'w_c_val': normal((nl, S5_WIDTH, D_MODEL), S5_WIDTH ** -0.5),
        'w_c_gate': normal((nl, S5_WIDTH, D_MODEL), S5_WIDTH ** -0.5),
        'w_out': normal((nl, D_MODEL, D_MODEL), D_MODEL ** -0.5),
        'norm_ffn': gain((nl, D_MODEL)),
        'peer_w_query': normal((nl, D_MODEL, PEER_HEADS * 2 * PEER_KEY_DIM), D_MODEL ** -0.5),
        'peer_keys1': normal((nl, PEER_KEYS, PEER_KEY_DIM), PEER_KEY_DIM ** -0.5),
        'peer_keys2': normal((nl, PEER_KEYS, PEER_KEY_DIM), PEER_KEY_DIM ** -0.5),
        'peer_u': normal((nl, PEER_EXPERTS, D_MODEL), D_MODEL ** -0.5),
        'peer_v': normal((nl, PEER_EXPERTS, D_MODEL), PEER_HEADS ** -0.5),
        'ple_w': normal((nl, PLE_DIM, D_MODEL), PLE_DIM ** -0.5),
        'ple_norm': gain((nl, D_MODEL)),
        'ple_w_gate': normal((nl, D_MODEL, D_MODEL), D_MODEL ** -0.5),
    }

def reference(x, p, norm_mix, w_in, att_q_gain, att_k_gain, w_a_out, dn_conv, dn_a_log, dn_dt_bias, dn_out_gain, w_b_out, s5_a_re, s5_a_im, s5_log_dt, s5_b_re, s5_b_im, s5_c_re, s5_c_im, s5_d, w_c_val, w_c_gate, w_out, norm_ffn, peer_w_query, peer_keys1, peer_keys2, peer_u, peer_v, ple_w, ple_norm, ple_w_gate):
    for i in range(DEPTH):
        x = hybrid_layer(x, p[i], norm_mix[i], w_in[i], att_q_gain[i], att_k_gain[i], w_a_out[i], dn_conv[i], dn_a_log[i], dn_dt_bias[i], dn_out_gain[i], w_b_out[i], s5_a_re[i], s5_a_im[i], s5_log_dt[i], s5_b_re[i], s5_b_im[i], s5_c_re[i], s5_c_im[i], s5_d[i], w_c_val[i], w_c_gate[i], w_out[i], norm_ffn[i], peer_w_query[i], peer_keys1[i], peer_keys2[i], peer_u[i], peer_v[i], ple_w[i], ple_norm[i], ple_w_gate[i])
    return x


_drawn_inputs = setup_inputs


def setup_inputs(seed=0):
    import zlib

    import numpy as np

    out = dict(_drawn_inputs(seed))
    spreads = {}
    factors = {'att_q_gain': 3.487, 'att_k_gain': 3.847, 's5_a_re': 8.0, 'ple_norm': 5.418}
    for name, (base, spread) in spreads.items():
        noise = np.random.default_rng([zlib.crc32(name.encode()), seed]).standard_normal(out[name].shape)
        drawn = base * np.exp(spread * noise) if base else spread * noise
        out[name] = __import__('jax').numpy.asarray(drawn.astype(out[name].dtype))
    for name, factor in factors.items():
        out[name] = (out[name] * factor).astype(out[name].dtype)
    return out
```

```python
from collections import namedtuple
from contextlib import ExitStack

import numpy as np

import concourse.bass as bass
from concourse import mybir

F32 = mybir.dt.float32
U32 = mybir.dt.uint32
I32 = mybir.dt.int32
ALU = mybir.AluOpType
ACT = mybir.ActivationFunctionType
AX_X = mybir.AxisListType.X

P = 128
T = 512
NT = T // P
D = 1024
KD = D // P
DEPTH = 2
EPS = 1e-6

HEAD = 64
SLOTS = 4
GROUPS = 3
WINDOW = 128
QKV_ATT = (GROUPS + 2) * SLOTS * HEAD
QK_HEADS = (GROUPS + 1) * SLOTS
DN = 4
S5_BLOCKS = 8
S5_G = 16
PEER_HEADS = 8
KEYS = 128
TOPK = 16
EXPERTS = KEYS * KEYS
PLE = 256

COL_ATT = 0
COL_QKV = COL_ATT + QKV_ATT
COL_Z = COL_QKV + 3 * DN * P
COL_BA = COL_Z + DN * P
COL_U = COL_BA + 2 * DN
COL_GATES = COL_U + 256
IN_COLS = COL_GATES + 3 * D

PANEL = 256
RING = 3
BANKS = 3
NEG = -1e30
PI = float(np.pi)
TWO_PI_HI = 6.28125
TWO_PI_LO = float(2 * np.pi - 6.28125)
SLOPES = 2.0 ** (-8.0 * np.arange(1, GROUPS * SLOTS + 1) / (GROUPS * SLOTS))


def shape_constants():
    i = np.arange(P)[:, None]
    j = np.arange(P)[None, :]
    parts = {}
    parts["ident"] = np.eye(P)
    parts["ones"] = np.ones((P, P))
    parts["triu"] = i <= j
    parts["strict"] = np.where(i > j, 0.0, NEG)
    parts["incl_t"] = np.where(j >= i, 0.0, NEG)
    for b in (1, 2, 4, 8, 16, 32, 64):
        parts[f"join{b}"] = (i // (2 * b) == j // (2 * b)) & (j // b % 2 == 1) & (i // b % 2 == 0)
    parts["join1_low"] = ((i // 2 == j // 2) & (i % 2 == 1) & (j % 2 == 0))
    far = 1e33
    d = np.concatenate([4 * (i - j) + delta for delta in range(3, -4, -1)], axis=1)
    parts["dist_g0"] = np.where((d >= 0) & (d <= WINDOW), d, far)
    d = 4 * (i - j)
    parts["dist_g1"] = np.where(d >= 0, d, far)
    parts["dist_g2"] = np.where((d >= 0) & (d % 16 == 0), d, far)
    rows = np.zeros((P, 8, 8))
    rows[:, np.arange(8), np.arange(8)] = 1
    parts["to_row"] = rows.reshape(P, 64)
    spread = np.zeros((P, 8, P))
    for n in range(8):
        spread[n, n] = float(P) ** -0.5 if n < DN else 1.0
    parts["spread_qk"] = spread.reshape(P, 8 * P)
    spread = np.zeros((P, DN, P))
    for n in range(DN):
        spread[n, n] = 1.0
    parts["spread"] = spread.reshape(P, DN * P)
    parts["iota"] = np.broadcast_to(np.arange(TOPK), (P, TOPK))
    parts["eps"] = np.full((P, 1), EPS)
    where, at = {}, 0
    for name, a in parts.items():
        where[name] = (at, a.shape[1])
        at += a.shape[1]
    return np.concatenate([np.asarray(a, np.float32) for a in parts.values()], axis=1), where


CONSTS, WHERE = shape_constants()


class Link:

    def __init__(self, eng, sem):
        self.eng, self.sem, self.n = eng, sem, 0

    def mark(self, ins):
        self.n += 1
        ins.then_inc(self.sem, 1)

    def settle(self):
        self.eng.wait_ge(self.sem, self.n)

    def step(self, ins):
        self.mark(ins)
        self.settle()

    def restart(self):
        self.settle()
        self.eng.sem_clear(self.sem)
        self.n = 0


class Machine:
    pass


def over(ap, shape):
    return ap.to_broadcast(list(shape))


def semaphores(nc, ctx, names):
    names = names.split()
    return namedtuple("Semaphores", names)(*[ctx.enter_context(nc.semaphore(n)) for n in names])


def clear(nc, group):
    nums = sorted(s.num for s in group)
    assert nums[-1] - nums[0] == len(nums) - 1
    nc.all_engine_barrier(sems_to_clear=range(nums[0], nums[-1] + 1))


COMMON = "landed0 landed1 landed2 params_in act_filled act_read vec_filled vec_read act_step vec_step pool_step"


class Panels:

    def __init__(self, m, s, sources):
        self.m, self.s, self.sources = m, s, sources
        self.released = []

    def landed(self, pe, n):
        pe.wait_ge((self.s.landed0, self.s.landed1, self.s.landed2)[n % RING], 16 * (n // RING + 1))
        return self.m.ring[:, n % RING]

    def stream(self, sp):
        for n, (src, kt, cols) in enumerate(self.sources):
            if n >= RING:
                sem, count = self.released[n - RING]
                sp.wait_ge(sem, count)
            dst = self.m.ring[:, n % RING].rearrange("p (k c) -> p k c", k=kt)[:, :, 0:cols]
            sp.dma_start(dst, src).then_inc((self.s.landed0, self.s.landed1, self.s.landed2)[n % RING], 16)


def panel_view(slot, kt, cols=None):
    v = slot.rearrange("p (k c) -> p k c", k=kt)
    return v if cols is None else v[:, :, 0:cols]


def weight(ap, layer, k0, kt, c0, cols):
    return ap[bass.ds(layer, 1), k0 * P:(k0 + kt) * P, c0:c0 + cols].rearrange("l (k p) c -> p (l k) c", p=P)


class Banks:

    def __init__(self, pe, banks, filled, read):
        self.pe, self.banks, self.filled, self.read, self.n = pe, banks, filled, read, 0

    def open(self):
        self.n += 1
        if self.n > len(self.banks):
            self.pe.wait_ge(self.read, self.n - len(self.banks))
        return self.banks[(self.n - 1) % len(self.banks)]

    def all_read(self):
        self.pe.wait_ge(self.read, self.n)


class Reader:

    def __init__(self, eng, banks, filled, read):
        self.eng, self.banks, self.filled, self.read, self.n = eng, banks, filled, read, 0

    def take(self):
        self.n += 1
        self.eng.wait_ge(self.filled, self.n)
        return self.banks[(self.n - 1) % len(self.banks)]

    def settle(self):
        self.eng.wait_ge(self.read, self.n)



def norm_scalar(m, s, act, step, ss, rms, h):
    for t in range(NT):
        step.mark(m.nc.scalar.activation(h[:, t], m.x[:, t], ACT.Square, accum_out=ss[:, t:t + 1]))
    step.settle()
    m.nc.scalar.activation(rms, ss, ACT.Sqrt, bias=m.c("eps"), scale=1.0 / D).then_inc(s.rms_ready, 1)


def norm_vector(m, s, v, step, rms, rstd, gain, h):
    v.wait_ge(s.rms_ready, 1)
    step.step(m.nc.vector.reciprocal(rstd, rms))
    for t in range(NT):
        m.nc.vector.scalar_tensor_tensor(out=h[:, t], in0=m.x[:, t], scalar=rstd[:, t:t + 1], in1=gain,
                                         op0=ALU.mult, op1=ALU.mult).then_inc(s.h_ready, 1)


def norm_transposes(m, s, pe, to_act, to_vec, h):
    for t in range(NT):
        pe.wait_ge(s.h_ready, t + 1)
        for half, banks in ((0, to_act), (1, to_vec)):
            bank = banks.open()
            for k in range(4):
                kk = 4 * half + k
                ins = m.nc.tensor.transpose(bank[:, k * P:(k + 1) * P], h[:, t, kk * P:(kk + 1) * P], m.c("ident"))
            ins.then_inc(banks.filled, 1)
    to_act.all_read()
    to_vec.all_read()


def norm_copy(m, eng, reader, half):
    for t in range(NT):
        bank = reader.take()
        dst = m.hT[:, 4 * half:4 * half + 4, t * P:(t + 1) * P]
        src = bank[:, :].rearrange("p (k n) -> p k n", k=4)
        if half == 0:
            m.nc.scalar.activation(dst, src, ACT.Copy).then_inc(reader.read, 1)
        else:
            m.nc.vector.tensor_copy(dst, src).then_inc(reader.read, 1)



def phase_project(m, layer):
    nc, io = m.nc, m.io
    with ExitStack() as ctx:
        s = semaphores(nc, ctx, COMMON + " rms_ready h_ready s5_to_act s5_from_act seed_ready bb_placed qk_sq qk_ss qk_rms qk_ready")
        sb = lambda n, shape, dt=F32: ctx.enter_context(nc.sbuf_tensor(n, shape, dt))
        gain = sb("gain_mix", [P, D])
        qk_gain = sb("qk_gain", [P, QK_HEADS * HEAD])
        small = sb("small1", [P, 256])
        s5s = sb("s5_small", [P, 26, 8])
        s5i = sb("s5_int", [P, 8], I32)
        bmat = sb("s5_b", [P, 2, 8, 16])
        cmat = sb("s5_c", [P, 2, 8, 16])
        bb = sb("s5_bb", [P, 2, 8, 16])
        bbt = sb("s5_bbt", [P, 4, 8, 16])
        bbd = sb("s5_bbd", [P, 2, 8 * P])
        pool_t = sb("rot_tmp", [P, 2, 4 * 256])
        pool_w = sb("rot_w", [P, 6, 4])
        h = m.work_a[:, :].rearrange("p (t d) -> p t d", t=NT)
        ss, rms, rstd = small[:, 0:4], small[:, 4:8], small[:, 8:12]
        qss, qrms, qrstd = small[:, 16:80], small[:, 80:144], small[:, 144:208]
        rows = [(weight(io.w_in, layer, 0, KD, COL_U, 256), KD, 256)]
        rows += [(weight(io.w_in, layer, 0, KD, n * PANEL, PANEL), KD, PANEL) for n in range(5)]
        rows += [(weight(io.w_in, layer, 0, KD, COL_BA, 2 * DN), KD, 2 * DN)]
        panels = Panels(m, s, rows)
        NPARAM = 16

        block = ctx.enter_context(nc.Block())

        @block.tensor
        def _(pe):
            to_act = Banks(pe, m.banks[0:3], s.act_filled, s.act_read)
            to_vec = Banks(pe, m.banks[3:6], s.vec_filled, s.vec_read)
            norm_transposes(m, s, pe, to_act, to_vec, h)
            w = panel_view(panels.landed(pe, 0), KD)
            for mt in range(2):
                bank = to_act.open()
                for k in range(KD):
                    ins = nc.tensor.matmul(bank[:, :], w[:, k, mt * P:(mt + 1) * P], m.hT[:, k, :],
                                           start=(k == 0), stop=(k == KD - 1))
                ins.then_inc(s.act_filled, 1)
            panels.released.append((s.act_filled, to_act.n))
            for n in range(5):
                w = panel_view(panels.landed(pe, n + 1), KD)
                for r in range(4):
                    banks = (to_act, to_vec)[r % 2]
                    bank = banks.open()
                    for k in range(KD):
                        ins = nc.tensor.matmul(bank[:, 0:PANEL], m.hT[:, k, r::4], w[:, k, :],
                                               start=(k == 0), stop=(k == KD - 1))
                    ins.then_inc(banks.filled, 1)
                panels.released.append((s.vec_filled, to_vec.n))
            w = panel_view(panels.landed(pe, 6), KD)
            bank = to_vec.open()
            for c in range(NT):
                for k in range(KD):
                    ins = nc.tensor.matmul(bank[:, c * 8:c * 8 + 8], m.hT[:, k, c * P:(c + 1) * P], w[:, k, 0:8],
                                           start=(k == 0), stop=(k == KD - 1))
            ins.then_inc(s.vec_filled, 1)
            panels.released.append((s.vec_filled, to_vec.n))
            pe.wait_ge(s.bb_placed, 1)
            for part in range(2):
                for half in range(2):
                    bank = to_act.open()
                    for b in range(4):
                        at = (4 * half + b) * P
                        ins = nc.tensor.transpose(bank[:, b * P:(b + 1) * P], bbd[:, part, at:at + P], m.c("ident"))
                    ins.then_inc(s.act_filled, 1)
            pe.wait_ge(s.qk_ready, 1)
            for b in range(8):
                banks = (to_act, to_vec)[b % 2]
                bank = banks.open()
                for r in range(4):
                    ins = nc.tensor.transpose(bank[:, r * P:(r + 1) * P], m.att_qk[:, r, b * P:(b + 1) * P], m.c("ident"))
                ins.then_inc(banks.filled, 1)
            to_act.all_read()
            to_vec.all_read()

        @block.sync
        def _(sp):
            def load(dst, src):
                sp.dma_start(dst, src).then_inc(s.params_in, 16)
            load(gain[:, :], io.norm_mix[bass.ds(layer, 1), :].partition_broadcast(P).rearrange("p l d -> p (l d)"))
            for n in range(2):
                src = (io.att_q_gain, io.att_k_gain)[n][bass.ds(layer, 1), :].partition_broadcast(P)
                load(qk_gain[:, n * HEAD:(n + 1) * HEAD], src.rearrange("p l d -> p (l d)"))
            load(s5s[:, 0], io.s5_a_re[bass.ds(layer, 1)].rearrange("l p b -> p (l b)"))
            load(s5s[:, 1], io.s5_a_im[bass.ds(layer, 1)].rearrange("l p b -> p (l b)"))
            for hh in range(2):
                src = io.s5_log_dt[bass.ds(layer, 1), hh, :].partition_broadcast(64)
                load(s5s[64 * hh:64 * hh + 64, 2], src.rearrange("p l b -> p (l b)"))
            for n, a in enumerate((io.s5_b_re, io.s5_b_im)):
                load(bmat[:, n], a[bass.ds(layer, 1)].rearrange("l (b p) c -> p (l b) c", p=P))
            for n, a in enumerate((io.s5_c_re, io.s5_c_im)):
                load(cmat[:, n], a[bass.ds(layer, 1)].rearrange("l (b p) c -> p (l b) c", p=P))
            load(m.s5_d[:, :], io.s5_d[bass.ds(layer, 1)].rearrange("l p c -> p (l c)"))
            load(m.conv_w[:, :, :], io.dn_conv[bass.ds(layer, 1)].rearrange("l p b k -> p (l b) k"))
            load(m.a_log[:, :], io.dn_a_log[bass.ds(layer, 1), :].partition_broadcast(P).rearrange("p l d -> p (l d)"))
            load(m.dt_bias[:, :], io.dn_dt_bias[bass.ds(layer, 1), :].partition_broadcast(P).rearrange("p l d -> p (l d)"))
            load(m.out_gain[:, :], io.dn_out_gain[bass.ds(layer, 1)].rearrange("l p c -> p (l c)"))
            panels.stream(sp)

        @block.scalar
        def _(act):
            step = Link(act, s.act_step)
            banks = Reader(act, m.banks[0:3], s.act_filled, s.act_read)
            norm_scalar(m, s, act, step, ss, rms, h)
            act.wait_ge(s.params_in, 16 * NPARAM)
            nc.scalar.activation(s5s[:, 3], s5s[:, 2], ACT.Exp).then_inc(s.s5_from_act, 1)
            act.wait_ge(s.s5_to_act, 1)
            nc.scalar.activation(m.mag[:, :], s5s[:, 4], ACT.Exp).then_inc(s.s5_from_act, 1)
            act.wait_ge(s.s5_to_act, 2)
            nc.scalar.activation(s5s[:, 8], s5s[:, 6], ACT.Sin).then_inc(s.s5_from_act, 1)
            nc.scalar.activation(s5s[:, 9], s5s[:, 7], ACT.Sin).then_inc(s.s5_from_act, 1)
            norm_copy(m, act, banks, 0)
            for mt in range(2):
                bank = banks.take()
                nc.scalar.activation(m.uT[:, mt, :], bank[:, :], ACT.Copy).then_inc(s.act_read, 1)
            for n in range(5):
                for r in (0, 2):
                    bank = banks.take()
                    dst = m.att_qk[:, r, n * PANEL:(n + 1) * PANEL] if n < 4 else m.att_v[:, r, :]
                    nc.scalar.activation(dst, bank[:, 0:PANEL], ACT.Copy).then_inc(s.act_read, 1)
            for part in range(2):
                for half in range(2):
                    bank = banks.take()
                    nc.scalar.activation(m.s5_in[:, part, half * 512:half * 512 + 512], bank[:, :], ACT.Copy).then_inc(s.act_read, 1)
            act.wait_ge(s.qk_sq, 1)
            banks.settle()
            nc.scalar.activation(m.work_a[:, :], m.att_qk[:, :, :].rearrange("p r c -> p (r c)"), ACT.Square).then_inc(s.qk_ss, 1)
            act.wait_ge(s.qk_sq, 2)
            nc.scalar.activation(qrms, qss, ACT.Sqrt, bias=m.c("eps"), scale=1.0 / HEAD).then_inc(s.qk_rms, 1)
            for b in range(0, 8, 2):
                bank = banks.take()
                nc.scalar.activation(m.qkT[:, b, :], bank[:, :], ACT.Copy).then_inc(s.act_read, 1)

        @block.vector
        def _(v):
            step = Link(v, s.vec_step)
            banks = Reader(v, m.banks[3:6], s.vec_filled, s.vec_read)
            tt, ts = nc.vector.tensor_tensor, nc.vector.tensor_scalar
            for b in (bbd, m.s5_out):
                step.mark(nc.vector.memset(b[:, :, :], 0.0))
            v.wait_ge(s.params_in, 16 * NPARAM)
            norm_vector(m, s, v, step, rms, rstd, gain[:, :], h)
            re, im, dt, ldt, th = s5s[:, 0], s5s[:, 1], s5s[:, 3], s5s[:, 4], s5s[:, 5]
            v.wait_ge(s.s5_from_act, 1)
            tt(ldt, re, dt, ALU.mult).then_inc(s.s5_to_act, 1)
            step.step(tt(th, im, dt, ALU.mult))
            step.step(ts(s5s[:, 6], th, 1.0 / (2 * PI), None, ALU.mult))
            step.step(nc.vector.tensor_copy(s5i[:, :], s5s[:, 6]))
            step.step(nc.vector.tensor_copy(s5s[:, 6], s5i[:, :]))
            step.step(nc.vector.scalar_tensor_tensor(out=s5s[:, 7], in0=s5s[:, 6], scalar=-TWO_PI_HI, in1=th, op0=ALU.mult, op1=ALU.add))
            step.step(nc.vector.scalar_tensor_tensor(out=s5s[:, 6], in0=s5s[:, 6], scalar=-TWO_PI_LO, in1=s5s[:, 7], op0=ALU.mult, op1=ALU.add))
            step.step(ts(s5s[:, 7], s5s[:, 6], PI / 2, None, ALU.add))
            for n in (6, 7):
                for cmp, bound, turn in ((ALU.is_gt, PI, -2 * PI), (ALU.is_lt, -PI, 2 * PI)):
                    step.step(ts(s5s[:, 10], s5s[:, n], bound, turn, cmp, ALU.mult))
                    step.step(tt(s5s[:, n], s5s[:, n], s5s[:, 10], ALU.add))
            step.step(ts(s5s[:, 6], s5s[:, 6], 3.1415925, -3.1415925, ALU.min, ALU.max))
            ts(s5s[:, 7], s5s[:, 7], 3.1415925, -3.1415925, ALU.min, ALU.max).then_inc(s.s5_to_act, 1)
            v.wait_ge(s.s5_from_act, 4)
            sin, cos = s5s[:, 8], s5s[:, 9]
            step.mark(nc.vector.tensor_copy(m.seed[:, 0], cos))
            nc.vector.tensor_copy(m.seed[:, 1], sin).then_inc(s.seed_ready, 1)
            g = [s5s[:, n] for n in range(11, 26)]
            step.mark(tt(g[0], m.mag[:, :], cos, ALU.mult))
            step.mark(tt(g[1], m.mag[:, :], sin, ALU.mult))
            step.mark(tt(g[2], re, re, ALU.mult))
            step.step(tt(g[3], im, im, ALU.mult))
            step.mark(ts(g[0], g[0], -1.0, None, ALU.add))
            step.step(tt(g[2], g[2], g[3], ALU.add))
            step.mark(nc.vector.reciprocal(g[4], g[2]))
            step.mark(tt(g[5], g[0], re, ALU.mult))
            step.mark(tt(g[6], g[1], im, ALU.mult))
            step.mark(tt(g[7], g[1], re, ALU.mult))
            step.step(tt(g[8], g[0], im, ALU.mult))
            step.mark(tt(g[5], g[5], g[6], ALU.add))
            step.step(tt(g[7], g[7], g[8], ALU.subtract))
            step.mark(tt(g[5], g[5], g[4], ALU.mult))
            step.step(tt(g[7], g[7], g[4], ALU.mult))
            cr = over(g[5].unsqueeze(2), (P, 8, 16))
            ci = over(g[7].unsqueeze(2), (P, 8, 16))
            step.mark(tt(bbt[:, 0], bmat[:, 0], cr, ALU.mult))
            step.mark(tt(bbt[:, 1], bmat[:, 1], ci, ALU.mult))
            step.mark(tt(bbt[:, 2], bmat[:, 1], cr, ALU.mult))
            step.step(tt(bbt[:, 3], bmat[:, 0], ci, ALU.mult))
            step.mark(tt(bb[:, 0], bbt[:, 0], bbt[:, 1], ALU.subtract))
            step.step(tt(bb[:, 1], bbt[:, 2], bbt[:, 3], ALU.add))
            for part in range(2):
                for b in range(8):
                    for hh in range(2):
                        rows_ = slice(64 * hh, 64 * hh + 64)
                        at = b * P + 32 * (b % 4) + 16 * hh
                        step.mark(nc.vector.tensor_copy(bbd[rows_, part, at:at + 16], bb[rows_, part, b]))
                        step.mark(ts(m.s5_out[rows_, part, at:at + 16], cmat[rows_, part, b], (1.0, -1.0)[part], None, ALU.mult))
            step.settle()
            v.sem_inc(s.bb_placed, 1)
            norm_copy(m, v, banks, 1)
            for n in range(5):
                for r in (1, 3):
                    bank = banks.take()
                    dst = m.att_qk[:, r, n * PANEL:(n + 1) * PANEL] if n < 4 else m.att_v[:, r, :]
                    nc.vector.tensor_copy(dst, bank[:, 0:PANEL]).then_inc(s.vec_read, 1)
            bank = banks.take()
            nc.vector.tensor_copy(m.ba[:, :, :], bank[:, 0:32].rearrange("p (c k) -> p c k", c=NT)).then_inc(s.vec_read, 1)
            banks.settle()
            step.mark(nc.vector.tensor_copy(qk_gain[:, 12 * HEAD:].rearrange("p (g c) -> p g c", g=4),
                                            over(qk_gain[:, HEAD:2 * HEAD].unsqueeze(1), (P, 4, HEAD))))
            step.step(ts(qk_gain[:, 0:HEAD], qk_gain[:, 0:HEAD], HEAD ** -0.5, None, ALU.mult))
            step.step(nc.vector.tensor_copy(qk_gain[:, HEAD:12 * HEAD].rearrange("p (g c) -> p g c", g=11),
                                            over(qk_gain[:, 0:HEAD].unsqueeze(1), (P, 11, HEAD))))
            v.sem_inc(s.qk_sq, 1)
            v.wait_ge(s.qk_ss, 1)
            nc.vector.tensor_reduce(qss, m.work_a[:, :].rearrange("p (g c) -> p g c", c=HEAD), AX_X, ALU.add).then_inc(s.qk_sq, 1)
            v.wait_ge(s.qk_rms, 1)
            step.step(nc.vector.reciprocal(qrstd, qrms))
            qk = m.att_qk[:, :, :].rearrange("p r (g c) -> p (r g) c", c=HEAD)
            step.step(tt(qk, qk, over(qrstd.unsqueeze(2), (P, 64, HEAD)), ALU.mult))
            tt(m.att_qk[:, :, :], m.att_qk[:, :, :], over(qk_gain[:, :].unsqueeze(1), (P, 4, 1024)), ALU.mult).then_inc(s.qk_ready, 1)
            for b in range(1, 8, 2):
                bank = banks.take()
                nc.vector.tensor_copy(m.qkT[:, b, :], bank[:, :]).then_inc(s.vec_read, 1)

        @block.gpsimd
        def _(pool):
            step = Link(pool, s.pool_step)
            tt = nc.gpsimd.tensor_tensor
            step.mark(nc.gpsimd.memset(m.rot[:, 0, :, 0:1], 1.0))
            step.mark(nc.gpsimd.memset(m.rot[:, 1, :, 0:1], 0.0))
            pool.wait_ge(s.seed_ready, 1)
            step.settle()
            for q in range(2):
                bl = slice(4 * q, 4 * q + 4)
                w = [m.seed[:, 0, bl], m.seed[:, 1, bl]]
                n = 1
                while n < T:
                    wr = over(w[0].unsqueeze(2), (P, 4, n))
                    wi = over(w[1].unsqueeze(2), (P, 4, n))
                    re, im = m.rot[:, 0, bl, 0:n], m.rot[:, 1, bl, 0:n]
                    t = [pool_t[:, k, 0:4 * n].rearrange("p (b n) -> p b n", b=4) for k in range(2)]
                    step.mark(tt(t[0], re, wr, ALU.mult))
                    step.step(tt(t[1], im, wi, ALU.mult))
                    step.step(tt(m.rot[:, 0, bl, n:2 * n], t[0], t[1], ALU.subtract))
                    step.mark(tt(t[0], re, wi, ALU.mult))
                    step.step(tt(t[1], im, wr, ALU.mult))
                    step.step(tt(m.rot[:, 1, bl, n:2 * n], t[0], t[1], ALU.add))
                    n *= 2
                    if n < T:
                        e = [pool_w[:, k] for k in range(6)]
                        new = (2, 3) if n.bit_length() % 2 == 0 else (4, 5)
                        step.mark(tt(e[0], w[0], w[0], ALU.mult))
                        step.step(tt(e[1], w[1], w[1], ALU.mult))
                        step.mark(tt(e[new[0]], e[0], e[1], ALU.subtract))
                        step.step(tt(e[new[1]], w[0], w[1], ALU.mult))
                        step.step(tt(e[new[1]], e[new[1]], e[new[1]], ALU.add))
                        w = [e[new[0]], e[new[1]]]
    clear(nc, s)



def phase_attend(m, layer):
    nc = m.nc
    with ExitStack() as ctx:
        s = semaphores(nc, ctx, COMMON + " soft_ready exp_done folded o_filled o_ready ur_ready scanned x_ready y_done y_read gelu_done")
        sb = lambda n, shape, dt=F32: ctx.enter_context(nc.sbuf_tensor(n, shape, dt))
        small = sb("small2", [P, 64])
        bu = sb("s5_bu", [P, 2, T])
        ptmp = sb("s5_ptmp", [P, 2, T])
        ur = sb("s5_ur", [P, 2, 2, T])
        z = sb("s5_z", [P, 2, T])
        vtmp = sb("s5_vtmp", [P, 2, T])
        xs = sb("s5_x", [P, 2, T])
        wb = m.att_qk[:, :, :].rearrange("p r c -> p (r c)")
        e = [wb[:, k * 768:(k + 1) * 768] for k in range(2)]
        pt = [wb[:, 1536 + k * 512:2048 + k * 512] for k in range(2)]
        osb = [wb[:, 2560 + k * 256:2816 + k * 256] for k in range(2)]
        nmax, den, rden = small[:, 0:16], small[:, 16:32], small[:, 32:48]
        obanks, ybank = (m.banks[7], m.banks[2]), m.banks[6]
        N = 4 * SLOTS
        pt_count, bu_count, at_count = {}, {}, {}

        def a_order(it):
            out = []
            if it >= 1:
                out.append(("pt", it - 1))
                if (it - 1) % 4 == 1 and it - 1 >= 4:
                    out.append(("at", (it - 1) // 4 - 1))
            if it % 2 == 0 and it // 2 < S5_BLOCKS:
                out.append(("bu", it // 2))
            return out

        block = ctx.enter_context(nc.Block())

        @block.tensor
        def _(pe):
            to_act = Banks(pe, m.banks[0:2], s.act_filled, s.act_read)
            to_vec = Banks(pe, m.banks[3:6], s.vec_filled, s.vec_read)

            def scores(it):
                r, sl = it // 4, it % 4
                rows = slice(64 * (sl % 2), 64 * (sl % 2) + 64)
                k = m.qkT[rows, (GROUPS * SLOTS + sl) // 2]
                q = [m.qkT[rows, (4 * g + sl) // 2, r * P:(r + 1) * P] for g in range(GROUPS)]
                bank = to_vec.open()
                nc.tensor.matmul(bank[:, :], q[0], k, start=True, stop=True).then_inc(s.vec_filled, 1)
                bank = to_vec.open()
                nc.tensor.matmul(bank[:, 0:P], q[1], k[:, r * P:(r + 1) * P], start=True, stop=True)
                nc.tensor.matmul(bank[:, P:2 * P], q[2], k[:, r * P:(r + 1) * P], start=True, stop=True).then_inc(s.vec_filled, 1)

            def values(it):
                r, sl = it // 4, it % 4
                pe.wait_ge(s.folded, it + 1)
                bank = to_act.open()
                for r2 in range(4):
                    ins = nc.tensor.transpose(bank[:, r2 * P:(r2 + 1) * P], e[it % 2][:, r2 * P:(r2 + 1) * P], m.c("ident"))
                ins.then_inc(s.act_filled, 1)
                pt_count[it] = to_act.n
                if sl == 0 and r >= 2:
                    pe.wait_ge(s.o_ready, r - 1)
                to_act.all_read()
                at = HEAD * sl
                for r2 in range(4):
                    ins = nc.tensor.matmul(obanks[r % 2][:, at:at + HEAD], pt[it % 2][:, r2 * P:(r2 + 1) * P],
                                           m.att_v[:, r2, sl * HEAD:(sl + 1) * HEAD], start=(r2 == 0), stop=(r2 == 3))
                ins.then_inc(s.o_filled, 1)

            def out_transpose(r):
                pe.wait_ge(s.o_ready, r + 1)
                bank = to_act.open()
                for k in range(2):
                    ins = nc.tensor.transpose(bank[:, k * P:(k + 1) * P], osb[r % 2][:, k * P:(k + 1) * P], m.c("ident"))
                ins.then_inc(s.act_filled, 1)
                at_count[r] = to_act.n

            def s5_input(b):
                for part in range(2):
                    bank = to_act.open()
                    nc.tensor.matmul(bank[:, :], m.s5_in[:, part, b * P:(b + 1) * P], m.uT[:, b // 4, :],
                                     start=True, stop=True).then_inc(s.act_filled, 1)
                bu_count[b] = to_act.n

            def s5_output(b):
                pe.wait_ge(s.x_ready, b + 1)
                if b == 4:
                    pe.wait_ge(s.y_read, 1)
                for part in range(2):
                    ins = nc.tensor.matmul(ybank[:, :], m.s5_out[:, part, b * P:(b + 1) * P], xs[:, part, :],
                                           start=(b % 4 == 0 and part == 0), stop=(b % 4 == 3 and part == 1))
                ins.then_inc(s.y_done, 1)

            for it in range(N + 6):
                if it < N:
                    scores(it)
                for what, n in a_order(it) if it <= N else ():
                    {"pt": values, "at": out_transpose, "bu": s5_input}[what](n)
                if it % 2 == 1 and 0 <= (it - 3) // 2 < S5_BLOCKS:
                    s5_output((it - 3) // 2)
            out_transpose(3)

        @block.scalar
        def _(act):
            banks = Reader(act, m.banks[0:2], s.act_filled, s.act_read)

            def copy(what, n):
                bank = banks.take()
                if what == "pt":
                    if n >= 2:
                        act.wait_ge(s.o_filled, n - 1)
                    nc.scalar.activation(pt[n % 2], bank[:, :], ACT.Copy).then_inc(s.act_read, 1)
                elif what == "at":
                    nc.scalar.activation(m.aT[:, :, n::4], bank[:, 0:256].rearrange("p (k q) -> p k q", k=2),
                                         ACT.Copy).then_inc(s.act_read, 1)
                else:
                    if n >= 1:
                        act.wait_ge(s.ur_ready, n)
                    nc.scalar.activation(bu[:, 0, :], bank[:, :], ACT.Copy).then_inc(s.act_read, 1)
                    bank = banks.take()
                    nc.scalar.activation(bu[:, 1, :], bank[:, :], ACT.Copy).then_inc(s.act_read, 1)

            for it in range(N + 1):
                if it < N:
                    act.wait_ge(s.soft_ready, it + 1)
                    nc.scalar.activation(e[it % 2], e[it % 2], ACT.Exp, bias=nmax[:, it:it + 1],
                                         accum_out=den[:, it:it + 1]).then_inc(s.exp_done, 1)
                for what, n in a_order(it):
                    copy(what, n)
            copy("at", 3)
            for yt in range(2):
                act.wait_ge(s.y_read, yt + 1)
                nc.scalar.activation(m.sT[:, yt, :], m.sT[:, yt, :], ACT.Gelu_apprx_tanh).then_inc(s.gelu_done, 1)

        @block.vector
        def _(v):
            step = Link(v, s.vec_step)
            banks = Reader(v, m.banks[3:6], s.vec_filled, s.vec_read)
            tt, stt = nc.vector.tensor_tensor, nc.vector.scalar_tensor_tensor

            def soft(it):
                r, sl = it // 4, it % 4
                if it >= 2:
                    v.wait_ge(s.act_filled, pt_count[it - 2])
                bank = banks.take()
                stt(out=e[it % 2][:, 0:512], in0=m.c("dist_g0")[:, (3 - r) * P:(7 - r) * P], scalar=-float(SLOPES[sl]),
                    in1=bank[:, :], op0=ALU.mult, op1=ALU.add).then_inc(s.vec_read, 1)
                bank = banks.take()
                step.mark(stt(out=e[it % 2][:, 512:640], in0=m.c("dist_g1"), scalar=-float(SLOPES[SLOTS + sl]),
                              in1=bank[:, 0:P], op0=ALU.mult, op1=ALU.add))
                stt(out=e[it % 2][:, 640:768], in0=m.c("dist_g2"), scalar=-float(SLOPES[2 * SLOTS + sl]),
                    in1=bank[:, P:2 * P], op0=ALU.mult, op1=ALU.add).then_inc(s.vec_read, 1)
                banks.settle()
                step.settle()
                nc.vector.tensor_reduce(nmax[:, it:it + 1], e[it % 2], AX_X, ALU.max, negate=True).then_inc(s.soft_ready, 1)

            def fold(it):
                r = it // 4
                v.wait_ge(s.exp_done, it + 1)
                own = e[it % 2][:, r * P:(r + 1) * P]
                step.step(tt(own, own, e[it % 2][:, 512:640], ALU.add))
                tt(own, own, e[it % 2][:, 640:768], ALU.add).then_inc(s.folded, 1)

            def normalise(r):
                v.wait_ge(s.o_filled, 4 * r + 4)
                if r >= 2:
                    v.wait_ge(s.act_filled, at_count[r - 2])
                step.step(nc.vector.reciprocal(rden[:, 4 * r:4 * r + 4], den[:, 4 * r:4 * r + 4]))
                tt(osb[r % 2].rearrange("p (s c) -> p s c", s=4),
                   obanks[r % 2][:, 0:256].rearrange("p (s c) -> p s c", s=4),
                   over(rden[:, 4 * r:4 * r + 4].unsqueeze(2), (P, 4, HEAD)), ALU.mult).then_inc(s.o_ready, 1)

            def recur(b):
                v.wait_ge(s.ur_ready, b + 1)
                if b >= 1:
                    step.settle()
                for part in range(2):
                    nc.vector.tensor_tensor_scan(z[:, part, :], over(m.mag[:, b:b + 1], (P, T)), ur[:, b % 2, part, :],
                                                 0.0, ALU.mult, ALU.add).then_inc(s.scanned, 1)
                v.wait_ge(s.scanned, 2 * b + 2)
                cos, sin = m.rot[:, 0, b, :], m.rot[:, 1, b, :]
                if b >= 1:
                    v.wait_ge(s.y_done, b)
                    v.wait_ge(s.x_ready, b)
                step.mark(tt(vtmp[:, 0], z[:, 0], cos, ALU.mult))
                step.step(tt(vtmp[:, 1], z[:, 1], sin, ALU.mult))
                step.step(tt(xs[:, 0], vtmp[:, 0], vtmp[:, 1], ALU.subtract))
                step.mark(tt(vtmp[:, 0], z[:, 0], sin, ALU.mult))
                step.step(tt(vtmp[:, 1], z[:, 1], cos, ALU.mult))
                tt(xs[:, 1], vtmp[:, 0], vtmp[:, 1], ALU.add).then_inc(s.x_ready, 1)

            def skip(yt):
                v.wait_ge(s.y_done, 4 * yt + 4)
                stt(out=m.sT[:, yt, :], in0=m.uT[:, yt, :], scalar=m.s5_d[:, yt:yt + 1], in1=ybank[:, :],
                    op0=ALU.mult, op1=ALU.add).then_inc(s.y_read, 1)

            for it in range(N + 4):
                if it < N:
                    soft(it)
                if 1 <= it <= N:
                    fold(it - 1)
                if it >= 2 and (it - 2) % 4 == 3 and (it - 2) // 4 < 4:
                    normalise((it - 2) // 4)
                if it in (11, 19):
                    skip((it - 11) // 8)
                if it % 2 == 1 and it // 2 < S5_BLOCKS:
                    recur(it // 2)

        @block.gpsimd
        def _(pool):
            step = Link(pool, s.pool_step)
            tt = nc.gpsimd.tensor_tensor
            for b in range(S5_BLOCKS):
                cos, sin = m.rot[:, 0, b, :], m.rot[:, 1, b, :]
                pool.wait_ge(s.act_read, bu_count[b])
                if b >= 2:
                    pool.wait_ge(s.scanned, 2 * b - 2)
                if b >= 1:
                    pool.wait_ge(s.ur_ready, b)
                step.mark(tt(ptmp[:, 0], bu[:, 0], cos, ALU.mult))
                step.step(tt(ptmp[:, 1], bu[:, 1], sin, ALU.mult))
                step.step(tt(ur[:, b % 2, 0], ptmp[:, 0], ptmp[:, 1], ALU.add))
                step.mark(tt(ptmp[:, 0], bu[:, 1], cos, ALU.mult))
                step.step(tt(ptmp[:, 1], bu[:, 0], sin, ALU.mult))
                tt(ur[:, b % 2, 1], ptmp[:, 0], ptmp[:, 1], ALU.subtract).then_inc(s.ur_ready, 1)
    clear(nc, s)



JOINS = (2, 4, 8, 16, 32, 64)


def phase_deltanet(m, layer):
    nc, io = m.nc, m.io
    with ExitStack() as ctx:
        s = semaphores(nc, ctx, COMMON + " conv_done silu_done sq_ready row_used rows_sum rows_root rows_ready gate_a gate_v "
                       "tri_ready expo_ready decay_ready l_ready x_ready ct_ready vn_ready state_ready o_rows")
        sb = lambda n, shape, dt=F32: ctx.enter_context(nc.sbuf_tensor(n, shape, dt))
        raw = sb("dn_raw", [P, 3 * DN, T + 3])
        cv = sb("dn_conv", [P, 2, T])
        sq = sb("dn_sq", [P, 2, T])
        rows = sb("dn_rows", [8, T])
        small = sb("small3", [P, 240])
        big = lambda n: sb(n, [P, NT, T])
        lm, at, er, xt, lt, kbg, kdec, vb = (big(n) for n in ("dn_l", "dn_at", "dn_er", "dn_xt", "dn_lt", "dn_kbg", "dn_kdec", "dn_vb"))
        ct = sb("dn_ct", [P, 2, T])
        yb = sb("dn_y", [P, 2, T])
        vn = sb("dn_vn", [P, T])
        state = sb("dn_state", [P, T])
        x = [raw[:, 8 + c, 0:T] for c in range(NT)]
        heads = lambda a: a.rearrange("p (h n) -> p h n", h=DN)
        g16 = [small[:, 16 * k:16 * k + 16] for k in range(15)]
        beta, xg, na, lnp, g, gc, ngc, t3, ekd, eg, bg, gl = g16[0:12]
        ea = g16[12][:, 0:4]
        ch = lambda a: a.rearrange("p (c h) -> p c h", c=NT)
        rbank = m.banks[6]
        panels = Panels(m, s, [(weight(io.w_in, layer, 0, KD, COL_QKV + n * PANEL, PANEL), KD, PANEL) for n in range(8)])
        qt = lambda h, c: raw[:, h, 3 + c * P:3 + (c + 1) * P]
        kt = lambda h, c: raw[:, DN + h, 3 + c * P:3 + (c + 1) * P]
        vt = lambda h, c: raw[:, 2 * DN + h, 3 + c * P:3 + (c + 1) * P]
        hs = lambda h: slice(h * P, (h + 1) * P)
        vtok_count, gc_count, lt_count, wt_count = {}, {}, {}, {}

        def join_tail(pe, mm, to_act, to_vec, lv, c, y_count):
            pe.wait_ge(s.act_read, y_count)
            if lv < len(JOINS) - 1:
                bank = to_vec.open()
                for h in range(DN):
                    ins = mm(bank[:, hs(h)], xt[:, c, hs(h)], yb[:, c % 2, hs(h)], start=True, stop=True)
                ins.then_inc(s.vec_filled, 1)
            bank = to_vec.open()
            for h in range(DN):
                ins = mm(bank[:, hs(h)], yb[:, c % 2, hs(h)], xt[:, c, hs(h)], start=True, stop=True)
            ins.then_inc(s.vec_filled, 1)

        block = ctx.enter_context(nc.Block())

        @block.tensor
        def _(pe):
            to_act = Banks(pe, m.banks[0:3], s.act_filled, s.act_read)
            to_vec = Banks(pe, m.banks[3:6], s.vec_filled, s.vec_read)
            mm = nc.tensor.matmul

            def projection(n, mt, banks, w):
                bank = banks.open()
                for k in range(KD):
                    ins = mm(bank[:, :], w[:, k, mt * P:(mt + 1) * P], m.hT[:, k, :], start=(k == 0), stop=(k == KD - 1))
                ins.then_inc(banks.filled, 1)

            for n in range(6):
                w = panel_view(panels.landed(pe, n), KD)
                projection(n, 0, to_act, w)
                projection(n, 1, to_vec, w)
                panels.released.append((s.vec_filled, to_vec.n))
            pe.wait_ge(s.gate_v, 2)
            bank = to_act.open()
            mm(bank[:, 0:16], m.c("triu"), g, start=True, stop=True).then_inc(s.act_filled, 1)
            gc_count[0] = to_act.n
            for c in range(NT):
                pe.wait_ge(s.tri_ready, c + 1)
                bank = to_vec.open()
                mm(bank[:, :], m.c("ones"), lt[:, c, :], start=True, stop=True).then_inc(s.vec_filled, 1)
            for t in range(8):
                pe.wait_ge(s.sq_ready, t + 1)
                mm(rbank[0:8, :], m.c("to_row")[:, 8 * t:8 * t + 8], sq[:, t % 2, :],
                   start=(t == 0), stop=(t == 7)).then_inc(s.rows_sum, 1)
            pe.wait_ge(s.rows_ready, 1)
            for t in range(8):
                bank = to_vec.open()
                mm(bank[:, :], m.c("spread_qk")[0:8, t * P:(t + 1) * P], rows[:, :], start=True, stop=True).then_inc(s.vec_filled, 1)
            to_vec.all_read()
            for c in range(NT):
                bank = to_act.open()
                for h in range(DN):
                    ins = nc.tensor.transpose(bank[:, hs(h)], vt(h, c), m.c("ident"))
                ins.then_inc(s.act_filled, 1)
                vtok_count[c] = to_act.n
            for c in range(NT):
                for a, b in ((kt, kt), (kt, qt)):
                    bank = to_vec.open()
                    for h in range(DN):
                        ins = mm(bank[:, hs(h)], a(h, c), b(h, c), start=True, stop=True)
                    ins.then_inc(s.vec_filled, 1)
                bank = to_vec.open()
                for h in range(DN):
                    ins = nc.tensor.transpose(bank[:, hs(h)], kt(h, c), m.c("ident"))
                ins.then_inc(s.vec_filled, 1)
            for c in range(NT):
                pe.wait_ge(s.l_ready, c + 1)
                bank = to_act.open()
                for h in range(DN):
                    ins = nc.tensor.transpose(bank[:, hs(h)], lm[:, c, hs(h)], m.c("ident"))
                ins.then_inc(s.act_filled, 1)
                lt_count[c] = to_act.n
            for lv, b in enumerate(JOINS):
                for c in range(NT):
                    pe.wait_ge(s.ct_ready, lv * NT + c + 1)
                    pe.wait_ge(s.x_ready, lv * NT + c + 1)
                    bank = to_act.open()
                    for h in range(DN):
                        ins = mm(bank[:, hs(h)], ct[:, c % 2, hs(h)], x[c][:, hs(h)], start=True, stop=True)
                    ins.then_inc(s.act_filled, 1)
                    if c >= 1:
                        join_tail(pe, mm, to_act, to_vec, lv, c - 1, to_act.n - 1)
                join_tail(pe, mm, to_act, to_vec, lv, NT - 1, to_act.n)
            for c in range(NT):
                pe.wait_ge(s.x_ready, len(JOINS) * NT + c + 1)
                bank = to_act.open()
                for h in range(DN):
                    ins = mm(bank[:, hs(h)], xt[:, c, hs(h)], vb[:, c, hs(h)], start=True, stop=True)
                ins.then_inc(s.act_filled, 1)
                bank = to_act.open()
                for h in range(DN):
                    ins = mm(bank[:, hs(h)], kbg[:, c, hs(h)], xt[:, c, hs(h)], start=True, stop=True)
                ins.then_inc(s.act_filled, 1)
                wt_count[c] = to_act.n
            to_act.all_read()
            for c in range(NT):
                if c:
                    pe.wait_ge(s.state_ready, c)
                    bank = to_vec.open()
                    for h in range(DN):
                        ins = mm(bank[:, hs(h)], lt[:, c, hs(h)], state[:, hs(h)], start=True, stop=True)
                    ins.then_inc(s.vec_filled, 1)
                    pe.wait_ge(s.vn_ready, c)
                src = lambda h: vn[:, hs(h)] if c else lm[:, 0, hs(h)]
                bank = to_act.open()
                for h in range(DN):
                    ins = mm(bank[:, hs(h)], src(h), at[:, c, hs(h)], start=True, stop=(c == 0))
                    if c:
                        ins = mm(bank[:, hs(h)], state[:, hs(h)], er[:, c, hs(h)], start=False, stop=True)
                ins.then_inc(s.act_filled, 1)
                if c < NT - 1:
                    bank = to_vec.open()
                    for h in range(DN):
                        ins = mm(bank[:, hs(h)], kdec[:, c, hs(h)], src(h), start=True, stop=True)
                    ins.then_inc(s.vec_filled, 1)
            for h in range(DN):
                pe.wait_ge(s.sq_ready, 8 + h + 1)
                mm(rbank[0:8, :], m.c("to_row")[:, 8 * h:8 * h + 8], sq[:, h % 2, :],
                   start=(h == 0), stop=(h == DN - 1)).then_inc(s.rows_sum, 1)
            for n in range(2):
                w = panel_view(panels.landed(pe, 6 + n), KD)
                for mt in range(2):
                    projection(6 + n, mt, to_act, w)
                panels.released.append((s.act_filled, to_act.n))
            pe.wait_ge(s.rows_ready, 2)
            for h in range(DN):
                bank = to_vec.open()
                mm(bank[:, :], m.c("spread")[0:8, h * P:(h + 1) * P], rows[:, :], start=True, stop=True).then_inc(s.vec_filled, 1)

        @block.sync
        def _(sp):
            panels.stream(sp)

        @block.scalar
        def _(act):
            step = Link(act, s.act_step)
            banks = Reader(act, m.banks[0:3], s.act_filled, s.act_read)
            f = nc.scalar.activation
            step.mark(f(ch(beta), m.ba[:, :, 0:DN], ACT.Sigmoid))
            act.wait_ge(s.gate_v, 1)
            step.mark(f(ea, m.a_log[:, :], ACT.Exp))
            step.step(f(lnp, na, ACT.Exp))
            f(lnp, lnp, ACT.Ln, bias=1.0).then_inc(s.gate_a, 1)
            for n in range(6):
                bank = banks.take()
                f(raw[:, 2 * n, 3:], bank[:, :], ACT.Copy).then_inc(s.act_read, 1)
            for t in range(3 * DN):
                act.wait_ge(s.conv_done, t + 1)
                f(raw[:, t, 3:], cv[:, t % 2, :], ACT.Silu).then_inc(s.silu_done, 1)
            bank = banks.take()
            step.mark(f(gc, bank[:, 0:16], ACT.Copy))
            step.mark(f(ngc, bank[:, 0:16], ACT.Copy, scale=-1.0))
            f(eg, bank[:, 0:16], ACT.Exp).then_inc(s.act_read, 1)
            banks.settle()
            step.settle()
            act.sem_inc(s.gate_a, 1)
            act.wait_ge(s.silu_done, 3 * DN)
            for t in range(8):
                if t >= 2:
                    act.wait_ge(s.rows_sum, t - 1)
                f(sq[:, t % 2, :], raw[:, t, 3:], ACT.Square).then_inc(s.sq_ready, 1)
            act.wait_ge(s.rows_sum, 8)
            f(rows[:, :], rbank[0:8, :], ACT.Sqrt, bias=m.c("eps")[0:8, :]).then_inc(s.rows_root, 1)
            for c in range(NT):
                act.wait_ge(s.expo_ready, c + 1)
                for h in range(DN):
                    n = 4 * c + h
                    step.mark(f(lm[:, c, hs(h)], lm[:, c, hs(h)], ACT.Exp, bias=gc[:, n:n + 1]))
                    step.mark(f(at[:, c, hs(h)], at[:, c, hs(h)], ACT.Exp, bias=ngc[:, n:n + 1]))
                step.mark(f(ekd[:, 4 * c:4 * c + 4], t3[:, 4 * c:4 * c + 4], ACT.Exp))
                f(er[:, c, :], er[:, c, :], ACT.Exp).then_inc(s.decay_ready, 1)
            step.settle()
            for c in range(NT):
                bank = banks.take()
                for h in range(DN):
                    n = 4 * c + h
                    ins = f(vb[:, c, hs(h)], bank[:, hs(h)], ACT.Copy, scale=beta[:, n:n + 1])
                    if h < DN - 1:
                        step.mark(ins)
                ins.then_inc(s.act_read, 1)
            for c in range(NT):
                bank = banks.take()
                f(lt[:, c, :], bank[:, :], ACT.Copy).then_inc(s.act_read, 1)
            for lv in range(len(JOINS)):
                for c in range(NT):
                    bank = banks.take()
                    if lv * NT + c >= 2:
                        act.wait_ge(s.x_ready, NT + lv * NT + c - 1)
                    f(yb[:, c % 2, :], bank[:, :], ACT.Copy).then_inc(s.act_read, 1)
            for c in range(NT):
                bank = banks.take()
                f(lm[:, c, :], bank[:, :], ACT.Copy).then_inc(s.act_read, 1)
                bank = banks.take()
                f(lt[:, c, :], bank[:, :], ACT.Copy).then_inc(s.act_read, 1)
            for c in range(NT):
                bank = banks.take()
                f(m.bT[:, :, c * P:(c + 1) * P], heads(bank[:, :]), ACT.Copy).then_inc(s.act_read, 1)
            banks.settle()
            for h in range(DN):
                if h >= 2:
                    act.wait_ge(s.rows_sum, 8 + h - 1)
                f(sq[:, h % 2, :], m.bT[:, h, :], ACT.Square).then_inc(s.sq_ready, 1)
            for h in range(DN):
                bank = banks.take()
                f(raw[:, h, 3:], bank[:, :], ACT.Silu).then_inc(s.act_read, 1)
            act.wait_ge(s.rows_sum, 8 + DN)
            f(rows[:, :], rbank[0:8, :], ACT.Sqrt, bias=m.c("eps")[0:8, :], scale=1.0 / P).then_inc(s.rows_root, 1)

        @block.vector
        def _(v):
            step = Link(v, s.vec_step)
            banks = Reader(v, m.banks[3:6], s.vec_filled, s.vec_read)
            tt, ts, stt = nc.vector.tensor_tensor, nc.vector.tensor_scalar, nc.vector.scalar_tensor_tensor
            step.mark(nc.vector.memset(raw[:, :, 0:3], 0.0))
            step.step(tt(ch(xg), m.ba[:, :, DN:2 * DN], over(m.dt_bias[:, :].unsqueeze(1), (P, NT, DN)), ALU.add))
            stt(out=na, in0=xg, scalar=-1.0, in1=xg, op0=ALU.mult, op1=ALU.min).then_inc(s.gate_v, 1)
            v.wait_ge(s.gate_a, 1)
            step.step(stt(out=xg, in0=xg, scalar=0.0, in1=lnp, op0=ALU.max, op1=ALU.add))
            stt(out=ch(g), in0=ch(xg), scalar=-1.0, in1=over(ea.unsqueeze(1), (P, NT, DN)), op0=ALU.mult, op1=ALU.mult).then_inc(s.gate_v, 1)
            v.wait_ge(s.gate_v, 2)
            for c in range(NT):
                tt(heads(lt[:, c, :]), over(m.c("triu").unsqueeze(1), (P, DN, P)),
                   over(g[:, 4 * c:4 * c + 4].unsqueeze(2), (P, DN, P)), ALU.mult).then_inc(s.tri_ready, 1)
            for n in range(6):
                bank = banks.take()
                nc.vector.tensor_copy(raw[:, 2 * n + 1, 3:], bank[:, :]).then_inc(s.vec_read, 1)
            banks.settle()
            for t in range(3 * DN):
                if t % 2 == 0:
                    v.wait_ge(s.act_read, t // 2 + 1)
                if t >= 2:
                    v.wait_ge(s.silu_done, t - 1)
                o = cv[:, t % 2, :]
                step.step(ts(o, raw[:, t, 0:T], m.conv_w[:, t, 0:1], None, ALU.mult))
                for k in (1, 2, 3):
                    ins = stt(out=o, in0=raw[:, t, k:k + T], scalar=m.conv_w[:, t, k:k + 1], in1=o, op0=ALU.mult, op1=ALU.add)
                    if k < 3:
                        step.step(ins)
                ins.then_inc(s.conv_done, 1)
            v.wait_ge(s.gate_a, 2)
            step.step(tt(bg, beta, eg, ALU.mult))
            for c in range(NT):
                bank = banks.take()
                step.mark(tt(heads(lm[:, c, :]), over(m.c("strict").unsqueeze(1), (P, DN, P)), heads(bank[:, :]), ALU.subtract))
                step.mark(tt(heads(at[:, c, :]), over(m.c("incl_t").unsqueeze(1), (P, DN, P)), heads(bank[:, :]), ALU.add))
                step.mark(tt(t3[:, 4 * c:4 * c + 4].unsqueeze(2), heads(bank[:, :])[:, :, P - 1:P], gc[:, 4 * c:4 * c + 4].unsqueeze(2), ALU.subtract))
                step.step(nc.vector.tensor_copy(er[:, c, :], bank[:, :]))
                v.sem_inc(s.vec_read, 1)
                v.sem_inc(s.expo_ready, 1)
            v.wait_ge(s.rows_root, 1)
            nc.vector.reciprocal(rows[:, :], rows[:, :]).then_inc(s.rows_ready, 1)
            for t in range(8):
                bank = banks.take()
                tt(raw[:, t, 3:], raw[:, t, 3:], bank[:, :], ALU.mult).then_inc(s.vec_read, 1)
            v.wait_ge(s.act_read, vtok_count[NT - 1])
            for c in range(NT):
                v.wait_ge(s.decay_ready, c + 1)
                bank = banks.take()
                for h in range(DN):
                    n = 4 * c + h
                    ins = stt(out=lm[:, c, hs(h)], in0=bank[:, hs(h)], scalar=beta[:, n:n + 1], in1=lm[:, c, hs(h)], op0=ALU.mult, op1=ALU.mult)
                    if h < DN - 1:
                        step.mark(ins)
                ins.then_inc(s.vec_read, 1)
                banks.settle()
                step.settle()
                v.sem_inc(s.l_ready, 1)
                step.step(nc.vector.tensor_copy(gl[:, 4 * c:4 * c + 4].unsqueeze(2), heads(er[:, c, :])[:, :, P - 1:P]))
                step.mark(tt(heads(er[:, c, :]), heads(er[:, c, :]), raw[:, 0:DN, 3 + c * P:3 + (c + 1) * P], ALU.mult))
                bank = banks.take()
                tt(at[:, c, :], at[:, c, :], bank[:, :], ALU.mult).then_inc(s.vec_read, 1)
                bank = banks.take()
                step.mark(tt(heads(kbg[:, c, :]), heads(bank[:, :]), over(bg[:, 4 * c:4 * c + 4].unsqueeze(2), (P, DN, P)), ALU.mult))
                tt(heads(kdec[:, c, :]), heads(bank[:, :]), over(ekd[:, 4 * c:4 * c + 4].unsqueeze(2), (P, DN, P)), ALU.mult).then_inc(s.vec_read, 1)
                step.step(tt(heads(x[c]), heads(lm[:, c, :]), over(m.c("join1_low").unsqueeze(1), (P, DN, P)), ALU.mult))
                step.mark(tt(heads(x[c]), over(m.c("ident").unsqueeze(1), (P, DN, P)), heads(x[c]), ALU.subtract))
            for c in range(NT):
                v.wait_ge(s.act_read, lt_count[c])
                step.step(tt(heads(xt[:, c, :]), heads(lt[:, c, :]), over(m.c("join1").unsqueeze(1), (P, DN, P)), ALU.mult))
                tt(heads(xt[:, c, :]), over(m.c("ident").unsqueeze(1), (P, DN, P)), heads(xt[:, c, :]), ALU.subtract).then_inc(s.x_ready, 1)
            for lv in range(len(JOINS)):
                for c in range(NT):
                    v.wait_ge(s.x_ready, lv * NT + c + 1)
                    if lv < len(JOINS) - 1:
                        bank = banks.take()
                        tt(x[c], x[c], bank[:, :], ALU.subtract).then_inc(s.vec_read, 1)
                    bank = banks.take()
                    tt(xt[:, c, :], xt[:, c, :], bank[:, :], ALU.subtract).then_inc(s.vec_read, 1)
                    banks.settle()
                    v.sem_inc(s.x_ready, 1)
            for c in range(NT):
                if c:
                    bank = banks.take()
                    v.wait_ge(s.vec_read, banks.n - 1)
                    tt(vn[:, :], lm[:, c, :], bank[:, :], ALU.subtract).then_inc(s.vec_read, 1)
                    banks.settle()
                    v.sem_inc(s.vn_ready, 1)
                if c < NT - 1:
                    bank = banks.take()
                    if c == 0:
                        nc.vector.tensor_copy(state[:, :], bank[:, :]).then_inc(s.vec_read, 1)
                    else:
                        for h in range(DN):
                            n = 4 * c + h
                            ins = stt(out=state[:, hs(h)], in0=state[:, hs(h)], scalar=gl[:, n:n + 1], in1=bank[:, hs(h)], op0=ALU.mult, op1=ALU.add)
                            if h < DN - 1:
                                step.mark(ins)
                        ins.then_inc(s.vec_read, 1)
                    banks.settle()
                    step.settle()
                    v.sem_inc(s.state_ready, 1)
            v.wait_ge(s.rows_root, 2)
            nc.vector.reciprocal(rows[:, :], rows[:, :]).then_inc(s.rows_ready, 1)
            for h in range(DN):
                bank = banks.take()
                tt(m.bT[:, h, :], m.bT[:, h, :], bank[:, :], ALU.mult).then_inc(s.vec_read, 1)
                banks.settle()
                step.mark(stt(out=m.bT[:, h, :], in0=m.bT[:, h, :], scalar=m.out_gain[:, 0:1], in1=raw[:, h, 3:], op0=ALU.mult, op1=ALU.mult))

        @block.gpsimd
        def _(pool):
            for lv, b in enumerate(JOINS):
                for c in range(NT):
                    pool.wait_ge(s.act_read, lt_count[c])
                    n = lv * NT + c
                    if n >= 2:
                        pool.wait_ge(s.x_ready, NT + n - 1)
                        pool.wait_ge(s.ct_ready, n)
                    nc.gpsimd.tensor_tensor(heads(ct[:, c % 2, :]), heads(lt[:, c, :]), over(m.c(f"join{b}").unsqueeze(1), (P, DN, P)),
                                            ALU.mult).then_inc(s.ct_ready, 1)
    clear(nc, s)



def phase_combine(m, layer):
    nc, io = m.nc, m.io
    with ExitStack() as ctx:
        s = semaphores(nc, ctx, COMMON + " out_w sig_ready comb_ready")
        sb = lambda n, shape, dt=F32: ctx.enter_context(nc.sbuf_tensor(n, shape, dt))
        wa = sb("w_a", [P, 2, D])
        wb = sb("w_b", [P, 4, D])
        wv = sb("w_cv", [P, 2, D])
        wg = sb("w_cg", [P, 2, D])
        sig = sb("sig", [P, 4, 2, T])
        tmp = sb("comb_tmp", [P, 4, T])
        comb = sb("comb", [P, KD, T])
        rows = []
        for mm_ in range(KD // 2):
            rows += [(weight(io.w_in, layer, 0, KD, COL_GATES + br * D + mm_ * PANEL, PANEL), KD, PANEL) for br in range(3)]
        rows += [(weight(io.w_out, layer, 0, KD, n * PANEL, PANEL), KD, PANEL) for n in range(4)]
        panels = Panels(m, s, rows)
        block = ctx.enter_context(nc.Block())

        @block.tensor
        def _(pe):
            to_act = Banks(pe, m.banks[0:3], s.act_filled, s.act_read)
            to_vec = Banks(pe, m.banks[3:6], s.vec_filled, s.vec_read)

            def product(banks, pairs, cols=slice(0, T)):
                bank = banks.open()
                for n, (a, b) in enumerate(pairs):
                    ins = nc.tensor.matmul(bank[:, cols], a, b, start=(n == 0), stop=(n == len(pairs) - 1))
                ins.then_inc(banks.filled, 1)

            for mp in range(KD // 2):
                gates = [panel_view(panels.landed(pe, 3 * mp + br), KD) for br in range(3)]
                for half in range(2):
                    mt = 2 * mp + half
                    cols = slice(mt * P, (mt + 1) * P)
                    for br in range(3):
                        w = gates[br]
                        product(to_act, [(w[:, k, half * P:(half + 1) * P], m.hT[:, k, :]) for k in range(KD)])
                    if mt == 0:
                        pe.wait_ge(s.out_w, 16 * 4)
                    product(to_act, [(wg[:, k, cols], m.sT[:, k, :]) for k in range(2)])
                    product(to_vec, [(wa[:, k, cols], m.aT[:, k, :]) for k in range(2)])
                    product(to_vec, [(wb[:, k, cols], m.bT[:, k, :]) for k in range(4)])
                    product(to_vec, [(wv[:, k, cols], m.sT[:, k, :]) for k in range(2)])
                for br in range(3):
                    panels.released.append((s.vec_filled, to_vec.n))
            pe.wait_ge(s.comb_ready, KD)
            for n in range(4):
                w = panel_view(panels.landed(pe, 3 * KD // 2 + n), KD)
                for t in range(NT):
                    product(to_vec, [(comb[:, k, t * P:(t + 1) * P], w[:, k, :]) for k in range(KD)], slice(0, PANEL))
                panels.released.append((s.vec_filled, to_vec.n))

        @block.sync
        def _(sp):
            panels.stream(sp)

        @block.scalar
        def _(act):
            for dst, src, kt in ((wg, io.w_c_gate, 2), (wa, io.w_a_out, 2), (wb, io.w_b_out, 4), (wv, io.w_c_val, 2)):
                act.dma_start(dst[:, :, :], weight(src, layer, 0, kt, 0, D)).then_inc(s.out_w, 16)
            banks = Reader(act, m.banks[0:3], s.act_filled, s.act_read)
            for mt in range(KD):
                if mt >= 2:
                    act.wait_ge(s.comb_ready, mt - 1)
                for br in range(4):
                    bank = banks.take()
                    nc.scalar.activation(sig[:, br, mt % 2, :], bank[:, :], ACT.Sigmoid).then_inc(s.act_read, 1)

        @block.vector
        def _(v):
            step = Link(v, s.vec_step)
            banks = Reader(v, m.banks[3:6], s.vec_filled, s.vec_read)
            tt = nc.vector.tensor_tensor
            for mt in range(KD):
                v.wait_ge(s.act_read, 4 * mt + 4)
                if mt:
                    v.wait_ge(s.comb_ready, mt)
                for n, br in enumerate((0, 1, 3)):
                    bank = banks.take()
                    tt(tmp[:, n], sig[:, br, mt % 2, :], bank[:, :], ALU.mult).then_inc(s.vec_read, 1)
                banks.settle()
                step.mark(tt(tmp[:, 3], tmp[:, 2], sig[:, 2, mt % 2, :], ALU.mult))
                step.step(tt(tmp[:, 0], tmp[:, 0], tmp[:, 1], ALU.add))
                tt(comb[:, mt, :], tmp[:, 0], tmp[:, 3], ALU.add).then_inc(s.comb_ready, 1)
            for n in range(4):
                for t in range(NT):
                    bank = banks.take()
                    xs = m.x[:, t, n * PANEL:(n + 1) * PANEL]
                    tt(xs, xs, bank[:, 0:PANEL], ALU.add).then_inc(s.vec_read, 1)
    clear(nc, s)



def phase_query(m, layer):
    nc, io = m.nc, m.io
    with ExitStack() as ctx:
        s = semaphores(nc, ctx, COMMON + " rms_ready h_ready")
        sb = lambda n, shape, dt=F32: ctx.enter_context(nc.sbuf_tensor(n, shape, dt))
        gain = sb("gain_ffn", [P, D])
        small = sb("small5", [P, 16])
        keys = sb("keys", [P, 2, KEYS])
        qry = sb("qry", [P, 2 * PEER_HEADS, T])
        ss, rms, rstd = small[:, 0:4], small[:, 4:8], small[:, 8:12]
        panels = Panels(m, s, [(weight(io.peer_w_query, layer, 0, KD, n * PANEL, PANEL), KD, PANEL) for n in range(8)])
        block = ctx.enter_context(nc.Block())

        @block.tensor
        def _(pe):
            to_act = Banks(pe, m.banks[0:3], s.act_filled, s.act_read)
            to_vec = Banks(pe, m.banks[3:6], s.vec_filled, s.vec_read)
            norm_transposes(m, s, pe, to_act, to_vec, m.h)
            for n in range(8):
                w = panel_view(panels.landed(pe, n), KD)
                for half, banks in ((0, to_act), (1, to_vec)):
                    bank = banks.open()
                    for k in range(KD):
                        ins = nc.tensor.matmul(bank[:, :], w[:, k, half * P:(half + 1) * P], m.hT[:, k, :],
                                               start=(k == 0), stop=(k == KD - 1))
                    ins.then_inc(banks.filled, 1)
                panels.released.append((s.vec_filled, to_vec.n))
            to_act.all_read()
            to_vec.all_read()
            pe.wait_ge(s.params_in, 16 * 3)
            for t in range(NT):
                for hp in range(PEER_HEADS // 2):
                    banks = (to_act, to_vec)[hp % 2]
                    bank = banks.open()
                    for q in range(4):
                        ins = nc.tensor.matmul(bank[:, q * KEYS:(q + 1) * KEYS], qry[:, 4 * hp + q, t * P:(t + 1) * P],
                                               keys[:, q % 2, :], start=True, stop=True)
                    ins.then_inc(banks.filled, 1)

        @block.sync
        def _(sp):
            sp.dma_start(gain[:, :], io.norm_ffn[bass.ds(layer, 1), :].partition_broadcast(P).rearrange("p l d -> p (l d)")).then_inc(s.params_in, 16)
            for n, a in enumerate((io.peer_keys1, io.peer_keys2)):
                sp.dma_start(keys[:, n, :], a[bass.ds(layer, 1)].rearrange("l d k -> d (l k)")).then_inc(s.params_in, 16)
            panels.stream(sp)

        @block.scalar
        def _(act):
            step = Link(act, s.act_step)
            banks = Reader(act, m.banks[0:3], s.act_filled, s.act_read)
            norm_scalar(m, s, act, step, ss, rms, m.h)
            norm_copy(m, act, banks, 0)
            for n in range(8):
                bank = banks.take()
                nc.scalar.activation(qry[:, 2 * n, :], bank[:, :], ACT.Copy).then_inc(s.act_read, 1)
            for t in range(NT):
                for hp in (0, 2):
                    bank = banks.take()
                    nc.scalar.activation(m.scores[:, t, hp * 512:hp * 512 + 512], bank[:, :], ACT.Copy).then_inc(s.act_read, 1)

        @block.vector
        def _(v):
            step = Link(v, s.vec_step)
            banks = Reader(v, m.banks[3:6], s.vec_filled, s.vec_read)
            v.wait_ge(s.params_in, 16 * 3)
            norm_vector(m, s, v, step, rms, rstd, gain[:, :], m.h)
            norm_copy(m, v, banks, 1)
            for n in range(8):
                bank = banks.take()
                nc.vector.tensor_copy(qry[:, 2 * n + 1, :], bank[:, :]).then_inc(s.vec_read, 1)
            for t in range(NT):
                for hp in (1, 3):
                    bank = banks.take()
                    nc.vector.tensor_copy(m.scores[:, t, hp * 512:hp * 512 + 512], bank[:, :]).then_inc(s.vec_read, 1)
    clear(nc, s)



def phase_embed(m, layer):
    nc, io = m.nc, m.io
    with ExitStack() as ctx:
        s = semaphores(nc, ctx, COMMON + " rms_ready h_ready sig_used")
        sb = lambda n, shape, dt=F32: ctx.enter_context(nc.sbuf_tensor(n, shape, dt))
        gain = sb("gain_ple", [P, D])
        small = sb("small7", [P, 16])
        h = sb("h_ple", [P, NT, D])
        pT = sb("pT", [P, 2, T])
        wp = sb("w_ple", [P, 2, D])
        sig = sb("sig_ple", [P, 2, PANEL])
        ss, rms, rstd = small[:, 0:4], small[:, 4:8], small[:, 8:12]
        panels = Panels(m, s, [(weight(io.ple_w_gate, layer, 0, KD, n * PANEL, PANEL), KD, PANEL) for n in range(4)])
        block = ctx.enter_context(nc.Block())

        @block.tensor
        def _(pe):
            to_act = Banks(pe, m.banks[0:3], s.act_filled, s.act_read)
            to_vec = Banks(pe, m.banks[3:6], s.vec_filled, s.vec_read)
            norm_transposes(m, s, pe, to_act, to_vec, h)
            pe.wait_ge(s.params_in, 16 * 3)
            for n in range(4):
                w = panel_view(panels.landed(pe, n), KD)
                for t in range(NT):
                    tok = slice(t * P, (t + 1) * P)
                    bank = to_act.open()
                    for k in range(KD):
                        ins = nc.tensor.matmul(bank[:, 0:PANEL], m.hT[:, k, tok], w[:, k, :], start=(k == 0), stop=(k == KD - 1))
                    ins.then_inc(s.act_filled, 1)
                    bank = to_vec.open()
                    for k in range(2):
                        ins = nc.tensor.matmul(bank[:, 0:PANEL], pT[:, k, tok], wp[:, k, n * PANEL:(n + 1) * PANEL], start=(k == 0), stop=(k == 1))
                    ins.then_inc(s.vec_filled, 1)
                panels.released.append((s.act_filled, to_act.n))

        @block.sync
        def _(sp):
            sp.dma_start(gain[:, :], io.ple_norm[bass.ds(layer, 1), :].partition_broadcast(P).rearrange("p l d -> p (l d)")).then_inc(s.params_in, 16)
            sp.dma_start(pT[:, :, :], weight(io.p, layer, 0, 2, 0, T)).then_inc(s.params_in, 16)
            sp.dma_start(wp[:, :, :], weight(io.ple_w, layer, 0, 2, 0, D)).then_inc(s.params_in, 16)
            panels.stream(sp)

        @block.scalar
        def _(act):
            step = Link(act, s.act_step)
            banks = Reader(act, m.banks[0:3], s.act_filled, s.act_read)
            norm_scalar(m, s, act, step, ss, rms, h)
            norm_copy(m, act, banks, 0)
            for i in range(4 * NT):
                bank = banks.take()
                if i >= 2:
                    act.wait_ge(s.sig_used, i - 1)
                nc.scalar.activation(sig[:, i % 2, :], bank[:, 0:PANEL], ACT.Sigmoid).then_inc(s.act_read, 1)

        @block.vector
        def _(v):
            step = Link(v, s.vec_step)
            banks = Reader(v, m.banks[3:6], s.vec_filled, s.vec_read)
            v.wait_ge(s.params_in, 16 * 3)
            norm_vector(m, s, v, step, rms, rstd, gain[:, :], h)
            norm_copy(m, v, banks, 1)
            for i in range(4 * NT):
                n, t = i // NT, i % NT
                bank = banks.take()
                v.wait_ge(s.act_read, NT + i + 1)
                nc.vector.tensor_tensor(sig[:, i % 2, :], sig[:, i % 2, :], bank[:, 0:PANEL], ALU.mult).then_inc(s.vec_read, 1)
                banks.settle()
                xs = m.x[:, t, n * PANEL:(n + 1) * PANEL]
                nc.vector.tensor_tensor(xs, xs, sig[:, i % 2, :], ALU.add).then_inc(s.sig_used, 1)
    clear(nc, s)



RINGS = 8
TURN = 2 * TOPK
TURNS = PEER_HEADS // 2
LEAST = -3e38


def phase_peer(m, layer):
    nc, io = m.nc, m.io
    with ExitStack() as ctx:
        s = semaphores(nc, ctx, "vec_step topped exp_done selected u_free v_free out_free tanh_in tanh_done w_ready dg_done idx_here paced paced_v")
        sb = lambda n, shape, dt=F32: ctx.enter_context(nc.sbuf_tensor(n, shape, dt))
        u = sb("u_rows", [P, RINGS, D])
        vr = sb("v_rows", [P, RINGS, D])
        dg = sb("dg", [P, RINGS, P])
        hcur = sb("h_tile", [P, D])
        sc = sb("sel_s", [P, 2, KEYS])
        sc2 = sb("sel_s2", [P, 2, KEYS])
        val = sb("sel_v", [P, 2, TOPK])
        vi = sb("sel_i", [P, 2, TOPK], U32)
        vif = sb("sel_if", [P, 2, TOPK])
        cand = sb("sel_c", [P, TOPK, TOPK])
        cand2 = sb("sel_c2", [P, TOPK, TOPK])
        top = sb("sel_top", [P, TOPK])
        pos = sb("sel_pos", [P, TOPK], U32)
        ab = sb("sel_ab", [P, 2, TOPK], U32)
        abf = sb("sel_abf", [P, 2, TOPK])
        hit = sb("sel_hit", [P, 2 * TOPK, TOPK])
        chosen = sb("sel_ch", [P, 2, TOPK])
        expo = sb("sel_e", [P, TOPK])
        one = sb("sel_one", [P, 8])
        idx_all = sb("idx_all", [P, NT * PEER_HEADS * TOPK], U32)
        gate_all = sb("gate_all", [P, NT * PEER_HEADS * TOPK])
        idx = [sb(f"idx{k}", [P, TOPK], U32) for k in range(2)]
        act_u = sb("act_u", [P, TURN])
        inner = sb("act_in", [P, TURN])
        th = sb("act_th", [P, TURN])
        w = sb("act_w", [P, TURN])
        scores = m.scores[:, :, :].rearrange("p t c -> p (t c)")
        hflat = m.h[:, :, :].rearrange("p t d -> p (t d)")
        xflat = m.x[:, :, :].rearrange("p t d -> p (t d)")
        tables = io.peer_u.rearrange("l e d -> (l e) d"), io.peer_v.rearrange("l e d -> (l e) d")
        out_banks = [(m.banks[4], m.banks[5]), (m.banks[6], m.banks[7])]

        def turns(eng, tile, turn):
            with eng.Fori(0, NT - 1) as t:
                tile(t)
                with eng.Fori(0, TURNS) as q:
                    turn(t, q, t * TURNS + q, True)
            tile(NT - 1)
            with eng.Fori(0, TURNS) as q:
                turn(NT - 1, q, (NT - 1) * TURNS + q, False)

        def landed(eng, sems, b, n):
            uses = (layer * (NT * TURNS) + b) * (TURN // RINGS) + (n // RINGS + 1)
            eng.wait_ge(sems[n % RINGS], uses * 16)

        block = ctx.enter_context(nc.Block())

        @block.gpsimd
        def _(pool):
            pool.sem_inc(s.u_free, RINGS)
            pool.sem_inc(s.v_free, RINGS)
            pool.sem_inc(s.out_free, 2)

            def paced():
                pool.sem_inc(s.paced, 1)

            def turn(t, q, b, more):
                for hh in range(2):
                    pool.wait_ge(s.selected, b * 2 + (hh + 1))
                    paced()
                    nc.gpsimd.tensor_copy(idx[hh][:, :], idx_all[:, bass.ds((b * 2 + hh) * TOPK, TOPK)]).then_inc(s.idx_here, 1)
                    pool.wait_ge(s.idx_here, b * 2 + (hh + 1))
                    paced()
                    for g in range(TOPK // RINGS):
                        for free, rows, table, sems in ((s.u_free, u, tables[0], m.u_landed), (s.v_free, vr, tables[1], m.v_landed)):
                            for k in range(RINGS):
                                n = hh * TOPK + g * RINGS + k
                                pool.wait_ge(free, b * TURN + (n + 1))
                                paced()
                                nc.gpsimd.indirect_dma_start(
                                    out=rows[:, k, :], out_offset=None, in_=table,
                                    in_offset=bass.IndirectOffsetOnAxis(ap=idx[hh][:, g * RINGS + k:g * RINGS + k + 1], axis=0),
                                ).then_inc(sems[k], 16)

            turns(pool, lambda t: None, turn)

        @block.vector
        def _(v):
            step = Link(v, s.vec_step)
            tt, ts, stt = nc.vector.tensor_tensor, nc.vector.tensor_scalar, nc.vector.scalar_tensor_tensor

            def choose(j):
                step.step(nc.vector.tensor_copy(sc[:, :, :].rearrange("p a k -> p (a k)"), scores[:, bass.ds(j * 2 * KEYS, 2 * KEYS)]))
                for half in range(2):
                    step.mark(nc.vector.max(val[:, half, 0:8], sc[:, half, :]))
                step.settle()
                for half in range(2):
                    step.mark(nc.vector.max_index(vi[:, half, 0:8], val[:, half, 0:8], sc[:, half, :]))
                    step.mark(nc.vector.match_replace(sc2[:, half, :], val[:, half, 0:8], sc[:, half, :], LEAST))
                step.settle()
                for half in range(2):
                    step.mark(nc.vector.max(val[:, half, 8:16], sc2[:, half, :]))
                step.settle()
                for half in range(2):
                    step.mark(nc.vector.max_index(vi[:, half, 8:16], val[:, half, 8:16], sc2[:, half, :]))
                step.mark(tt(cand[:, :, :], over(val[:, 0, :].unsqueeze(2), (P, TOPK, TOPK)), over(val[:, 1, :].unsqueeze(1), (P, TOPK, TOPK)), ALU.add))
                step.settle()
                cf, cf2 = (a[:, :, :].rearrange("p a b -> p (a b)") for a in (cand, cand2))
                step.mark(nc.vector.tensor_copy(vif[:, :, :], vi[:, :, :]))
                step.step(nc.vector.max(top[:, 0:8], cf))
                step.mark(ts(one[:, 0:1], top[:, 0:1], -1.0, None, ALU.mult))
                step.mark(nc.vector.max_index(pos[:, 0:8], top[:, 0:8], cf))
                step.step(nc.vector.match_replace(cf2, top[:, 0:8], cf, LEAST))
                nc.vector.max(top[:, 8:16], cf2).then_inc(s.topped, 1)
                v.wait_ge(s.topped, j + 1)
                v.sem_inc(s.paced_v, 1)
                step.step(nc.vector.max_index(pos[:, 8:16], top[:, 8:16], cf2))
                step.mark(ts(ab[:, 0, :], pos[:, :], 4, None, ALU.logical_shift_right))
                step.step(ts(ab[:, 1, :], pos[:, :], 15, None, ALU.bitwise_and))
                step.step(nc.vector.tensor_copy(abf[:, :, :], ab[:, :, :]))
                step.step(tt(hit[:, :, :], over(abf[:, :, :].rearrange("p a k -> p (a k)").unsqueeze(2), (P, 2 * TOPK, TOPK)),
                             over(m.c("iota").unsqueeze(1), (P, 2 * TOPK, TOPK)), ALU.is_equal))
                h4 = hit[:, :, :].rearrange("p (a k) n -> p a k n", a=2)
                step.step(tt(h4, h4, over(vif[:, :, :].unsqueeze(2), (P, 2, TOPK, TOPK)), ALU.mult))
                step.step(nc.vector.tensor_reduce(chosen[:, :, :].rearrange("p a k -> p (a k)"), hit[:, :, :], AX_X, ALU.add))
                step.step(stt(out=chosen[:, 0, :], in0=chosen[:, 0, :], scalar=float(KEYS), in1=chosen[:, 1, :], op0=ALU.mult, op1=ALU.add))
                step.mark(ts(idx_all[:, bass.ds(j * TOPK, TOPK)], chosen[:, 0, :], m.row_base[:, 0:1], None, ALU.add))
                v.wait_ge(s.exp_done, j + 1)
                step.step(nc.vector.reciprocal(one[:, 2:3], one[:, 1:2]))
                step.step(ts(gate_all[:, bass.ds(j * TOPK, TOPK)], expo[:, :], one[:, 2:3], None, ALU.mult))
                v.sem_inc(s.selected, 1)
                step.restart()

            def group(b, g):
                at = slice(g * RINGS, (g + 1) * RINGS)
                for k in range(RINGS):
                    n = g * RINGS + k
                    landed(v, m.u_landed, b, n)
                    nc.vector.tensor_tensor_reduce(out=u[:, k, :], in0=u[:, k, :], in1=hcur[:, :], scale=1.0, scalar=0.0,
                                                   op0=ALU.mult, op1=ALU.add, accum_out=act_u[:, n:n + 1]).then_inc(s.u_free, 1)
                v.wait_ge(s.u_free, b * TURN + ((g + 2) * RINGS))
                step.step(tt(inner[:, at], act_u[:, at], act_u[:, at], ALU.mult))
                step.step(ts(inner[:, at], inner[:, at], 0.044715, 1.0, ALU.mult, ALU.add))
                tt(inner[:, at], inner[:, at], act_u[:, at], ALU.mult).then_inc(s.tanh_in, 1)
                v.wait_ge(s.tanh_done, b * 4 + (g + 1))
                step.step(stt(out=th[:, at], in0=th[:, at], scalar=1.0, in1=act_u[:, at], op0=ALU.add, op1=ALU.mult))
                stt(out=w[:, at], in0=th[:, at], scalar=0.5, in1=gate_all[:, bass.ds((b * 4 + g) * RINGS, RINGS)],
                    op0=ALU.mult, op1=ALU.mult).then_inc(s.w_ready, 1)

            def add_out(t, b, hh):
                v.wait_ge(s.v_free, b * TURN + (RINGS + TOPK * (hh + 1)))
                v.sem_inc(s.paced_v, 1)
                for half in range(2):
                    xs = xflat[:, bass.ds(t * D + half * 512, 512)]
                    step.mark(tt(xs, xs, out_banks[hh][half][:, :], ALU.add))
                step.settle()
                v.sem_inc(s.out_free, 1)

            def tile(t):
                step.step(nc.vector.tensor_copy(hcur[:, :], hflat[:, bass.ds(t * D, D)]))
                step.restart()

            def turn(t, q, b, more):
                group(b, 0)
                group(b, 1)
                step.restart()
                if more:
                    choose(b * 2 + PEER_HEADS)
                group(b, 2)
                add_out(t, b, 0)
                group(b, 3)
                step.restart()
                if more:
                    choose(b * 2 + (PEER_HEADS + 1))
                add_out(t, b, 1)
                step.restart()

            with v.Fori(0, PEER_HEADS) as j:
                choose(j)
            turns(v, tile, turn)
            step.step(ts(m.row_base[:, :], m.row_base[:, :], float(EXPERTS), None, ALU.add))

        @block.scalar
        def _(act):
            def weigh(j):
                act.wait_ge(s.topped, j + 1)
                nc.scalar.activation(expo[:, :], top[:, :], ACT.Exp, bias=one[:, 0:1], accum_out=one[:, 1:2]).then_inc(s.exp_done, 1)

            def group(b, g):
                at = slice(g * RINGS, (g + 1) * RINGS)
                act.wait_ge(s.tanh_in, b * 4 + (g + 1))
                nc.scalar.activation(th[:, at], inner[:, at], ACT.Tanh, scale=0.7978845608028654).then_inc(s.tanh_done, 1)
                act.wait_ge(s.w_ready, b * 4 + (g + 1))
                for k in range(RINGS):
                    n = g * RINGS + k
                    act.wait_ge(s.v_free, b * TURN + (n + 1))
                    nc.scalar.activation(dg[:, k, :], m.c("ident"), ACT.Copy, scale=w[:, n:n + 1]).then_inc(s.dg_done, 1)

            def turn(t, q, b, more):
                group(b, 0)
                group(b, 1)
                if more:
                    weigh(b * 2 + PEER_HEADS)
                group(b, 2)
                group(b, 3)
                if more:
                    weigh(b * 2 + (PEER_HEADS + 1))

            with act.Fori(0, PEER_HEADS) as j:
                weigh(j)
            turns(act, lambda t: None, turn)

        @block.tensor
        def _(pe):
            def turn(t, q, b, more):
                for hh in range(2):
                    pe.wait_ge(s.out_free, b * 2 + (hh + 1))
                    for i in range(TOPK):
                        n = hh * TOPK + i
                        landed(pe, m.v_landed, b, n)
                        pe.wait_ge(s.dg_done, b * TURN + (n + 1))
                        for half in range(2):
                            ins = nc.tensor.matmul(out_banks[hh][half][:, :], dg[:, n % RINGS, :], vr[:, n % RINGS, half * 512:half * 512 + 512],
                                                   start=(i == 0), stop=(i == TOPK - 1))
                        ins.then_inc(s.v_free, 1)

            turns(pe, lambda t: None, turn)
    clear(nc, s)


def decoder_trunk(nc, io, phases="1234567"):
    with ExitStack() as ctx:
        sb = lambda n, shape, dt=F32: ctx.enter_context(nc.sbuf_tensor(n, shape, dt))
        once = semaphores(nc, ctx, "loaded stored")
        swdge = [ctx.enter_context(nc.semaphore(f"{n}_landed{k}")) for n in "uv" for k in range(RINGS)]
        m = Machine()
        m.nc, m.io, m.u_landed, m.v_landed = nc, io, swdge[:RINGS], swdge[RINGS:]
        m.banks = [ctx.enter_context(nc.psum_tensor(f"bank{k}", [P, 512], F32)) for k in range(8)]
        consts = sb("consts", [P, CONSTS.shape[1]])
        m.c = lambda name: consts[:, WHERE[name][0]:WHERE[name][0] + WHERE[name][1]]
        m.x = sb("x", [P, NT, D])
        m.row_base = sb("row_base", [P, 1])

        with nc.Block() as block:
            @block.sync
            def _(sp):
                sp.dma_start(consts[:, :], io.consts).then_inc(once.loaded, 16)
                sp.dma_start(m.x[:, :, :], io.x.rearrange("b (t p) d -> p (b t) d", p=P)).then_inc(once.loaded, 16)
                sp.wait_ge(once.loaded, 32)

            @block.vector
            def _(v):
                nc.vector.memset(m.row_base[:, :], 0.0)

        with nc.Fori(0, DEPTH) as layer:
            with ExitStack() as mix:
                sm = lambda n, shape, dt=F32: mix.enter_context(nc.sbuf_tensor(n, shape, dt))
                m.hT = sm("hT", [P, KD, T])
                ring = sm("ring", [P, RING, KD * PANEL])
                m.ring = ring
                m.aT = sm("aT", [P, 2, T])
                m.sT = sm("sT", [P, 2, T])
                m.ba = sm("ba", [P, NT, 2 * DN])
                m.conv_w = sm("conv_w", [P, 3 * DN, 4])
                m.a_log = sm("a_log", [P, DN])
                m.dt_bias = sm("dt_bias", [P, DN])
                m.out_gain = sm("out_gain", [P, 1])
                with ExitStack() as front:
                    sf = lambda n, shape, dt=F32: front.enter_context(nc.sbuf_tensor(n, shape, dt))
                    m.work_a = sf("work_a", [P, NT * D])
                    m.qkT = m.work_a[:, :].rearrange("p (b n) -> p b n", b=8)
                    m.att_qk = sf("att_qk", [P, 4, QK_HEADS * HEAD])
                    m.att_v = sf("att_v", [P, 4, SLOTS * HEAD])
                    m.uT = sf("uT", [P, 2, T])
                    m.rot = sf("rot", [P, 2, 8, T])
                    m.s5_in = sf("s5_in", [P, 2, 8 * P])
                    m.s5_out = sf("s5_out", [P, 2, 8 * P])
                    m.s5_d = sf("s5_d", [P, 2])
                    m.mag = sf("mag", [P, 8])
                    m.seed = sf("seed", [P, 2, 8])
                    if "1" in phases:
                        phase_project(m, layer)
                    if "2" in phases:
                        phase_attend(m, layer)
                m.bT = sm("bT", [P, DN, T])
                if "3" in phases:
                    phase_deltanet(m, layer)
                if "4" in phases:
                    phase_combine(m, layer)
            with ExitStack() as ffn:
                sf = lambda n, shape, dt=F32: ffn.enter_context(nc.sbuf_tensor(n, shape, dt))
                m.h = sf("h", [P, NT, D])
                m.scores = sf("scores", [P, NT, 2 * PEER_HEADS * KEYS])
                with ExitStack() as front:
                    m.hT = front.enter_context(nc.sbuf_tensor("hT_ffn", [P, KD, T], F32))
                    m.ring = front.enter_context(nc.sbuf_tensor("ring_ffn", [P, RING, KD * PANEL], F32))
                    if "5" in phases:
                        phase_query(m, layer)
                if "6" in phases:
                    phase_peer(m, layer)
            with ExitStack() as back:
                m.hT = back.enter_context(nc.sbuf_tensor("hT_ple", [P, KD, T], F32))
                m.ring = back.enter_context(nc.sbuf_tensor("ring_ple", [P, RING, KD * PANEL], F32))
                if "7" in phases:
                    phase_embed(m, layer)

        with nc.Block() as block:
            @block.sync
            def _(sp):
                sp.dma_start(io.out.rearrange("b (t p) d -> p (b t) d", p=P), m.x[:, :, :]).then_inc(once.stored, 16)
                sp.wait_ge(once.stored, 16)


def kernel(**inputs):
    import concourse.bacc as bacc
    from concourse.bass_utils import run_bass_kernel_spmd

    a = {k: np.asarray(v) for k, v in inputs.items()}
    n = DEPTH
    swap = lambda t: np.ascontiguousarray(np.swapaxes(t, -1, -2))
    a["dn_conv"] = np.ascontiguousarray(a["dn_conv"].reshape(n, 4, 3 * DN, P).transpose(0, 3, 2, 1))
    a["s5_a_re"] = swap(a["s5_a_re"].reshape(n, S5_BLOCKS, P))
    a["s5_a_im"] = swap(a["s5_a_im"].reshape(n, S5_BLOCKS, P))
    a["s5_b_re"] = a["s5_b_re"].reshape(n, S5_BLOCKS * P, 16)
    a["s5_b_im"] = a["s5_b_im"].reshape(n, S5_BLOCKS * P, 16)
    a["s5_c_re"] = swap(a["s5_c_re"]).reshape(n, S5_BLOCKS * P, 16)
    a["s5_c_im"] = swap(a["s5_c_im"]).reshape(n, S5_BLOCKS * P, 16)
    a["s5_d"] = swap(a["s5_d"].reshape(n, 2, P))
    a["s5_log_dt"] = swap(a["s5_log_dt"].reshape(n, S5_BLOCKS, 2))
    a["dn_out_gain"] = a["dn_out_gain"].reshape(n, P, 1)
    a["peer_keys1"] = swap(a["peer_keys1"])
    a["peer_keys2"] = swap(a["peer_keys2"])
    a["p"] = swap(a["p"].reshape(n, T, PLE))
    a["consts"] = CONSTS
    nc = bacc.Bacc("TRN2", target_bir_lowering=False, num_devices=1)
    arrays, aps = {}, {}
    for name, t in a.items():
        t = np.ascontiguousarray(t)
        arrays[f"in_{name}"] = t
        aps[name] = nc.dram_tensor(f"in_{name}", t.shape, mybir.dt.from_np(t.dtype), kind="ExternalInput").ap()
    aps["out"] = nc.dram_tensor("out_x", (1, T, D), F32, kind="ExternalOutput").ap()
    io = namedtuple("Arrays", list(aps))(*aps.values())
    decoder_trunk(nc, io)
    got = run_bass_kernel_spmd(nc, [arrays], core_ids=[0])
    return got.results[0]["out_x"]
```

```python
from collections import namedtuple
from contextlib import ExitStack

import numpy as np

import concourse.bass as bass
from concourse import mybir

F32 = mybir.dt.float32
U32 = mybir.dt.uint32
I32 = mybir.dt.int32
ALU = mybir.AluOpType
ACT = mybir.ActivationFunctionType
AX_X = mybir.AxisListType.X

P = 128
T = 512
NT = T // P
D = 1024
KD = D // P
DEPTH = 2
EPS = 1e-6

HEAD = 64
SLOTS = 4
GROUPS = 3
WINDOW = 128
QKV_ATT = (GROUPS + 2) * SLOTS * HEAD
QK_HEADS = (GROUPS + 1) * SLOTS
DN = 4
S5_BLOCKS = 8
S5_G = 16
PEER_HEADS = 8
KEYS = 128
TOPK = 16
EXPERTS = KEYS * KEYS
PLE = 256

COL_ATT = 0
COL_QKV = COL_ATT + QKV_ATT
COL_Z = COL_QKV + 3 * DN * P
COL_BA = COL_Z + DN * P
COL_U = COL_BA + 2 * DN
COL_GATES = COL_U + 256
IN_COLS = COL_GATES + 3 * D

PANEL = 256
RING = 3
BANKS = 3
NEG = -1e30
PI = float(np.pi)
TWO_PI_HI = 6.28125
TWO_PI_LO = float(2 * np.pi - 6.28125)
SLOPES = 2.0 ** (-8.0 * np.arange(1, GROUPS * SLOTS + 1) / (GROUPS * SLOTS))


def shape_constants():
    i = np.arange(P)[:, None]
    j = np.arange(P)[None, :]
    parts = {}
    parts["ident"] = np.eye(P)
    parts["ones"] = np.ones((P, P))
    parts["triu"] = i <= j
    parts["strict"] = np.where(i > j, 0.0, NEG)
    parts["incl_t"] = np.where(j >= i, 0.0, NEG)
    for b in (1, 2, 4, 8, 16, 32, 64):
        parts[f"join{b}"] = (i // (2 * b) == j // (2 * b)) & (j // b % 2 == 1) & (i // b % 2 == 0)
    parts["join1_low"] = ((i // 2 == j // 2) & (i % 2 == 1) & (j % 2 == 0))
    far = 1e33
    d = np.concatenate([4 * (i - j) + delta for delta in range(3, -4, -1)], axis=1)
    parts["dist_g0"] = np.where((d >= 0) & (d <= WINDOW), d, far)
    d = 4 * (i - j)
    parts["dist_g1"] = np.where(d >= 0, d, far)
    parts["dist_g2"] = np.where((d >= 0) & (d % 16 == 0), d, far)
    rows = np.zeros((P, 8, 8))
    rows[:, np.arange(8), np.arange(8)] = 1
    parts["to_row"] = rows.reshape(P, 64)
    spread = np.zeros((P, 8, P))
    for n in range(8):
        spread[n, n] = float(P) ** -0.5 if n < DN else 1.0
    parts["spread_qk"] = spread.reshape(P, 8 * P)
    spread = np.zeros((P, DN, P))
    for n in range(DN):
        spread[n, n] = 1.0
    parts["spread"] = spread.reshape(P, DN * P)
    parts["iota"] = np.broadcast_to(np.arange(TOPK), (P, TOPK))
    parts["eps"] = np.full((P, 1), EPS)
    where, at = {}, 0
    for name, a in parts.items():
        where[name] = (at, a.shape[1])
        at += a.shape[1]
    return np.concatenate([np.asarray(a, np.float32) for a in parts.values()], axis=1), where


CONSTS, WHERE = shape_constants()


class Link:

    def __init__(self, eng, sem):
        self.eng, self.sem, self.n = eng, sem, 0

    def mark(self, ins):
        self.n += 1
        ins.then_inc(self.sem, 1)

    def settle(self):
        self.eng.wait_ge(self.sem, self.n)

    def step(self, ins):
        self.mark(ins)
        self.settle()

    def restart(self):
        self.settle()
        self.eng.sem_clear(self.sem)
        self.n = 0


class Machine:
    pass


def over(ap, shape):
    return ap.to_broadcast(list(shape))


def semaphores(nc, ctx, names):
    names = names.split()
    return namedtuple("Semaphores", names)(*[ctx.enter_context(nc.semaphore(n)) for n in names])


def clear(nc, group):
    nums = sorted(s.num for s in group)
    assert nums[-1] - nums[0] == len(nums) - 1
    nc.all_engine_barrier(sems_to_clear=range(nums[0], nums[-1] + 1))


COMMON = "landed0 landed1 landed2 params_in act_filled act_read vec_filled vec_read act_step vec_step pool_step"


class Panels:

    def __init__(self, m, s, sources, early=0):
        self.m, self.sources, self.early = m, sources, early
        self.sems = s.landed0, s.landed1, s.landed2
        self.released = []

    def landed(self, pe, n):
        if n >= self.early:
            pe.wait_ge(self.sems[n % RING], 16 * ((n - self.early) // RING + 1))
        return self.m.ring[:, n % RING]

    def load(self, sp, n, source):
        src, kt, cols = source
        if n >= RING:
            sem, count = self.released[n - RING]
            sp.wait_ge(sem, count)
        dst = self.m.ring[:, n % RING].rearrange("p (k c) -> p k c", k=kt)[:, :, 0:cols]
        sp.dma_start(dst, src).then_inc(self.sems[n % RING], 16)

    def stream(self, sp, following=()):
        end = len(self.sources)
        for n in range(self.early, end):
            self.load(sp, n, self.sources[n])
        if following:
            for n in range(end, end + RING):
                self.load(sp, n, following[n % RING])
            for slot in range(RING):
                loads = len([n for n in range(self.early, end + RING) if n % RING == slot])
                sp.wait_ge(self.sems[slot], 16 * loads)


def panel_view(slot, kt, cols=None):
    v = slot.rearrange("p (k c) -> p k c", k=kt)
    return v if cols is None else v[:, :, 0:cols]


def weight(ap, layer, k0, kt, c0, cols):
    return ap[bass.ds(layer, 1), k0 * P:(k0 + kt) * P, c0:c0 + cols].rearrange("l (k p) c -> p (l k) c", p=P)


class Banks:

    def __init__(self, pe, banks, filled, read):
        self.pe, self.banks, self.filled, self.read, self.n = pe, banks, filled, read, 0

    def open(self):
        self.n += 1
        if self.n > len(self.banks):
            self.pe.wait_ge(self.read, self.n - len(self.banks))
        return self.banks[(self.n - 1) % len(self.banks)]

    def all_read(self):
        self.pe.wait_ge(self.read, self.n)


class Reader:

    def __init__(self, eng, banks, filled, read):
        self.eng, self.banks, self.filled, self.read, self.n = eng, banks, filled, read, 0

    def take(self):
        self.n += 1
        self.eng.wait_ge(self.filled, self.n)
        return self.banks[(self.n - 1) % len(self.banks)]

    def settle(self):
        self.eng.wait_ge(self.read, self.n)


def input_panels(io, layer, phase):
    cols = {"project": [COL_U] + [COL_ATT + n * PANEL for n in range(QKV_ATT // PANEL)],
            "deltanet": [COL_QKV + n * PANEL for n in range(4 * DN * P // PANEL)],
            "combine": [COL_GATES + br * D + n * PANEL for n in range(D // PANEL) for br in range(3)]}[phase]
    return [(weight(io.w_in, layer, 0, KD, c, PANEL), KD, PANEL) for c in cols]



def norm_scalar(m, s, act, step, ss, rms, h):
    for t in range(NT):
        step.mark(m.nc.scalar.activation(h[:, t], m.x[:, t], ACT.Square, accum_out=ss[:, t:t + 1]))
    step.settle()
    m.nc.scalar.activation(rms, ss, ACT.Sqrt, bias=m.c("eps"), scale=1.0 / D).then_inc(s.rms_ready, 1)


def norm_vector(m, s, v, step, rms, rstd, gain, h):
    v.wait_ge(s.rms_ready, 1)
    step.step(m.nc.vector.reciprocal(rstd, rms))
    for t in range(NT):
        m.nc.vector.scalar_tensor_tensor(out=h[:, t], in0=m.x[:, t], scalar=rstd[:, t:t + 1], in1=gain,
                                         op0=ALU.mult, op1=ALU.mult).then_inc(s.h_ready, 1)


def norm_transposes(m, s, pe, to_act, to_vec, h):
    for t in range(NT):
        pe.wait_ge(s.h_ready, t + 1)
        for half, banks in ((0, to_act), (1, to_vec)):
            bank = banks.open()
            for k in range(4):
                kk = 4 * half + k
                ins = m.nc.tensor.transpose(bank[:, k * P:(k + 1) * P], h[:, t, kk * P:(kk + 1) * P], m.c("ident"))
            ins.then_inc(banks.filled, 1)
    to_act.all_read()
    to_vec.all_read()


def norm_copy(m, eng, reader, half):
    for t in range(NT):
        bank = reader.take()
        dst = m.hT[:, 4 * half:4 * half + 4, t * P:(t + 1) * P]
        src = bank[:, :].rearrange("p (k n) -> p k n", k=4)
        if half == 0:
            m.nc.scalar.activation(dst, src, ACT.Copy).then_inc(reader.read, 1)
        else:
            m.nc.vector.tensor_copy(dst, src).then_inc(reader.read, 1)



def phase_project(m, layer):
    nc, io = m.nc, m.io
    with ExitStack() as ctx:
        s = semaphores(nc, ctx, COMMON + " rms_ready h_ready s5_to_act s5_from_act seed_ready bb_placed qk_sq qk_ss qk_rms qk_ready")
        sb = lambda n, shape, dt=F32: ctx.enter_context(nc.sbuf_tensor(n, shape, dt))
        gain = sb("gain_mix", [P, D])
        qk_gain = sb("qk_gain", [P, QK_HEADS * HEAD])
        small = sb("small1", [P, 256])
        s5s = sb("s5_small", [P, 26, 8])
        s5i = sb("s5_int", [P, 8], I32)
        bmat = sb("s5_b", [P, 2, 8, 16])
        cmat = sb("s5_c", [P, 2, 8, 16])
        bb = sb("s5_bb", [P, 2, 8, 16])
        bbt = sb("s5_bbt", [P, 4, 8, 16])
        bbd = sb("s5_bbd", [P, 2, 8 * P])
        pool_t = sb("rot_tmp", [P, 2, 4 * 256])
        pool_w = sb("rot_w", [P, 6, 4])
        h = m.work_a[:, :].rearrange("p (t d) -> p t d", t=NT)
        ss, rms, rstd = small[:, 0:4], small[:, 4:8], small[:, 8:12]
        qss, qrms, qrstd = small[:, 16:80], small[:, 80:144], small[:, 144:208]
        rows = input_panels(io, layer, "project")
        rows += [(weight(io.w_in, layer, 0, KD, COL_BA, 2 * DN), KD, 2 * DN)]
        panels = Panels(m, s, rows)
        NPARAM = 16

        block = ctx.enter_context(nc.Block())

        @block.tensor
        def _(pe):
            to_act = Banks(pe, m.banks[0:3], s.act_filled, s.act_read)
            to_vec = Banks(pe, m.banks[3:6], s.vec_filled, s.vec_read)
            norm_transposes(m, s, pe, to_act, to_vec, h)
            w = panel_view(panels.landed(pe, 0), KD)
            for mt in range(2):
                bank = to_act.open()
                for k in range(KD):
                    ins = nc.tensor.matmul(bank[:, :], w[:, k, mt * P:(mt + 1) * P], m.hT[:, k, :],
                                           start=(k == 0), stop=(k == KD - 1))
                ins.then_inc(s.act_filled, 1)
            panels.released.append((s.act_filled, to_act.n))
            for n in range(5):
                w = panel_view(panels.landed(pe, n + 1), KD)
                for r in range(4):
                    banks = (to_act, to_vec)[r % 2]
                    bank = banks.open()
                    for k in range(KD):
                        ins = nc.tensor.matmul(bank[:, 0:PANEL], m.hT[:, k, r::4], w[:, k, :],
                                               start=(k == 0), stop=(k == KD - 1))
                    ins.then_inc(banks.filled, 1)
                panels.released.append((s.vec_filled, to_vec.n))
            w = panel_view(panels.landed(pe, 6), KD)
            bank = to_vec.open()
            for c in range(NT):
                for k in range(KD):
                    ins = nc.tensor.matmul(bank[:, c * 8:c * 8 + 8], m.hT[:, k, c * P:(c + 1) * P], w[:, k, 0:8],
                                           start=(k == 0), stop=(k == KD - 1))
            ins.then_inc(s.vec_filled, 1)
            panels.released.append((s.vec_filled, to_vec.n))
            pe.wait_ge(s.bb_placed, 1)
            for part in range(2):
                for half in range(2):
                    bank = to_act.open()
                    for b in range(4):
                        at = (4 * half + b) * P
                        ins = nc.tensor.transpose(bank[:, b * P:(b + 1) * P], bbd[:, part, at:at + P], m.c("ident"))
                    ins.then_inc(s.act_filled, 1)
            pe.wait_ge(s.qk_ready, 1)
            for b in range(8):
                banks = (to_act, to_vec)[b % 2]
                bank = banks.open()
                for r in range(4):
                    ins = nc.tensor.transpose(bank[:, r * P:(r + 1) * P], m.att_qk[:, r, b * P:(b + 1) * P], m.c("ident"))
                ins.then_inc(banks.filled, 1)
            to_act.all_read()
            to_vec.all_read()

        @block.sync
        def _(sp):
            def load(dst, src):
                sp.dma_start(dst, src).then_inc(s.params_in, 16)
            load(gain[:, :], io.norm_mix[bass.ds(layer, 1), :].partition_broadcast(P).rearrange("p l d -> p (l d)"))
            for n in range(2):
                src = (io.att_q_gain, io.att_k_gain)[n][bass.ds(layer, 1), :].partition_broadcast(P)
                load(qk_gain[:, n * HEAD:(n + 1) * HEAD], src.rearrange("p l d -> p (l d)"))
            load(s5s[:, 0], io.s5_a_re[bass.ds(layer, 1)].rearrange("l p b -> p (l b)"))
            load(s5s[:, 1], io.s5_a_im[bass.ds(layer, 1)].rearrange("l p b -> p (l b)"))
            for hh in range(2):
                src = io.s5_log_dt[bass.ds(layer, 1), hh, :].partition_broadcast(64)
                load(s5s[64 * hh:64 * hh + 64, 2], src.rearrange("p l b -> p (l b)"))
            for n, a in enumerate((io.s5_b_re, io.s5_b_im)):
                load(bmat[:, n], a[bass.ds(layer, 1)].rearrange("l (b p) c -> p (l b) c", p=P))
            for n, a in enumerate((io.s5_c_re, io.s5_c_im)):
                load(cmat[:, n], a[bass.ds(layer, 1)].rearrange("l (b p) c -> p (l b) c", p=P))
            load(m.s5_d[:, :], io.s5_d[bass.ds(layer, 1)].rearrange("l p c -> p (l c)"))
            load(m.conv_w[:, :, :], io.dn_conv[bass.ds(layer, 1)].rearrange("l p b k -> p (l b) k"))
            load(m.a_log[:, :], io.dn_a_log[bass.ds(layer, 1), :].partition_broadcast(P).rearrange("p l d -> p (l d)"))
            load(m.dt_bias[:, :], io.dn_dt_bias[bass.ds(layer, 1), :].partition_broadcast(P).rearrange("p l d -> p (l d)"))
            load(m.out_gain[:, :], io.dn_out_gain[bass.ds(layer, 1)].rearrange("l p c -> p (l c)"))
            panels.stream(sp, input_panels(io, layer, "deltanet"))

        @block.scalar
        def _(act):
            step = Link(act, s.act_step)
            banks = Reader(act, m.banks[0:3], s.act_filled, s.act_read)
            norm_scalar(m, s, act, step, ss, rms, h)
            act.wait_ge(s.params_in, 16 * NPARAM)
            nc.scalar.activation(s5s[:, 3], s5s[:, 2], ACT.Exp).then_inc(s.s5_from_act, 1)
            act.wait_ge(s.s5_to_act, 1)
            nc.scalar.activation(m.mag[:, :], s5s[:, 4], ACT.Exp).then_inc(s.s5_from_act, 1)
            act.wait_ge(s.s5_to_act, 2)
            nc.scalar.activation(s5s[:, 8], s5s[:, 6], ACT.Sin).then_inc(s.s5_from_act, 1)
            nc.scalar.activation(s5s[:, 9], s5s[:, 7], ACT.Sin).then_inc(s.s5_from_act, 1)
            norm_copy(m, act, banks, 0)
            for mt in range(2):
                bank = banks.take()
                nc.scalar.activation(m.uT[:, mt, :], bank[:, :], ACT.Copy).then_inc(s.act_read, 1)
            for n in range(5):
                for r in (0, 2):
                    bank = banks.take()
                    dst = m.att_qk[:, r, n * PANEL:(n + 1) * PANEL] if n < 4 else m.att_v[:, r, :]
                    nc.scalar.activation(dst, bank[:, 0:PANEL], ACT.Copy).then_inc(s.act_read, 1)
            for part in range(2):
                for half in range(2):
                    bank = banks.take()
                    nc.scalar.activation(m.s5_in[:, part, half * 512:half * 512 + 512], bank[:, :], ACT.Copy).then_inc(s.act_read, 1)
            act.wait_ge(s.qk_sq, 1)
            banks.settle()
            nc.scalar.activation(m.work_a[:, :], m.att_qk[:, :, :].rearrange("p r c -> p (r c)"), ACT.Square).then_inc(s.qk_ss, 1)
            act.wait_ge(s.qk_sq, 2)
            nc.scalar.activation(qrms, qss, ACT.Sqrt, bias=m.c("eps"), scale=1.0 / HEAD).then_inc(s.qk_rms, 1)
            for b in range(0, 8, 2):
                bank = banks.take()
                nc.scalar.activation(m.qkT[:, b, :], bank[:, :], ACT.Copy).then_inc(s.act_read, 1)

        @block.vector
        def _(v):
            step = Link(v, s.vec_step)
            banks = Reader(v, m.banks[3:6], s.vec_filled, s.vec_read)
            tt, ts = nc.vector.tensor_tensor, nc.vector.tensor_scalar
            for b in (bbd, m.s5_out):
                step.mark(nc.vector.memset(b[:, :, :], 0.0))
            v.wait_ge(s.params_in, 16 * NPARAM)
            norm_vector(m, s, v, step, rms, rstd, gain[:, :], h)
            re, im, dt, ldt, th = s5s[:, 0], s5s[:, 1], s5s[:, 3], s5s[:, 4], s5s[:, 5]
            v.wait_ge(s.s5_from_act, 1)
            tt(ldt, re, dt, ALU.mult).then_inc(s.s5_to_act, 1)
            step.step(tt(th, im, dt, ALU.mult))
            step.step(ts(s5s[:, 6], th, 1.0 / (2 * PI), None, ALU.mult))
            step.step(nc.vector.tensor_copy(s5i[:, :], s5s[:, 6]))
            step.step(nc.vector.tensor_copy(s5s[:, 6], s5i[:, :]))
            step.step(nc.vector.scalar_tensor_tensor(out=s5s[:, 7], in0=s5s[:, 6], scalar=-TWO_PI_HI, in1=th, op0=ALU.mult, op1=ALU.add))
            step.step(nc.vector.scalar_tensor_tensor(out=s5s[:, 6], in0=s5s[:, 6], scalar=-TWO_PI_LO, in1=s5s[:, 7], op0=ALU.mult, op1=ALU.add))
            step.step(ts(s5s[:, 7], s5s[:, 6], PI / 2, None, ALU.add))
            for n in (6, 7):
                for cmp, bound, turn in ((ALU.is_gt, PI, -2 * PI), (ALU.is_lt, -PI, 2 * PI)):
                    step.step(ts(s5s[:, 10], s5s[:, n], bound, turn, cmp, ALU.mult))
                    step.step(tt(s5s[:, n], s5s[:, n], s5s[:, 10], ALU.add))
            step.step(ts(s5s[:, 6], s5s[:, 6], 3.1415925, -3.1415925, ALU.min, ALU.max))
            ts(s5s[:, 7], s5s[:, 7], 3.1415925, -3.1415925, ALU.min, ALU.max).then_inc(s.s5_to_act, 1)
            v.wait_ge(s.s5_from_act, 4)
            sin, cos = s5s[:, 8], s5s[:, 9]
            step.mark(nc.vector.tensor_copy(m.seed[:, 0], cos))
            nc.vector.tensor_copy(m.seed[:, 1], sin).then_inc(s.seed_ready, 1)
            g = [s5s[:, n] for n in range(11, 26)]
            step.mark(tt(g[0], m.mag[:, :], cos, ALU.mult))
            step.mark(tt(g[1], m.mag[:, :], sin, ALU.mult))
            step.mark(tt(g[2], re, re, ALU.mult))
            step.step(tt(g[3], im, im, ALU.mult))
            step.mark(ts(g[0], g[0], -1.0, None, ALU.add))
            step.step(tt(g[2], g[2], g[3], ALU.add))
            step.mark(nc.vector.reciprocal(g[4], g[2]))
            step.mark(tt(g[5], g[0], re, ALU.mult))
            step.mark(tt(g[6], g[1], im, ALU.mult))
            step.mark(tt(g[7], g[1], re, ALU.mult))
            step.step(tt(g[8], g[0], im, ALU.mult))
            step.mark(tt(g[5], g[5], g[6], ALU.add))
            step.step(tt(g[7], g[7], g[8], ALU.subtract))
            step.mark(tt(g[5], g[5], g[4], ALU.mult))
            step.step(tt(g[7], g[7], g[4], ALU.mult))
            cr = over(g[5].unsqueeze(2), (P, 8, 16))
            ci = over(g[7].unsqueeze(2), (P, 8, 16))
            step.mark(tt(bbt[:, 0], bmat[:, 0], cr, ALU.mult))
            step.mark(tt(bbt[:, 1], bmat[:, 1], ci, ALU.mult))
            step.mark(tt(bbt[:, 2], bmat[:, 1], cr, ALU.mult))
            step.step(tt(bbt[:, 3], bmat[:, 0], ci, ALU.mult))
            step.mark(tt(bb[:, 0], bbt[:, 0], bbt[:, 1], ALU.subtract))
            step.step(tt(bb[:, 1], bbt[:, 2], bbt[:, 3], ALU.add))
            for part in range(2):
                for b in range(8):
                    for hh in range(2):
                        rows_ = slice(64 * hh, 64 * hh + 64)
                        at = b * P + 32 * (b % 4) + 16 * hh
                        step.mark(nc.vector.tensor_copy(bbd[rows_, part, at:at + 16], bb[rows_, part, b]))
                        step.mark(ts(m.s5_out[rows_, part, at:at + 16], cmat[rows_, part, b], (1.0, -1.0)[part], None, ALU.mult))
            step.settle()
            v.sem_inc(s.bb_placed, 1)
            norm_copy(m, v, banks, 1)
            for n in range(5):
                for r in (1, 3):
                    bank = banks.take()
                    dst = m.att_qk[:, r, n * PANEL:(n + 1) * PANEL] if n < 4 else m.att_v[:, r, :]
                    nc.vector.tensor_copy(dst, bank[:, 0:PANEL]).then_inc(s.vec_read, 1)
            bank = banks.take()
            nc.vector.tensor_copy(m.ba[:, :, :], bank[:, 0:32].rearrange("p (c k) -> p c k", c=NT)).then_inc(s.vec_read, 1)
            banks.settle()
            step.mark(nc.vector.tensor_copy(qk_gain[:, 12 * HEAD:].rearrange("p (g c) -> p g c", g=4),
                                            over(qk_gain[:, HEAD:2 * HEAD].unsqueeze(1), (P, 4, HEAD))))
            step.step(ts(qk_gain[:, 0:HEAD], qk_gain[:, 0:HEAD], HEAD ** -0.5, None, ALU.mult))
            step.step(nc.vector.tensor_copy(qk_gain[:, HEAD:12 * HEAD].rearrange("p (g c) -> p g c", g=11),
                                            over(qk_gain[:, 0:HEAD].unsqueeze(1), (P, 11, HEAD))))
            v.sem_inc(s.qk_sq, 1)
            v.wait_ge(s.qk_ss, 1)
            nc.vector.tensor_reduce(qss, m.work_a[:, :].rearrange("p (g c) -> p g c", c=HEAD), AX_X, ALU.add).then_inc(s.qk_sq, 1)
            v.wait_ge(s.qk_rms, 1)
            step.step(nc.vector.reciprocal(qrstd, qrms))
            qk = m.att_qk[:, :, :].rearrange("p r (g c) -> p (r g) c", c=HEAD)
            step.step(tt(qk, qk, over(qrstd.unsqueeze(2), (P, 64, HEAD)), ALU.mult))
            tt(m.att_qk[:, :, :], m.att_qk[:, :, :], over(qk_gain[:, :].unsqueeze(1), (P, 4, 1024)), ALU.mult).then_inc(s.qk_ready, 1)
            for b in range(1, 8, 2):
                bank = banks.take()
                nc.vector.tensor_copy(m.qkT[:, b, :], bank[:, :]).then_inc(s.vec_read, 1)

        @block.gpsimd
        def _(pool):
            step = Link(pool, s.pool_step)
            tt = nc.gpsimd.tensor_tensor
            step.mark(nc.gpsimd.memset(m.rot[:, 0, :, 0:1], 1.0))
            step.mark(nc.gpsimd.memset(m.rot[:, 1, :, 0:1], 0.0))
            pool.wait_ge(s.seed_ready, 1)
            step.settle()
            for q in range(2):
                bl = slice(4 * q, 4 * q + 4)
                w = [m.seed[:, 0, bl], m.seed[:, 1, bl]]
                n = 1
                while n < T:
                    wr = over(w[0].unsqueeze(2), (P, 4, n))
                    wi = over(w[1].unsqueeze(2), (P, 4, n))
                    re, im = m.rot[:, 0, bl, 0:n], m.rot[:, 1, bl, 0:n]
                    t = [pool_t[:, k, 0:4 * n].rearrange("p (b n) -> p b n", b=4) for k in range(2)]
                    step.mark(tt(t[0], re, wr, ALU.mult))
                    step.step(tt(t[1], im, wi, ALU.mult))
                    step.step(tt(m.rot[:, 0, bl, n:2 * n], t[0], t[1], ALU.subtract))
                    step.mark(tt(t[0], re, wi, ALU.mult))
                    step.step(tt(t[1], im, wr, ALU.mult))
                    step.step(tt(m.rot[:, 1, bl, n:2 * n], t[0], t[1], ALU.add))
                    n *= 2
                    if n < T:
                        e = [pool_w[:, k] for k in range(6)]
                        new = (2, 3) if n.bit_length() % 2 == 0 else (4, 5)
                        step.mark(tt(e[0], w[0], w[0], ALU.mult))
                        step.step(tt(e[1], w[1], w[1], ALU.mult))
                        step.mark(tt(e[new[0]], e[0], e[1], ALU.subtract))
                        step.step(tt(e[new[1]], w[0], w[1], ALU.mult))
                        step.step(tt(e[new[1]], e[new[1]], e[new[1]], ALU.add))
                        w = [e[new[0]], e[new[1]]]
    clear(nc, s)



def phase_attend(m, layer):
    nc = m.nc
    with ExitStack() as ctx:
        s = semaphores(nc, ctx, COMMON + " soft_ready exp_done folded o_filled o_ready ur_ready scanned x_ready y_done y_read gelu_done")
        sb = lambda n, shape, dt=F32: ctx.enter_context(nc.sbuf_tensor(n, shape, dt))
        small = sb("small2", [P, 64])
        bu = sb("s5_bu", [P, 2, T])
        ptmp = sb("s5_ptmp", [P, 2, T])
        ur = sb("s5_ur", [P, 2, 2, T])
        z = sb("s5_z", [P, 2, T])
        vtmp = sb("s5_vtmp", [P, 2, T])
        xs = sb("s5_x", [P, 2, T])
        wb = m.att_qk[:, :, :].rearrange("p r c -> p (r c)")
        e = [wb[:, k * 768:(k + 1) * 768] for k in range(2)]
        pt = [wb[:, 1536 + k * 512:2048 + k * 512] for k in range(2)]
        osb = [wb[:, 2560 + k * 256:2816 + k * 256] for k in range(2)]
        nmax, den, rden = small[:, 0:16], small[:, 16:32], small[:, 32:48]
        obanks, ybank = (m.banks[7], m.banks[2]), m.banks[6]
        N = 4 * SLOTS
        pt_count, bu_count, at_count = {}, {}, {}

        def a_order(it):
            out = []
            if it >= 1:
                out.append(("pt", it - 1))
                if (it - 1) % 4 == 1 and it - 1 >= 4:
                    out.append(("at", (it - 1) // 4 - 1))
            if it % 2 == 0 and it // 2 < S5_BLOCKS:
                out.append(("bu", it // 2))
            return out

        block = ctx.enter_context(nc.Block())

        @block.tensor
        def _(pe):
            to_act = Banks(pe, m.banks[0:2], s.act_filled, s.act_read)
            to_vec = Banks(pe, m.banks[3:6], s.vec_filled, s.vec_read)

            def scores(it):
                r, sl = it // 4, it % 4
                rows = slice(64 * (sl % 2), 64 * (sl % 2) + 64)
                k = m.qkT[rows, (GROUPS * SLOTS + sl) // 2]
                q = [m.qkT[rows, (4 * g + sl) // 2, r * P:(r + 1) * P] for g in range(GROUPS)]
                bank = to_vec.open()
                nc.tensor.matmul(bank[:, :], q[0], k, start=True, stop=True).then_inc(s.vec_filled, 1)
                bank = to_vec.open()
                nc.tensor.matmul(bank[:, 0:P], q[1], k[:, r * P:(r + 1) * P], start=True, stop=True)
                nc.tensor.matmul(bank[:, P:2 * P], q[2], k[:, r * P:(r + 1) * P], start=True, stop=True).then_inc(s.vec_filled, 1)

            def values(it):
                r, sl = it // 4, it % 4
                pe.wait_ge(s.folded, it + 1)
                bank = to_act.open()
                for r2 in range(4):
                    ins = nc.tensor.transpose(bank[:, r2 * P:(r2 + 1) * P], e[it % 2][:, r2 * P:(r2 + 1) * P], m.c("ident"))
                ins.then_inc(s.act_filled, 1)
                pt_count[it] = to_act.n
                if sl == 0 and r >= 2:
                    pe.wait_ge(s.o_ready, r - 1)
                to_act.all_read()
                at = HEAD * sl
                for r2 in range(4):
                    ins = nc.tensor.matmul(obanks[r % 2][:, at:at + HEAD], pt[it % 2][:, r2 * P:(r2 + 1) * P],
                                           m.att_v[:, r2, sl * HEAD:(sl + 1) * HEAD], start=(r2 == 0), stop=(r2 == 3))
                ins.then_inc(s.o_filled, 1)

            def out_transpose(r):
                pe.wait_ge(s.o_ready, r + 1)
                bank = to_act.open()
                for k in range(2):
                    ins = nc.tensor.transpose(bank[:, k * P:(k + 1) * P], osb[r % 2][:, k * P:(k + 1) * P], m.c("ident"))
                ins.then_inc(s.act_filled, 1)
                at_count[r] = to_act.n

            def s5_input(b):
                for part in range(2):
                    bank = to_act.open()
                    nc.tensor.matmul(bank[:, :], m.s5_in[:, part, b * P:(b + 1) * P], m.uT[:, b // 4, :],
                                     start=True, stop=True).then_inc(s.act_filled, 1)
                bu_count[b] = to_act.n

            def s5_output(b):
                pe.wait_ge(s.x_ready, b + 1)
                if b == 4:
                    pe.wait_ge(s.y_read, 1)
                for part in range(2):
                    ins = nc.tensor.matmul(ybank[:, :], m.s5_out[:, part, b * P:(b + 1) * P], xs[:, part, :],
                                           start=(b % 4 == 0 and part == 0), stop=(b % 4 == 3 and part == 1))
                ins.then_inc(s.y_done, 1)

            for it in range(N + 6):
                if it < N:
                    scores(it)
                for what, n in a_order(it) if it <= N else ():
                    {"pt": values, "at": out_transpose, "bu": s5_input}[what](n)
                if it % 2 == 1 and 0 <= (it - 3) // 2 < S5_BLOCKS:
                    s5_output((it - 3) // 2)
            out_transpose(3)

        @block.scalar
        def _(act):
            banks = Reader(act, m.banks[0:2], s.act_filled, s.act_read)

            def copy(what, n):
                bank = banks.take()
                if what == "pt":
                    if n >= 2:
                        act.wait_ge(s.o_filled, n - 1)
                    nc.scalar.activation(pt[n % 2], bank[:, :], ACT.Copy).then_inc(s.act_read, 1)
                elif what == "at":
                    nc.scalar.activation(m.aT[:, :, n::4], bank[:, 0:256].rearrange("p (k q) -> p k q", k=2),
                                         ACT.Copy).then_inc(s.act_read, 1)
                else:
                    if n >= 1:
                        act.wait_ge(s.ur_ready, n)
                    nc.scalar.activation(bu[:, 0, :], bank[:, :], ACT.Copy).then_inc(s.act_read, 1)
                    bank = banks.take()
                    nc.scalar.activation(bu[:, 1, :], bank[:, :], ACT.Copy).then_inc(s.act_read, 1)

            for it in range(N + 1):
                if it < N:
                    act.wait_ge(s.soft_ready, it + 1)
                    nc.scalar.activation(e[it % 2], e[it % 2], ACT.Exp, bias=nmax[:, it:it + 1],
                                         accum_out=den[:, it:it + 1]).then_inc(s.exp_done, 1)
                for what, n in a_order(it):
                    copy(what, n)
            copy("at", 3)
            for yt in range(2):
                act.wait_ge(s.y_read, yt + 1)
                nc.scalar.activation(m.sT[:, yt, :], m.sT[:, yt, :], ACT.Gelu_apprx_tanh).then_inc(s.gelu_done, 1)

        @block.vector
        def _(v):
            step = Link(v, s.vec_step)
            banks = Reader(v, m.banks[3:6], s.vec_filled, s.vec_read)
            tt, stt = nc.vector.tensor_tensor, nc.vector.scalar_tensor_tensor

            def soft(it):
                r, sl = it // 4, it % 4
                if it >= 2:
                    v.wait_ge(s.act_filled, pt_count[it - 2])
                bank = banks.take()
                stt(out=e[it % 2][:, 0:512], in0=m.c("dist_g0")[:, (3 - r) * P:(7 - r) * P], scalar=-float(SLOPES[sl]),
                    in1=bank[:, :], op0=ALU.mult, op1=ALU.add).then_inc(s.vec_read, 1)
                bank = banks.take()
                step.mark(stt(out=e[it % 2][:, 512:640], in0=m.c("dist_g1"), scalar=-float(SLOPES[SLOTS + sl]),
                              in1=bank[:, 0:P], op0=ALU.mult, op1=ALU.add))
                stt(out=e[it % 2][:, 640:768], in0=m.c("dist_g2"), scalar=-float(SLOPES[2 * SLOTS + sl]),
                    in1=bank[:, P:2 * P], op0=ALU.mult, op1=ALU.add).then_inc(s.vec_read, 1)
                banks.settle()
                step.settle()
                nc.vector.tensor_reduce(nmax[:, it:it + 1], e[it % 2], AX_X, ALU.max, negate=True).then_inc(s.soft_ready, 1)

            def fold(it):
                r = it // 4
                v.wait_ge(s.exp_done, it + 1)
                own = e[it % 2][:, r * P:(r + 1) * P]
                step.step(tt(own, own, e[it % 2][:, 512:640], ALU.add))
                tt(own, own, e[it % 2][:, 640:768], ALU.add).then_inc(s.folded, 1)

            def normalise(r):
                v.wait_ge(s.o_filled, 4 * r + 4)
                if r >= 2:
                    v.wait_ge(s.act_filled, at_count[r - 2])
                step.step(nc.vector.reciprocal(rden[:, 4 * r:4 * r + 4], den[:, 4 * r:4 * r + 4]))
                tt(osb[r % 2].rearrange("p (s c) -> p s c", s=4),
                   obanks[r % 2][:, 0:256].rearrange("p (s c) -> p s c", s=4),
                   over(rden[:, 4 * r:4 * r + 4].unsqueeze(2), (P, 4, HEAD)), ALU.mult).then_inc(s.o_ready, 1)

            def recur(b):
                v.wait_ge(s.ur_ready, b + 1)
                if b >= 1:
                    step.settle()
                for part in range(2):
                    nc.vector.tensor_tensor_scan(z[:, part, :], over(m.mag[:, b:b + 1], (P, T)), ur[:, b % 2, part, :],
                                                 0.0, ALU.mult, ALU.add).then_inc(s.scanned, 1)
                v.wait_ge(s.scanned, 2 * b + 2)
                cos, sin = m.rot[:, 0, b, :], m.rot[:, 1, b, :]
                if b >= 1:
                    v.wait_ge(s.y_done, b)
                    v.wait_ge(s.x_ready, b)
                step.mark(tt(vtmp[:, 0], z[:, 0], cos, ALU.mult))
                step.step(tt(vtmp[:, 1], z[:, 1], sin, ALU.mult))
                step.step(tt(xs[:, 0], vtmp[:, 0], vtmp[:, 1], ALU.subtract))
                step.mark(tt(vtmp[:, 0], z[:, 0], sin, ALU.mult))
                step.step(tt(vtmp[:, 1], z[:, 1], cos, ALU.mult))
                tt(xs[:, 1], vtmp[:, 0], vtmp[:, 1], ALU.add).then_inc(s.x_ready, 1)

            def skip(yt):
                v.wait_ge(s.y_done, 4 * yt + 4)
                stt(out=m.sT[:, yt, :], in0=m.uT[:, yt, :], scalar=m.s5_d[:, yt:yt + 1], in1=ybank[:, :],
                    op0=ALU.mult, op1=ALU.add).then_inc(s.y_read, 1)

            for it in range(N + 4):
                if it < N:
                    soft(it)
                if 1 <= it <= N:
                    fold(it - 1)
                if it >= 2 and (it - 2) % 4 == 3 and (it - 2) // 4 < 4:
                    normalise((it - 2) // 4)
                if it in (11, 19):
                    skip((it - 11) // 8)
                if it % 2 == 1 and it // 2 < S5_BLOCKS:
                    recur(it // 2)

        @block.gpsimd
        def _(pool):
            step = Link(pool, s.pool_step)
            tt = nc.gpsimd.tensor_tensor
            for b in range(S5_BLOCKS):
                cos, sin = m.rot[:, 0, b, :], m.rot[:, 1, b, :]
                pool.wait_ge(s.act_read, bu_count[b])
                if b >= 2:
                    pool.wait_ge(s.scanned, 2 * b - 2)
                if b >= 1:
                    pool.wait_ge(s.ur_ready, b)
                step.mark(tt(ptmp[:, 0], bu[:, 0], cos, ALU.mult))
                step.step(tt(ptmp[:, 1], bu[:, 1], sin, ALU.mult))
                step.step(tt(ur[:, b % 2, 0], ptmp[:, 0], ptmp[:, 1], ALU.add))
                step.mark(tt(ptmp[:, 0], bu[:, 1], cos, ALU.mult))
                step.step(tt(ptmp[:, 1], bu[:, 0], sin, ALU.mult))
                tt(ur[:, b % 2, 1], ptmp[:, 0], ptmp[:, 1], ALU.subtract).then_inc(s.ur_ready, 1)
    clear(nc, s)



JOINS = (2, 4, 8, 16, 32, 64)
CONVOLVED_AT = (0, 2, 5, 7)
VALUES_AT = 3


def phase_deltanet(m, layer):
    nc, io = m.nc, m.io
    with ExitStack() as ctx:
        s = semaphores(nc, ctx, COMMON + " conv_done silu_done sq_ready normed gate_a gate_v tri_ready expo_ready "
                       "decay_ready l_ready x_ready ct_ready vn_ready state_ready fill_filled fill_read")
        sb = lambda n, shape, dt=F32: ctx.enter_context(nc.sbuf_tensor(n, shape, dt))
        raw = sb("dn_raw", [P, 3 * DN, T + 3])
        cv = sb("dn_conv", [P, 2, T])
        sq = sb("dn_sq", [P, 2, T])
        rs = sb("dn_root", [P, 2, T])
        small = sb("small3", [P, 240])
        big = lambda n: sb(n, [P, NT, T])
        lm, at, er, xt, lt, kbg, kdec, vb = (big(n) for n in ("dn_l", "dn_at", "dn_er", "dn_xt", "dn_lt", "dn_kbg", "dn_kdec", "dn_vb"))
        ct = sb("dn_ct", [P, 2, T])
        yb = sb("dn_y", [P, 2, T])
        vn = sb("dn_vn", [P, T])
        state = sb("dn_state", [P, 2, T])
        x = lm
        heads = lambda a: a.rearrange("p (h n) -> p h n", h=DN)
        g16 = [small[:, 16 * k:16 * k + 16] for k in range(15)]
        beta, xg, na, lnp, g, gc, ngc, t3, ekd, eg, bg, gl = g16[0:12]
        ea = g16[12][:, 0:4]
        ch = lambda a: a.rearrange("p (c h) -> p c h", c=NT)
        panels = Panels(m, s, input_panels(io, layer, "deltanet"), early=RING)
        qt = lambda h, c: raw[:, h, 3 + c * P:3 + (c + 1) * P]
        kt = lambda h, c: raw[:, DN + h, 3 + c * P:3 + (c + 1) * P]
        vt = lambda h, c: raw[:, 2 * DN + h, 3 + c * P:3 + (c + 1) * P]
        hs = lambda h: slice(h * P, (h + 1) * P)
        raw_count, gc_count, sum_count, lt_count, vtok_count, y_count, z_count, out_count = ({} for _ in range(8))
        STEPS = len(JOINS) * NT
        BEFORE, BESIDE, IN_STEP = KD, 3, 2
        fill_end = [-(-((f + 1) * KD - BEFORE - BESIDE * NT) // IN_STEP) - 1 for f in range(2 * DN)]
        assert fill_end[2 * DN - 1] < STEPS and fill_end[DN - 1] < 2 * NT

        block = ctx.enter_context(nc.Block())

        @block.tensor
        def _(pe):
            to_act = Banks(pe, m.banks[0:3], s.act_filled, s.act_read)
            to_vec = Banks(pe, m.banks[3:6], s.vec_filled, s.vec_read)
            mm = nc.tensor.matmul

            def projection(n, mt, banks, w):
                bank = banks.open()
                for k in range(KD):
                    ins = mm(bank[:, :], w[:, k, mt * P:(mt + 1) * P], m.hT[:, k, :], start=(k == 0), stop=(k == KD - 1))
                ins.then_inc(banks.filled, 1)

            def sums(t, ready):
                pe.wait_ge(*ready)
                bank = to_act.open()
                mm(bank[:, :], m.c("ones"), sq[:, t % 2, :], start=True, stop=True).then_inc(s.act_filled, 1)
                return to_act.n

            def filling():
                for f in range(2 * DN):
                    n = 4 + f // 2
                    if f >= 2:
                        pe.wait_ge(s.fill_read, f - 1)
                    w = panel_view(panels.landed(pe, n), KD)
                    for k in range(KD):
                        ins = mm(m.banks[6 + f % 2][:, :], w[:, k, f % 2 * P:(f % 2 + 1) * P], m.hT[:, k, :], start=(k == 0), stop=(k == KD - 1))
                        if k == KD - 1:
                            ins.then_inc(s.fill_filled, 1)
                            if f % 2:
                                panels.released.append((s.fill_filled, f + 1))
                        yield

            pieces = filling()

            def fill(count):
                for _ in range(count):
                    next(pieces, None)

            for n in range(4):
                w = panel_view(panels.landed(pe, n), KD)
                projection(n, 0, to_act, w)
                raw_count[2 * n] = to_act.n
                if n == 0:
                    pe.wait_ge(s.gate_v, 2)
                    bank = to_act.open()
                    mm(bank[:, 0:16], m.c("triu"), g, start=True, stop=True).then_inc(s.act_filled, 1)
                    gc_count[0] = to_act.n
                else:
                    for t in (2 * n - 2, 2 * n - 1):
                        sum_count[t] = sums(t, (s.sq_ready, t + 1))
                projection(n, 1, to_vec, w)
                panels.released.append((s.vec_filled, to_vec.n))
                pe.wait_ge(s.tri_ready, n + 1)
                bank = to_vec.open()
                mm(bank[:, :], m.c("ones"), lt[:, n, :], start=True, stop=True).then_inc(s.vec_filled, 1)
            fill(BEFORE)
            for t in (6, 7):
                sum_count[t] = sums(t, (s.sq_ready, t + 1))

            def transposed_l(c):
                pe.wait_ge(s.l_ready, c + 1)
                bank = to_act.open()
                for h in range(DN):
                    ins = nc.tensor.transpose(bank[:, hs(h)], lm[:, c, hs(h)], m.c("ident"))
                ins.then_inc(s.act_filled, 1)
                lt_count[c] = to_act.n

            for c in range(NT):
                pe.wait_ge(s.normed, 8)
                for a, b in ((kt, kt), (kt, qt)):
                    bank = to_vec.open()
                    for h in range(DN):
                        ins = mm(bank[:, hs(h)], a(h, c), b(h, c), start=True, stop=True)
                    ins.then_inc(s.vec_filled, 1)
                bank = to_vec.open()
                for h in range(DN):
                    ins = nc.tensor.transpose(bank[:, hs(h)], kt(h, c), m.c("ident"))
                ins.then_inc(s.vec_filled, 1)
                fill(BESIDE)
                if c:
                    transposed_l(c - 1)
            transposed_l(NT - 1)

            def join_tail(i):
                c = i % NT
                pe.wait_ge(s.act_read, y_count[i])
                if i < STEPS - NT:
                    bank = to_vec.open()
                    for h in range(DN):
                        ins = mm(bank[:, hs(h)], xt[:, c, hs(h)], yb[:, i % 2, hs(h)], start=True, stop=True)
                    ins.then_inc(s.vec_filled, 1)
                bank = to_vec.open()
                for h in range(DN):
                    ins = mm(bank[:, hs(h)], yb[:, i % 2, hs(h)], xt[:, c, hs(h)], start=True, stop=True)
                ins.then_inc(s.vec_filled, 1)
                z_count[i] = to_vec.n

            for i in range(STEPS):
                c = i % NT
                pe.wait_ge(s.ct_ready, i + 1)
                pe.wait_ge(s.x_ready, i + 1)
                bank = to_act.open()
                for h in range(DN):
                    ins = mm(bank[:, hs(h)], ct[:, i % 2, hs(h)], x[:, c, hs(h)], start=True, stop=True)
                ins.then_inc(s.act_filled, 1)
                y_count[i] = to_act.n
                fill(IN_STEP)
                if i:
                    join_tail(i - 1)
                if i // NT == VALUES_AT:
                    pe.wait_ge(s.silu_done, 3 * DN)
                    bank = to_act.open()
                    for h in range(DN):
                        ins = nc.tensor.transpose(bank[:, hs(h)], vt(h, c), m.c("ident"))
                    ins.then_inc(s.act_filled, 1)
            join_tail(STEPS - 1)
            for c in range(NT):
                pe.wait_ge(s.x_ready, STEPS + c + 1)
                bank = to_act.open()
                for h in range(DN):
                    ins = mm(bank[:, hs(h)], xt[:, c, hs(h)], vb[:, c, hs(h)], start=True, stop=True)
                ins.then_inc(s.act_filled, 1)
                bank = to_act.open()
                for h in range(DN):
                    ins = mm(bank[:, hs(h)], kbg[:, c, hs(h)], xt[:, c, hs(h)], start=True, stop=True)
                ins.then_inc(s.act_filled, 1)
            to_act.all_read()
            for c in range(NT):
                if c:
                    pe.wait_ge(s.state_ready, c)
                    bank = to_vec.open()
                    for h in range(DN):
                        ins = mm(bank[:, hs(h)], lt[:, c, hs(h)], state[:, (c - 1) % 2, hs(h)], start=True, stop=True)
                    ins.then_inc(s.vec_filled, 1)
                    pe.wait_ge(s.vn_ready, c)
                src = lambda h: vn[:, hs(h)] if c else lm[:, 0, hs(h)]
                if c < NT - 1:
                    bank = to_vec.open()
                    for h in range(DN):
                        ins = mm(bank[:, hs(h)], kdec[:, c, hs(h)], src(h), start=True, stop=True)
                    ins.then_inc(s.vec_filled, 1)
                bank = to_act.open()
                for h in range(DN):
                    ins = mm(bank[:, hs(h)], src(h), at[:, c, hs(h)], start=True, stop=(c == 0))
                    if c:
                        ins = mm(bank[:, hs(h)], state[:, (c - 1) % 2, hs(h)], er[:, c, hs(h)], start=False, stop=True)
                ins.then_inc(s.act_filled, 1)
                out_count[c] = to_act.n
                if c:
                    sum_count[8 + c - 1] = sums(c - 1, (s.act_read, out_count[c - 1]))
            sum_count[8 + NT - 1] = sums(NT - 1, (s.act_read, out_count[NT - 1]))

        @block.sync
        def _(sp):
            panels.stream(sp, input_panels(io, layer, "combine"))

        @block.scalar
        def _(act):
            step = Link(act, s.act_step)
            banks = Reader(act, m.banks[0:3], s.act_filled, s.act_read)
            f = nc.scalar.activation
            step.mark(f(ch(beta), m.ba[:, :, 0:DN], ACT.Sigmoid))
            act.wait_ge(s.gate_v, 1)
            step.mark(f(ea, m.a_log[:, :], ACT.Exp))
            step.step(f(lnp, na, ACT.Exp))
            f(lnp, lnp, ACT.Ln, bias=1.0).then_inc(s.gate_a, 1)

            def root(u, scale=1.0):
                if u >= 2:
                    act.wait_ge(s.normed, u - 1)
                bank = banks.take()
                f(rs[:, u % 2, :], bank[:, :], ACT.Sqrt, bias=m.c("eps"), scale=scale).then_inc(s.act_read, 1)

            def silu(t):
                act.wait_ge(s.conv_done, t + 1)
                f(raw[:, t, 3:], cv[:, t % 2, :], ACT.Silu).then_inc(s.silu_done, 1)

            def decays(c):
                act.wait_ge(s.expo_ready, c + 1)
                for h in range(DN):
                    n = 4 * c + h
                    step.mark(f(lm[:, c, hs(h)], lm[:, c, hs(h)], ACT.Exp, bias=gc[:, n:n + 1]))
                    step.mark(f(at[:, c, hs(h)], at[:, c, hs(h)], ACT.Exp, bias=ngc[:, n:n + 1]))
                step.mark(f(ekd[:, 4 * c:4 * c + 4], t3[:, 4 * c:4 * c + 4], ACT.Exp))
                f(er[:, c, :], er[:, c, :], ACT.Exp).then_inc(s.decay_ready, 1)

            def filled(k):
                act.wait_ge(s.fill_filled, k + 1)
                dst, kind = (raw[:, 2 * DN + k, 3:], ACT.Copy) if k < DN else (raw[:, k - DN, 3:], ACT.Silu)
                f(dst, m.banks[6 + k % 2][:, :], kind).then_inc(s.fill_read, 1)

            for n in range(4):
                bank = banks.take()
                f(raw[:, 2 * n, 3:], bank[:, :], ACT.Copy).then_inc(s.act_read, 1)
                if n == 0:
                    bank = banks.take()
                    step.mark(f(gc, bank[:, 0:16], ACT.Copy))
                    step.mark(f(ngc, bank[:, 0:16], ACT.Copy, scale=-1.0))
                    f(eg, bank[:, 0:16], ACT.Exp).then_inc(s.act_read, 1)
                    banks.settle()
                    step.settle()
                    act.sem_inc(s.gate_a, 1)
                else:
                    root(2 * n - 2)
                    root(2 * n - 1)
                for t in (2 * n, 2 * n + 1):
                    silu(t)
                    act.wait_ge(s.silu_done, t + 1)
                    f(sq[:, t % 2, :], raw[:, t, 3:], ACT.Square).then_inc(s.sq_ready, 1)
                decays(n)
            filled(0)
            root(6)
            root(7)
            step.settle()
            done = 1
            for c in range(NT):
                if c:
                    bank = banks.take()
                    f(lt[:, c - 1, :], bank[:, :], ACT.Copy).then_inc(s.act_read, 1)
                if BEFORE + BESIDE * (c + 1) >= (done + 1) * KD:
                    filled(done)
                    done += 1
            bank = banks.take()
            f(lt[:, NT - 1, :], bank[:, :], ACT.Copy).then_inc(s.act_read, 1)
            for i in range(STEPS):
                lv, c = i // NT, i % NT
                bank = banks.take()
                if i >= 2:
                    act.wait_ge(s.vec_filled, z_count[i - 2])
                f(yb[:, i % 2, :], bank[:, :], ACT.Copy).then_inc(s.act_read, 1)
                if done < 2 * DN and i >= fill_end[done]:
                    filled(done)
                    done += 1
                if i - 2 in CONVOLVED_AT:
                    silu(2 * DN + CONVOLVED_AT.index(i - 2))
                if lv == VALUES_AT:
                    bank = banks.take()
                    for h in range(DN):
                        n = 4 * c + h
                        ins = f(vb[:, c, hs(h)], bank[:, hs(h)], ACT.Copy, scale=beta[:, n:n + 1])
                        if h < DN - 1:
                            step.mark(ins)
                    ins.then_inc(s.act_read, 1)
            step.settle()
            for c in range(NT):
                bank = banks.take()
                f(lm[:, c, :], bank[:, :], ACT.Copy).then_inc(s.act_read, 1)
                bank = banks.take()
                f(lt[:, c, :], bank[:, :], ACT.Copy).then_inc(s.act_read, 1)
            for c in range(NT):
                bank = banks.take()
                step.mark(f(m.bT[:, :, c * P:(c + 1) * P], heads(bank[:, :]), ACT.Copy))
                step.settle()
                f(sq[:, c % 2, :], bank[:, :], ACT.Square).then_inc(s.act_read, 1)
                if c:
                    root(8 + c - 1, 1.0 / P)
            root(8 + NT - 1, 1.0 / P)

        @block.vector
        def _(v):
            step = Link(v, s.vec_step)
            banks = Reader(v, m.banks[3:6], s.vec_filled, s.vec_read)
            tt, ts, stt = nc.vector.tensor_tensor, nc.vector.tensor_scalar, nc.vector.scalar_tensor_tensor
            step.mark(nc.vector.memset(raw[:, :, 0:3], 0.0))
            step.step(tt(ch(xg), m.ba[:, :, DN:2 * DN], over(m.dt_bias[:, :].unsqueeze(1), (P, NT, DN)), ALU.add))
            stt(out=na, in0=xg, scalar=-1.0, in1=xg, op0=ALU.mult, op1=ALU.min).then_inc(s.gate_v, 1)
            v.wait_ge(s.gate_a, 1)
            step.step(stt(out=xg, in0=xg, scalar=0.0, in1=lnp, op0=ALU.max, op1=ALU.add))
            stt(out=ch(g), in0=ch(xg), scalar=-1.0, in1=over(ea.unsqueeze(1), (P, NT, DN)), op0=ALU.mult, op1=ALU.mult).then_inc(s.gate_v, 1)
            v.wait_ge(s.gate_v, 2)
            for c in range(NT):
                tt(heads(lt[:, c, :]), over(m.c("triu").unsqueeze(1), (P, DN, P)),
                   over(g[:, 4 * c:4 * c + 4].unsqueeze(2), (P, DN, P)), ALU.mult).then_inc(s.tri_ready, 1)

            def conv(t):
                if t >= 2:
                    v.wait_ge(s.silu_done, t - 1)
                o = cv[:, t % 2, :]
                step.step(ts(o, raw[:, t, 0:T], m.conv_w[:, t, 0:1], None, ALU.mult))
                for k in (1, 2, 3):
                    ins = stt(out=o, in0=raw[:, t, k:k + T], scalar=m.conv_w[:, t, k:k + 1], in1=o, op0=ALU.mult, op1=ALU.add)
                    if k < 3:
                        step.step(ins)
                ins.then_inc(s.conv_done, 1)

            def exponents(c):
                bank = banks.take()
                step.mark(tt(heads(lm[:, c, :]), over(m.c("strict").unsqueeze(1), (P, DN, P)), heads(bank[:, :]), ALU.subtract))
                step.mark(tt(heads(at[:, c, :]), over(m.c("incl_t").unsqueeze(1), (P, DN, P)), heads(bank[:, :]), ALU.add))
                step.mark(tt(t3[:, 4 * c:4 * c + 4].unsqueeze(2), heads(bank[:, :])[:, :, P - 1:P], gc[:, 4 * c:4 * c + 4].unsqueeze(2), ALU.subtract))
                step.step(nc.vector.tensor_copy(er[:, c, :], bank[:, :]))
                v.sem_inc(s.vec_read, 1)
                v.sem_inc(s.expo_ready, 1)

            def unit_length(t):
                v.wait_ge(s.act_read, sum_count[t])
                step.step(nc.vector.reciprocal(rs[:, t % 2, :], rs[:, t % 2, :]))
                stt(out=raw[:, t, 3:], in0=raw[:, t, 3:], scalar=float(P) ** -0.5 if t < DN else 1.0, in1=rs[:, t % 2, :],
                    op0=ALU.mult, op1=ALU.mult).then_inc(s.normed, 1)

            for n in range(4):
                v.wait_ge(s.act_read, raw_count[2 * n])
                conv(2 * n)
                if n:
                    unit_length(2 * n - 2)
                    unit_length(2 * n - 1)
                bank = banks.take()
                nc.vector.tensor_copy(raw[:, 2 * n + 1, 3:], bank[:, :]).then_inc(s.vec_read, 1)
                banks.settle()
                conv(2 * n + 1)
                if n == 0:
                    v.wait_ge(s.gate_a, 2)
                    step.step(tt(bg, beta, eg, ALU.mult))
                exponents(n)
            unit_length(6)
            unit_length(7)

            def first_blocks(c):
                v.wait_ge(s.act_read, lt_count[c])
                step.mark(tt(heads(x[:, c, :]), heads(lm[:, c, :]), over(m.c("join1_low").unsqueeze(1), (P, DN, P)), ALU.mult))
                step.step(tt(heads(xt[:, c, :]), heads(lt[:, c, :]), over(m.c("join1").unsqueeze(1), (P, DN, P)), ALU.mult))
                step.mark(tt(heads(x[:, c, :]), over(m.c("ident").unsqueeze(1), (P, DN, P)), heads(x[:, c, :]), ALU.subtract))
                step.step(tt(heads(xt[:, c, :]), over(m.c("ident").unsqueeze(1), (P, DN, P)), heads(xt[:, c, :]), ALU.subtract))
                v.sem_inc(s.x_ready, 1)

            for c in range(NT):
                v.wait_ge(s.decay_ready, c + 1)
                bank = banks.take()
                for h in range(DN):
                    n = 4 * c + h
                    ins = stt(out=lm[:, c, hs(h)], in0=bank[:, hs(h)], scalar=beta[:, n:n + 1], in1=lm[:, c, hs(h)], op0=ALU.mult, op1=ALU.mult)
                    if h < DN - 1:
                        step.mark(ins)
                ins.then_inc(s.vec_read, 1)
                banks.settle()
                step.settle()
                v.sem_inc(s.l_ready, 1)
                step.step(nc.vector.tensor_copy(gl[:, 4 * c:4 * c + 4].unsqueeze(2), heads(er[:, c, :])[:, :, P - 1:P]))
                step.mark(tt(heads(er[:, c, :]), heads(er[:, c, :]), raw[:, 0:DN, 3 + c * P:3 + (c + 1) * P], ALU.mult))
                bank = banks.take()
                tt(at[:, c, :], at[:, c, :], bank[:, :], ALU.mult).then_inc(s.vec_read, 1)
                bank = banks.take()
                step.mark(tt(heads(kbg[:, c, :]), heads(bank[:, :]), over(bg[:, 4 * c:4 * c + 4].unsqueeze(2), (P, DN, P)), ALU.mult))
                tt(heads(kdec[:, c, :]), heads(bank[:, :]), over(ekd[:, 4 * c:4 * c + 4].unsqueeze(2), (P, DN, P)), ALU.mult).then_inc(s.vec_read, 1)
                if c:
                    first_blocks(c - 1)
            first_blocks(NT - 1)
            for i in range(STEPS):
                lv, c = i // NT, i % NT
                v.wait_ge(s.x_ready, i + 1)
                if lv < len(JOINS) - 1:
                    bank = banks.take()
                    tt(x[:, c, :], x[:, c, :], bank[:, :], ALU.subtract).then_inc(s.vec_read, 1)
                bank = banks.take()
                tt(xt[:, c, :], xt[:, c, :], bank[:, :], ALU.subtract).then_inc(s.vec_read, 1)
                banks.settle()
                v.sem_inc(s.x_ready, 1)
                if i in CONVOLVED_AT:
                    t = 2 * DN + CONVOLVED_AT.index(i)
                    v.wait_ge(s.fill_read, t - 2 * DN + 1)
                    conv(t)

            def gated(c):
                u = 8 + c
                v.wait_ge(s.act_read, sum_count[u])
                step.step(nc.vector.reciprocal(rs[:, u % 2, :], rs[:, u % 2, :]))
                step.step(tt(heads(rs[:, u % 2, :]), heads(rs[:, u % 2, :]), raw[:, 0:DN, 3 + c * P:3 + (c + 1) * P], ALU.mult))
                out = m.bT[:, :, c * P:(c + 1) * P]
                stt(out=out, in0=out, scalar=m.out_gain[:, 0:1], in1=heads(rs[:, u % 2, :]), op0=ALU.mult, op1=ALU.mult).then_inc(s.normed, 1)

            v.wait_ge(s.fill_read, 2 * DN)
            for c in range(NT):
                if c:
                    bank = banks.take()
                    v.wait_ge(s.vec_read, banks.n - 1)
                    tt(vn[:, :], lm[:, c, :], bank[:, :], ALU.subtract).then_inc(s.vec_read, 1)
                    banks.settle()
                    v.sem_inc(s.vn_ready, 1)
                if c < NT - 1:
                    bank = banks.take()
                    if c == 0:
                        nc.vector.tensor_copy(state[:, 0, :], bank[:, :]).then_inc(s.vec_read, 1)
                    else:
                        for h in range(DN):
                            n = 4 * c + h
                            ins = stt(out=state[:, c % 2, hs(h)], in0=state[:, (c - 1) % 2, hs(h)], scalar=gl[:, n:n + 1], in1=bank[:, hs(h)], op0=ALU.mult, op1=ALU.add)
                            if h < DN - 1:
                                step.mark(ins)
                        ins.then_inc(s.vec_read, 1)
                    banks.settle()
                    step.settle()
                    v.sem_inc(s.state_ready, 1)
                if c:
                    gated(c - 1)
            gated(NT - 1)

        @block.gpsimd
        def _(pool):
            for i in range(STEPS):
                pool.wait_ge(s.act_read, lt_count[i % NT])
                if i >= 2:
                    pool.wait_ge(s.act_filled, y_count[i - 2])
                    pool.wait_ge(s.ct_ready, i - 1)
                nc.gpsimd.tensor_tensor(heads(ct[:, i % 2, :]), heads(lt[:, i % NT, :]), over(m.c(f"join{JOINS[i // NT]}").unsqueeze(1), (P, DN, P)),
                                        ALU.mult).then_inc(s.ct_ready, 1)
    clear(nc, s)



def phase_combine(m, layer):
    nc, io = m.nc, m.io
    with ExitStack() as ctx:
        s = semaphores(nc, ctx, COMMON + " out_w sig_ready comb_ready")
        sb = lambda n, shape, dt=F32: ctx.enter_context(nc.sbuf_tensor(n, shape, dt))
        wa = sb("w_a", [P, 2, D])
        wb = sb("w_b", [P, 4, D])
        wv = sb("w_cv", [P, 2, D])
        wg = sb("w_cg", [P, 2, D])
        sig = sb("sig", [P, 4, 4, T])
        tmp = sb("comb_tmp", [P, 4, T])
        comb = sb("comb", [P, KD, T])
        rows = input_panels(io, layer, "combine")
        rows += [(weight(io.w_out, layer, 0, KD, n * PANEL, PANEL), KD, PANEL) for n in range(4)]
        panels = Panels(m, s, rows, early=RING)
        block = ctx.enter_context(nc.Block())

        @block.tensor
        def _(pe):
            to_act = Banks(pe, m.banks[0:3], s.act_filled, s.act_read)
            to_vec = Banks(pe, m.banks[3:6], s.vec_filled, s.vec_read)

            def product(banks, pairs, cols=slice(0, T)):
                bank = banks.open()
                for n, (a, b) in enumerate(pairs):
                    ins = nc.tensor.matmul(bank[:, cols], a, b, start=(n == 0), stop=(n == len(pairs) - 1))
                ins.then_inc(banks.filled, 1)

            for pair in range(KD // 2):
                for br in range(3):
                    w = panel_view(panels.landed(pe, 3 * pair + br), KD)
                    for half in range(2):
                        product(to_act, [(w[:, k, half * P:(half + 1) * P], m.hT[:, k, :]) for k in range(KD)])
                    panels.released.append((s.act_filled, to_act.n))
                if pair == 0:
                    pe.wait_ge(s.out_w, 16 * 4)
                for half in range(2):
                    mt = 2 * pair + half
                    cols = slice(mt * P, (mt + 1) * P)
                    product(to_act, [(wg[:, k, cols], m.sT[:, k, :]) for k in range(2)])
                    product(to_vec, [(wa[:, k, cols], m.aT[:, k, :]) for k in range(2)])
                    product(to_vec, [(wb[:, k, cols], m.bT[:, k, :]) for k in range(4)])
                    product(to_vec, [(wv[:, k, cols], m.sT[:, k, :]) for k in range(2)])
            pe.wait_ge(s.comb_ready, KD)
            for n in range(4):
                w = panel_view(panels.landed(pe, 3 * KD // 2 + n), KD)
                for t in range(NT):
                    product(to_vec, [(comb[:, k, t * P:(t + 1) * P], w[:, k, :]) for k in range(KD)], slice(0, PANEL))
                panels.released.append((s.vec_filled, to_vec.n))

        @block.sync
        def _(sp):
            panels.stream(sp)

        @block.scalar
        def _(act):
            for dst, src, kt in ((wg, io.w_c_gate, 2), (wa, io.w_a_out, 2), (wb, io.w_b_out, 4), (wv, io.w_c_val, 2)):
                act.dma_start(dst[:, :, :], weight(src, layer, 0, kt, 0, D)).then_inc(s.out_w, 16)
            banks = Reader(act, m.banks[0:3], s.act_filled, s.act_read)
            for pair in range(KD // 2):
                if pair >= 2:
                    act.wait_ge(s.comb_ready, 2 * pair - 2)
                for br, half in [(br, half) for br in range(3) for half in range(2)] + [(3, 0), (3, 1)]:
                    bank = banks.take()
                    nc.scalar.activation(sig[:, br, (2 * pair + half) % 4, :], bank[:, :], ACT.Sigmoid).then_inc(s.act_read, 1)

        @block.vector
        def _(v):
            step = Link(v, s.vec_step)
            banks = Reader(v, m.banks[3:6], s.vec_filled, s.vec_read)
            tt = nc.vector.tensor_tensor
            for mt in range(KD):
                v.wait_ge(s.act_read, 8 * (mt // 2) + 7 + mt % 2)
                if mt:
                    v.wait_ge(s.comb_ready, mt)
                for n, br in enumerate((0, 1, 3)):
                    bank = banks.take()
                    tt(tmp[:, n], sig[:, br, mt % 4, :], bank[:, :], ALU.mult).then_inc(s.vec_read, 1)
                banks.settle()
                step.mark(tt(tmp[:, 3], tmp[:, 2], sig[:, 2, mt % 4, :], ALU.mult))
                step.step(tt(tmp[:, 0], tmp[:, 0], tmp[:, 1], ALU.add))
                tt(comb[:, mt, :], tmp[:, 0], tmp[:, 3], ALU.add).then_inc(s.comb_ready, 1)
            for n in range(4):
                for t in range(NT):
                    bank = banks.take()
                    xs = m.x[:, t, n * PANEL:(n + 1) * PANEL]
                    tt(xs, xs, bank[:, 0:PANEL], ALU.add).then_inc(s.vec_read, 1)
    clear(nc, s)



def phase_embed(m, layer):
    nc, io = m.nc, m.io
    with ExitStack() as ctx:
        s = semaphores(nc, ctx, COMMON + " rms_ready h_ready sig_used")
        sb = lambda n, shape, dt=F32: ctx.enter_context(nc.sbuf_tensor(n, shape, dt))
        gain = sb("gain_ple", [P, D])
        small = sb("small7", [P, 16])
        h = sb("h_ple", [P, NT, D])
        pT = sb("pT", [P, 2, T])
        wp = sb("w_ple", [P, 2, D])
        sig = sb("sig_ple", [P, 2, PANEL])
        ss, rms, rstd = small[:, 0:4], small[:, 4:8], small[:, 8:12]
        panels = Panels(m, s, [(weight(io.ple_w_gate, layer, 0, KD, n * PANEL, PANEL), KD, PANEL) for n in range(4)])
        block = ctx.enter_context(nc.Block())

        @block.tensor
        def _(pe):
            to_act = Banks(pe, m.banks[0:3], s.act_filled, s.act_read)
            to_vec = Banks(pe, m.banks[3:6], s.vec_filled, s.vec_read)
            norm_transposes(m, s, pe, to_act, to_vec, h)
            pe.wait_ge(s.params_in, 16 * 3)
            for n in range(4):
                w = panel_view(panels.landed(pe, n), KD)
                for t in range(NT):
                    tok = slice(t * P, (t + 1) * P)
                    bank = to_act.open()
                    for k in range(KD):
                        ins = nc.tensor.matmul(bank[:, 0:PANEL], m.hT[:, k, tok], w[:, k, :], start=(k == 0), stop=(k == KD - 1))
                    ins.then_inc(s.act_filled, 1)
                    bank = to_vec.open()
                    for k in range(2):
                        ins = nc.tensor.matmul(bank[:, 0:PANEL], pT[:, k, tok], wp[:, k, n * PANEL:(n + 1) * PANEL], start=(k == 0), stop=(k == 1))
                    ins.then_inc(s.vec_filled, 1)
                panels.released.append((s.act_filled, to_act.n))

        @block.sync
        def _(sp):
            sp.dma_start(gain[:, :], io.ple_norm[bass.ds(layer, 1), :].partition_broadcast(P).rearrange("p l d -> p (l d)")).then_inc(s.params_in, 16)
            sp.dma_start(pT[:, :, :], weight(io.p, layer, 0, 2, 0, T)).then_inc(s.params_in, 16)
            sp.dma_start(wp[:, :, :], weight(io.ple_w, layer, 0, 2, 0, D)).then_inc(s.params_in, 16)
            panels.stream(sp)

        @block.scalar
        def _(act):
            step = Link(act, s.act_step)
            banks = Reader(act, m.banks[0:3], s.act_filled, s.act_read)
            norm_scalar(m, s, act, step, ss, rms, h)
            norm_copy(m, act, banks, 0)
            for i in range(4 * NT):
                bank = banks.take()
                if i >= 2:
                    act.wait_ge(s.sig_used, i - 1)
                nc.scalar.activation(sig[:, i % 2, :], bank[:, 0:PANEL], ACT.Sigmoid).then_inc(s.act_read, 1)

        @block.vector
        def _(v):
            step = Link(v, s.vec_step)
            banks = Reader(v, m.banks[3:6], s.vec_filled, s.vec_read)
            v.wait_ge(s.params_in, 16 * 3)
            norm_vector(m, s, v, step, rms, rstd, gain[:, :], h)
            norm_copy(m, v, banks, 1)
            for i in range(4 * NT):
                n, t = i // NT, i % NT
                bank = banks.take()
                v.wait_ge(s.act_read, NT + i + 1)
                nc.vector.tensor_tensor(sig[:, i % 2, :], sig[:, i % 2, :], bank[:, 0:PANEL], ALU.mult).then_inc(s.vec_read, 1)
                banks.settle()
                xs = m.x[:, t, n * PANEL:(n + 1) * PANEL]
                nc.vector.tensor_tensor(xs, xs, sig[:, i % 2, :], ALU.add).then_inc(s.sig_used, 1)
    clear(nc, s)



RINGS = 8
PAIRS = PEER_HEADS // 2
TURN = 2 * TOPK
LEAST = -3e38


def phase_peer(m, layer):
    nc, io = m.nc, m.io
    with ExitStack() as ctx:
        s = semaphores(nc, ctx, COMMON + " rms_ready h_ready queries_in panel_in query_filled query_here score_filled scores_here paced_sp "
                       "topped exp_done selected u_free v_free out_free tanh_in tanh_done w_ready dg_done idx_here paced paced_v")
        sb = lambda n, shape, dt=F32: ctx.enter_context(nc.sbuf_tensor(n, shape, dt))
        u = sb("u_rows", [P, RINGS, D])
        vr = sb("v_rows", [P, RINGS, D])
        dg = sb("dg", [P, RINGS, P])
        h = sb("h", [P, NT, D])
        hT = sb("hT_ffn", [P, KD, T])
        m.hT = hT
        hcur = sb("h_tile", [P, D])
        small = sb("small5", [P, 16])
        ss, rms, rstd = small[:, 0:4], small[:, 4:8], small[:, 8:12]
        keys = sb("keys", [P, 4, KEYS])
        panel = sb("panel_query", [P, KD, 4 * P])
        qry = sb("qry", [P, 4, T])
        scores = sb("scores", [P, PAIRS * NT, 4, KEYS])
        sc = sb("sel_s", [P, 2, KEYS])
        sc2 = sb("sel_s2", [P, 2, KEYS])
        val = sb("sel_v", [P, 2, TOPK])
        vi = sb("sel_i", [P, 2, TOPK], U32)
        vif = sb("sel_if", [P, 2, TOPK])
        cand = sb("sel_c", [P, TOPK, TOPK])
        cand2 = sb("sel_c2", [P, TOPK, TOPK])
        top = sb("sel_top", [P, TOPK])
        pos = sb("sel_pos", [P, TOPK], U32)
        ab = sb("sel_ab", [P, 2, TOPK], U32)
        abf = sb("sel_abf", [P, 2, TOPK])
        hit = sb("sel_hit", [P, 2 * TOPK, TOPK])
        chosen = sb("sel_ch", [P, 2, TOPK])
        expo = sb("sel_e", [P, TOPK])
        one = sb("sel_one", [P, 8])
        idx_all = sb("idx_all", [P, NT * PEER_HEADS * TOPK], U32)
        gate_all = sb("gate_all", [P, NT * PEER_HEADS * TOPK])
        idx = [sb(f"idx{k}", [P, TOPK], U32) for k in range(2)]
        act_u = sb("act_u", [P, TURN])
        inner = sb("act_in", [P, TURN])
        th = sb("act_th", [P, TURN])
        w = sb("act_w", [P, TURN])
        gain = u[:, 0, :]
        by_turn = scores[:, :, :, :].rearrange("p b c k -> p (b c k)")
        hflat = h[:, :, :].rearrange("p t d -> p (t d)")
        xflat = m.x[:, :, :].rearrange("p t d -> p (t d)")
        tables = io.peer_u.rearrange("l e d -> (l e) d"), io.peer_v.rearrange("l e d -> (l e) d")
        out_banks = [(m.banks[4], m.banks[5]), (m.banks[6], m.banks[7])]

        def turns(eng, turn):
            with eng.Fori(0, PAIRS - 1) as pair:
                with eng.Fori(0, NT) as t:
                    turn(pair, t, pair * NT + t, True, True)
            with eng.Fori(0, NT - 1) as t:
                turn(PAIRS - 1, t, (PAIRS - 1) * NT + t, False, True)
            turn(PAIRS - 1, NT - 1, PAIRS * NT - 1, False, False)

        def landed(eng, sems, b, n):
            uses = (layer * (NT * PAIRS) + b) * (TURN // RINGS) + (n // RINGS + 1)
            eng.wait_ge(sems[n % RINGS], uses * 16)

        block = ctx.enter_context(nc.Block())

        @block.gpsimd
        def _(pool):
            pool.sem_inc(s.u_free, RINGS)
            pool.sem_inc(s.v_free, RINGS)
            pool.sem_inc(s.out_free, 2)

            def paced():
                pool.sem_inc(s.paced, 1)

            def turn(pair, t, b, project, more):
                for hh in range(2):
                    pool.wait_ge(s.selected, b * 2 + (hh + 1))
                    paced()
                    nc.gpsimd.tensor_copy(idx[hh][:, :], idx_all[:, bass.ds((b * 2 + hh) * TOPK, TOPK)]).then_inc(s.idx_here, 1)
                    pool.wait_ge(s.idx_here, b * 2 + (hh + 1))
                    paced()
                    for g in range(TOPK // RINGS):
                        for free, rows, table, sems in ((s.u_free, u, tables[0], m.u_landed), (s.v_free, vr, tables[1], m.v_landed)):
                            for k in range(RINGS):
                                n = hh * TOPK + g * RINGS + k
                                pool.wait_ge(free, b * TURN + (n + 1))
                                paced()
                                nc.gpsimd.indirect_dma_start(
                                    out=rows[:, k, :], out_offset=None, in_=table,
                                    in_offset=bass.IndirectOffsetOnAxis(ap=idx[hh][:, g * RINGS + k:g * RINGS + k + 1], axis=0),
                                ).then_inc(sems[k], 16)

            turns(pool, turn)

        @block.sync
        def _(sp):
            sp.dma_start(gain, io.norm_ffn[bass.ds(layer, 1), :].partition_broadcast(P).rearrange("p l d -> p (l d)")).then_inc(s.params_in, 16)
            sp.dma_start(panel[:, :, :], weight(io.peer_w_query, layer, 0, KD, 0, 4 * P)).then_inc(s.queries_in, 16)
            for n, a in enumerate((io.peer_keys1, io.peer_keys2) * 2):
                sp.dma_start(keys[:, n, :], a[bass.ds(layer, 1)].rearrange("l d k -> d (l k)")).then_inc(s.queries_in, 16)
            sp.wait_ge(s.act_filled, NT + 1)
            sp.sem_inc(s.query_filled, 1)
            with sp.Fori(0, (PAIRS - 1) * NT) as b:
                sp.wait_ge(s.query_filled, b + 1)
                sp.sem_inc(s.paced_sp, 1)
                src = io.peer_w_query[bass.ds(layer, 1), :, bass.ds(b * P + 4 * P, P)].rearrange("l (k p) c -> p (l k) c", p=P)
                sp.dma_start(panel[:, :, 0:P], src).then_inc(s.panel_in, 16)

        @block.vector
        def _(v):
            step = Link(v, s.vec_step)
            banks = Reader(v, m.banks[2:4], s.vec_filled, s.vec_read)
            tt, ts, stt = nc.vector.tensor_tensor, nc.vector.tensor_scalar, nc.vector.scalar_tensor_tensor

            def choose(j):
                step.step(nc.vector.tensor_copy(sc[:, :, :].rearrange("p a k -> p (a k)"), by_turn[:, bass.ds(j * 2 * KEYS, 2 * KEYS)]))
                for half in range(2):
                    step.mark(nc.vector.max(val[:, half, 0:8], sc[:, half, :]))
                step.settle()
                for half in range(2):
                    step.mark(nc.vector.max_index(vi[:, half, 0:8], val[:, half, 0:8], sc[:, half, :]))
                    step.mark(nc.vector.match_replace(sc2[:, half, :], val[:, half, 0:8], sc[:, half, :], LEAST))
                step.settle()
                for half in range(2):
                    step.mark(nc.vector.max(val[:, half, 8:16], sc2[:, half, :]))
                step.settle()
                for half in range(2):
                    step.mark(nc.vector.max_index(vi[:, half, 8:16], val[:, half, 8:16], sc2[:, half, :]))
                step.mark(tt(cand[:, :, :], over(val[:, 0, :].unsqueeze(2), (P, TOPK, TOPK)), over(val[:, 1, :].unsqueeze(1), (P, TOPK, TOPK)), ALU.add))
                step.settle()
                cf, cf2 = (a[:, :, :].rearrange("p a b -> p (a b)") for a in (cand, cand2))
                step.mark(nc.vector.tensor_copy(vif[:, :, :], vi[:, :, :]))
                step.step(nc.vector.max(top[:, 0:8], cf))
                step.mark(ts(one[:, 0:1], top[:, 0:1], -1.0, None, ALU.mult))
                step.mark(nc.vector.max_index(pos[:, 0:8], top[:, 0:8], cf))
                step.step(nc.vector.match_replace(cf2, top[:, 0:8], cf, LEAST))
                nc.vector.max(top[:, 8:16], cf2).then_inc(s.topped, 1)
                v.wait_ge(s.topped, j + 1)
                v.sem_inc(s.paced_v, 1)
                step.step(nc.vector.max_index(pos[:, 8:16], top[:, 8:16], cf2))
                step.mark(ts(ab[:, 0, :], pos[:, :], 4, None, ALU.logical_shift_right))
                step.step(ts(ab[:, 1, :], pos[:, :], 15, None, ALU.bitwise_and))
                step.step(nc.vector.tensor_copy(abf[:, :, :], ab[:, :, :]))
                step.step(tt(hit[:, :, :], over(abf[:, :, :].rearrange("p a k -> p (a k)").unsqueeze(2), (P, 2 * TOPK, TOPK)),
                             over(m.c("iota").unsqueeze(1), (P, 2 * TOPK, TOPK)), ALU.is_equal))
                h4 = hit[:, :, :].rearrange("p (a k) n -> p a k n", a=2)
                step.step(tt(h4, h4, over(vif[:, :, :].unsqueeze(2), (P, 2, TOPK, TOPK)), ALU.mult))
                step.step(nc.vector.tensor_reduce(chosen[:, :, :].rearrange("p a k -> p (a k)"), hit[:, :, :], AX_X, ALU.add))
                step.step(stt(out=chosen[:, 0, :], in0=chosen[:, 0, :], scalar=float(KEYS), in1=chosen[:, 1, :], op0=ALU.mult, op1=ALU.add))
                step.mark(ts(idx_all[:, bass.ds(j * TOPK, TOPK)], chosen[:, 0, :], m.row_base[:, 0:1], None, ALU.add))
                v.wait_ge(s.exp_done, j + 1)
                step.step(nc.vector.reciprocal(one[:, 2:3], one[:, 1:2]))
                step.step(ts(gate_all[:, bass.ds(j * TOPK, TOPK)], expo[:, :], one[:, 2:3], None, ALU.mult))
                v.sem_inc(s.selected, 1)
                step.restart()

            def group(b, g):
                at = slice(g * RINGS, (g + 1) * RINGS)
                for k in range(RINGS):
                    n = g * RINGS + k
                    landed(v, m.u_landed, b, n)
                    nc.vector.tensor_tensor_reduce(out=u[:, k, :], in0=u[:, k, :], in1=hcur[:, :], scale=1.0, scalar=0.0,
                                                   op0=ALU.mult, op1=ALU.add, accum_out=act_u[:, n:n + 1]).then_inc(s.u_free, 1)
                v.wait_ge(s.u_free, b * TURN + ((g + 2) * RINGS))
                step.step(tt(inner[:, at], act_u[:, at], act_u[:, at], ALU.mult))
                step.step(ts(inner[:, at], inner[:, at], 0.044715, 1.0, ALU.mult, ALU.add))
                tt(inner[:, at], inner[:, at], act_u[:, at], ALU.mult).then_inc(s.tanh_in, 1)
                v.wait_ge(s.tanh_done, b * 4 + (g + 1))
                step.step(stt(out=th[:, at], in0=th[:, at], scalar=1.0, in1=act_u[:, at], op0=ALU.add, op1=ALU.mult))
                stt(out=w[:, at], in0=th[:, at], scalar=0.5, in1=gate_all[:, bass.ds((b * 4 + g) * RINGS, RINGS)],
                    op0=ALU.mult, op1=ALU.mult).then_inc(s.w_ready, 1)

            def add_out(t, b, hh):
                v.wait_ge(s.v_free, b * TURN + (RINGS + TOPK * (hh + 1)))
                v.sem_inc(s.paced_v, 1)
                for half in range(2):
                    xs = xflat[:, bass.ds(t * D + half * 512, 512)]
                    step.mark(tt(xs, xs, out_banks[hh][half][:, :], ALU.add))
                step.settle()
                v.sem_inc(s.out_free, 1)

            def turn(pair, t, b, project, more):
                step.step(nc.vector.tensor_copy(hcur[:, :], hflat[:, bass.ds(t * D, D)]))
                group(b, 0)
                group(b, 1)
                step.restart()
                if project:
                    v.wait_ge(s.scores_here, b + 1)
                    v.sem_inc(s.paced_v, 1)
                if more:
                    choose(b * 2 + 2)
                group(b, 2)
                add_out(t, b, 0)
                group(b, 3)
                step.restart()
                if project:
                    v.wait_ge(s.scores_here, b + 2)
                    v.sem_inc(s.paced_v, 1)
                if more:
                    choose(b * 2 + 3)
                add_out(t, b, 1)
                step.restart()

            v.wait_ge(s.params_in, 16)
            norm_vector(m, s, v, step, rms, rstd, gain, h)
            norm_copy(m, v, banks, 1)
            for c in (1, 3):
                bank = banks.take()
                nc.vector.tensor_copy(qry[:, c, :], bank[:, :]).then_inc(s.vec_read, 1)
            for c in (1, 3):
                bank = banks.take()
                nc.vector.tensor_copy(scores[:, 0:NT, c, :], bank[:, :].rearrange("p (t k) -> p t k", t=NT)).then_inc(s.vec_read, 1)
            banks.settle()
            v.wait_ge(s.act_read, NT + 4)
            step.restart()
            with v.Fori(0, 2) as j:
                choose(j)
            turns(v, turn)
            step.step(ts(m.row_base[:, :], m.row_base[:, :], float(EXPERTS), None, ALU.add))

        @block.scalar
        def _(act):
            def weigh(j):
                act.wait_ge(s.topped, j + 1)
                nc.scalar.activation(expo[:, :], top[:, :], ACT.Exp, bias=one[:, 0:1], accum_out=one[:, 1:2]).then_inc(s.exp_done, 1)

            def group(b, g):
                at = slice(g * RINGS, (g + 1) * RINGS)
                act.wait_ge(s.tanh_in, b * 4 + (g + 1))
                nc.scalar.activation(th[:, at], inner[:, at], ACT.Tanh, scale=0.7978845608028654).then_inc(s.tanh_done, 1)
                act.wait_ge(s.w_ready, b * 4 + (g + 1))
                for k in range(RINGS):
                    n = g * RINGS + k
                    act.wait_ge(s.v_free, b * TURN + (n + 1))
                    nc.scalar.activation(dg[:, k, :], m.c("ident"), ACT.Copy, scale=w[:, n:n + 1]).then_inc(s.dg_done, 1)

            def turn(pair, t, b, project, more):
                if project:
                    act.wait_ge(s.query_filled, b + 2)
                    nc.scalar.activation(qry[:, 0, :], m.banks[0][:, :], ACT.Copy).then_inc(s.query_here, 1)
                group(b, 0)
                group(b, 1)
                if project:
                    act.wait_ge(s.score_filled, b + 1)
                    nc.scalar.activation(scores[:, bass.ds(pair * NT + NT, NT), bass.ds(t, 1), :].rearrange("p b c k -> p b (c k)"),
                                         m.banks[2][:, :].rearrange("p (t k) -> p t k", t=NT), ACT.Copy).then_inc(s.scores_here, 1)
                if more:
                    weigh(b * 2 + 2)
                group(b, 2)
                group(b, 3)
                if more:
                    weigh(b * 2 + 3)

            step = Link(act, s.act_step)
            banks = Reader(act, m.banks[0:2], s.act_filled, s.act_read)
            norm_scalar(m, s, act, step, ss, rms, h)
            norm_copy(m, act, banks, 0)
            for c in (0, 2):
                bank = banks.take()
                nc.scalar.activation(qry[:, c, :], bank[:, :], ACT.Copy).then_inc(s.act_read, 1)
            for c in (0, 2):
                bank = banks.take()
                nc.scalar.activation(scores[:, 0:NT, c, :], bank[:, :].rearrange("p (t k) -> p t k", t=NT), ACT.Copy).then_inc(s.act_read, 1)
            banks.settle()
            act.sem_inc(s.scores_here, 1)
            with act.Fori(0, 2) as j:
                weigh(j)
            turns(act, turn)

        @block.tensor
        def _(pe):
            to_act = Banks(pe, m.banks[0:2], s.act_filled, s.act_read)
            to_vec = Banks(pe, m.banks[2:4], s.vec_filled, s.vec_read)
            norm_transposes(m, s, pe, to_act, to_vec, h)
            pe.wait_ge(s.queries_in, 16 * 5)
            for c in range(4):
                banks = (to_act, to_vec)[c % 2]
                bank = banks.open()
                for k in range(KD):
                    ins = nc.tensor.matmul(bank[:, :], panel[:, k, c * P:(c + 1) * P], hT[:, k, :], start=(k == 0), stop=(k == KD - 1))
                ins.then_inc(banks.filled, 1)
            for c in range(4):
                banks = (to_act, to_vec)[c % 2]
                bank = banks.open()
                for t in range(NT):
                    ins = nc.tensor.matmul(bank[:, t * KEYS:(t + 1) * KEYS], qry[:, c, t * P:(t + 1) * P], keys[:, c, :], start=True, stop=True)
                ins.then_inc(banks.filled, 1)
            to_act.all_read()
            to_vec.all_read()

            def queries(b):
                pe.wait_ge(s.panel_in, b * 16 + 16)
                pe.wait_ge(s.scores_here, b + 1)
                for k in range(KD):
                    ins = nc.tensor.matmul(m.banks[0][:, :], panel[:, k, 0:P], hT[:, k, :], start=(k == 0), stop=(k == KD - 1))
                ins.then_inc(s.query_filled, 1)

            def score(b, t_chunk):
                pe.wait_ge(s.query_here, b + 1)
                half_keys = keys[:, :, :].rearrange("p c k -> p (c k)")[:, bass.ds(t_chunk * KEYS, KEYS)]
                for t in range(NT):
                    ins = nc.tensor.matmul(m.banks[2][:, t * KEYS:(t + 1) * KEYS], qry[:, 0, t * P:(t + 1) * P], half_keys, start=True, stop=True)
                ins.then_inc(s.score_filled, 1)

            def turn(pair, t, b, project, more):
                if project:
                    queries(b)
                for hh in range(2):
                    pe.wait_ge(s.out_free, b * 2 + (hh + 1))
                    for i in range(TOPK):
                        n = hh * TOPK + i
                        if project and n == RINGS:
                            score(b, t)
                        landed(pe, m.v_landed, b, n)
                        pe.wait_ge(s.dg_done, b * TURN + (n + 1))
                        for half in range(2):
                            ins = nc.tensor.matmul(out_banks[hh][half][:, :], dg[:, n % RINGS, :], vr[:, n % RINGS, half * 512:half * 512 + 512],
                                                   start=(i == 0), stop=(i == TOPK - 1))
                        ins.then_inc(s.v_free, 1)

            turns(pe, turn)
    clear(nc, s)


def decoder_trunk(nc, io, phases="123456"):
    with ExitStack() as ctx:
        sb = lambda n, shape, dt=F32: ctx.enter_context(nc.sbuf_tensor(n, shape, dt))
        once = semaphores(nc, ctx, "loaded stored")
        swdge = [ctx.enter_context(nc.semaphore(f"{n}_landed{k}")) for n in "uv" for k in range(RINGS)]
        m = Machine()
        m.nc, m.io, m.u_landed, m.v_landed = nc, io, swdge[:RINGS], swdge[RINGS:]
        m.banks = [ctx.enter_context(nc.psum_tensor(f"bank{k}", [P, 512], F32)) for k in range(8)]
        consts = sb("consts", [P, CONSTS.shape[1]])
        m.c = lambda name: consts[:, WHERE[name][0]:WHERE[name][0] + WHERE[name][1]]
        m.x = sb("x", [P, NT, D])
        m.row_base = sb("row_base", [P, 1])

        with nc.Block() as block:
            @block.sync
            def _(sp):
                sp.dma_start(consts[:, :], io.consts).then_inc(once.loaded, 16)
                sp.dma_start(m.x[:, :, :], io.x.rearrange("b (t p) d -> p (b t) d", p=P)).then_inc(once.loaded, 16)
                sp.wait_ge(once.loaded, 32)

            @block.vector
            def _(v):
                nc.vector.memset(m.row_base[:, :], 0.0)

        with nc.Fori(0, DEPTH) as layer:
            with ExitStack() as mix:
                sm = lambda n, shape, dt=F32: mix.enter_context(nc.sbuf_tensor(n, shape, dt))
                m.hT = sm("hT", [P, KD, T])
                ring = sm("ring", [P, RING, KD * PANEL])
                m.ring = ring
                m.aT = sm("aT", [P, 2, T])
                m.sT = sm("sT", [P, 2, T])
                m.ba = sm("ba", [P, NT, 2 * DN])
                m.conv_w = sm("conv_w", [P, 3 * DN, 4])
                m.a_log = sm("a_log", [P, DN])
                m.dt_bias = sm("dt_bias", [P, DN])
                m.out_gain = sm("out_gain", [P, 1])
                with ExitStack() as front:
                    sf = lambda n, shape, dt=F32: front.enter_context(nc.sbuf_tensor(n, shape, dt))
                    m.work_a = sf("work_a", [P, NT * D])
                    m.qkT = m.work_a[:, :].rearrange("p (b n) -> p b n", b=8)
                    m.att_qk = sf("att_qk", [P, 4, QK_HEADS * HEAD])
                    m.att_v = sf("att_v", [P, 4, SLOTS * HEAD])
                    m.uT = sf("uT", [P, 2, T])
                    m.rot = sf("rot", [P, 2, 8, T])
                    m.s5_in = sf("s5_in", [P, 2, 8 * P])
                    m.s5_out = sf("s5_out", [P, 2, 8 * P])
                    m.s5_d = sf("s5_d", [P, 2])
                    m.mag = sf("mag", [P, 8])
                    m.seed = sf("seed", [P, 2, 8])
                    if "1" in phases:
                        phase_project(m, layer)
                    if "2" in phases:
                        phase_attend(m, layer)
                m.bT = sm("bT", [P, DN, T])
                if "3" in phases:
                    phase_deltanet(m, layer)
                if "4" in phases:
                    phase_combine(m, layer)
            if "5" in phases:
                phase_peer(m, layer)
            with ExitStack() as back:
                m.hT = back.enter_context(nc.sbuf_tensor("hT_ple", [P, KD, T], F32))
                m.ring = back.enter_context(nc.sbuf_tensor("ring_ple", [P, RING, KD * PANEL], F32))
                if "6" in phases:
                    phase_embed(m, layer)

        with nc.Block() as block:
            @block.sync
            def _(sp):
                sp.dma_start(io.out.rearrange("b (t p) d -> p (b t) d", p=P), m.x[:, :, :]).then_inc(once.stored, 16)
                sp.wait_ge(once.stored, 16)


def kernel(**inputs):
    import concourse.bacc as bacc
    from concourse.bass_utils import run_bass_kernel_spmd

    a = {k: np.asarray(v) for k, v in inputs.items()}
    n = DEPTH
    swap = lambda t: np.ascontiguousarray(np.swapaxes(t, -1, -2))
    a["dn_conv"] = np.ascontiguousarray(a["dn_conv"].reshape(n, 4, 3 * DN, P).transpose(0, 3, 2, 1))
    a["s5_a_re"] = swap(a["s5_a_re"].reshape(n, S5_BLOCKS, P))
    a["s5_a_im"] = swap(a["s5_a_im"].reshape(n, S5_BLOCKS, P))
    a["s5_b_re"] = a["s5_b_re"].reshape(n, S5_BLOCKS * P, 16)
    a["s5_b_im"] = a["s5_b_im"].reshape(n, S5_BLOCKS * P, 16)
    a["s5_c_re"] = swap(a["s5_c_re"]).reshape(n, S5_BLOCKS * P, 16)
    a["s5_c_im"] = swap(a["s5_c_im"]).reshape(n, S5_BLOCKS * P, 16)
    a["s5_d"] = swap(a["s5_d"].reshape(n, 2, P))
    a["s5_log_dt"] = swap(a["s5_log_dt"].reshape(n, S5_BLOCKS, 2))
    a["dn_out_gain"] = a["dn_out_gain"].reshape(n, P, 1)
    a["peer_keys1"] = swap(a["peer_keys1"])
    a["peer_keys2"] = swap(a["peer_keys2"])
    a["p"] = swap(a["p"].reshape(n, T, PLE))
    a["consts"] = CONSTS
    nc = bacc.Bacc("TRN2", target_bir_lowering=False, num_devices=1)
    arrays, aps = {}, {}
    for name, t in a.items():
        t = np.ascontiguousarray(t)
        arrays[f"in_{name}"] = t
        aps[name] = nc.dram_tensor(f"in_{name}", t.shape, mybir.dt.from_np(t.dtype), kind="ExternalInput").ap()
    aps["out"] = nc.dram_tensor("out_x", (1, T, D), F32, kind="ExternalOutput").ap()
    io = namedtuple("Arrays", list(aps))(*aps.values())
    decoder_trunk(nc, io)
    got = run_bass_kernel_spmd(nc, [arrays], core_ids=[0])
    return got.results[0]["out_x"]
```

```python
from collections import namedtuple
from contextlib import ExitStack

import numpy as np

import concourse.bass as bass
from concourse import mybir

F32 = mybir.dt.float32
U32 = mybir.dt.uint32
I32 = mybir.dt.int32
ALU = mybir.AluOpType
ACT = mybir.ActivationFunctionType
AX_X = mybir.AxisListType.X

P = 128
T = 512
NT = T // P
D = 1024
KD = D // P
DEPTH = 2
EPS = 1e-6

HEAD = 64
SLOTS = 4
GROUPS = 3
WINDOW = 128
QKV_ATT = (GROUPS + 2) * SLOTS * HEAD
QK_HEADS = (GROUPS + 1) * SLOTS
DN = 4
S5_BLOCKS = 8
S5_G = 16
PEER_HEADS = 8
KEYS = 128
TOPK = 16
EXPERTS = KEYS * KEYS
PLE = 256

COL_ATT = 0
COL_QKV = COL_ATT + QKV_ATT
COL_Z = COL_QKV + 3 * DN * P
COL_BA = COL_Z + DN * P
COL_U = COL_BA + 2 * DN
COL_GATES = COL_U + 256
IN_COLS = COL_GATES + 3 * D

PANEL = 256
RING = 3
BANKS = 3
NEG = -1e30
PI = float(np.pi)
TWO_PI_HI = 6.28125
TWO_PI_LO = float(2 * np.pi - 6.28125)
SLOPES = 2.0 ** (-8.0 * np.arange(1, GROUPS * SLOTS + 1) / (GROUPS * SLOTS))


def shape_constants():
    i = np.arange(P)[:, None]
    j = np.arange(P)[None, :]
    parts = {}
    parts["ident"] = np.eye(P)
    parts["ones"] = np.ones((P, P))
    parts["triu"] = i <= j
    parts["strict"] = np.where(i > j, 0.0, NEG)
    parts["incl_t"] = np.where(j >= i, 0.0, NEG)
    for b in (1, 2, 4, 8, 16, 32, 64):
        parts[f"join{b}"] = (i // (2 * b) == j // (2 * b)) & (j // b % 2 == 1) & (i // b % 2 == 0)
    parts["join1_low"] = ((i // 2 == j // 2) & (i % 2 == 1) & (j % 2 == 0))
    far = 1e33
    d = np.concatenate([4 * (i - j) + delta for delta in range(3, -4, -1)], axis=1)
    parts["dist_g0"] = np.where((d >= 0) & (d <= WINDOW), d, far)
    d = 4 * (i - j)
    parts["dist_g1"] = np.where(d >= 0, d, far)
    parts["dist_g2"] = np.where((d >= 0) & (d % 16 == 0), d, far)
    parts["iota"] = np.broadcast_to(np.arange(TOPK), (P, TOPK))
    parts["eps"] = np.full((P, 1), EPS)
    where, at = {}, 0
    for name, a in parts.items():
        where[name] = (at, a.shape[1])
        at += a.shape[1]
    return np.concatenate([np.asarray(a, np.float32) for a in parts.values()], axis=1), where


CONSTS, WHERE = shape_constants()


class Link:

    def __init__(self, eng, sem):
        self.eng, self.sem, self.n = eng, sem, 0

    def mark(self, ins):
        self.n += 1
        ins.then_inc(self.sem, 1)

    def settle(self):
        self.eng.wait_ge(self.sem, self.n)

    def step(self, ins):
        self.mark(ins)
        self.settle()

    def restart(self):
        self.settle()
        self.eng.sem_clear(self.sem)
        self.n = 0


class Machine:
    pass


def over(ap, shape):
    return ap.to_broadcast(list(shape))


def semaphores(nc, ctx, names):
    names = names.split()
    return namedtuple("Semaphores", names)(*[ctx.enter_context(nc.semaphore(n)) for n in names])


def clear(nc, group):
    nums = sorted(s.num for s in group)
    assert nums[-1] - nums[0] == len(nums) - 1
    nc.all_engine_barrier(sems_to_clear=range(nums[0], nums[-1] + 1))


COMMON = "landed0 landed1 landed2 params_in act_filled act_read vec_filled vec_read act_step vec_step pool_step"


class Panels:

    def __init__(self, m, s, sources, early=0):
        self.m, self.sources, self.early = m, sources, early
        self.sems = s.landed0, s.landed1, s.landed2
        self.released = []

    def landed(self, pe, n):
        if n >= self.early:
            pe.wait_ge(self.sems[n % RING], 16 * ((n - self.early) // RING + 1))
        return self.m.ring[:, n % RING]

    def load(self, sp, n, source):
        src, kt, cols = source
        if n >= RING:
            sem, count = self.released[n - RING]
            sp.wait_ge(sem, count)
        dst = self.m.ring[:, n % RING].rearrange("p (k c) -> p k c", k=kt)[:, :, 0:cols]
        sp.dma_start(dst, src).then_inc(self.sems[n % RING], 16)

    def stream(self, sp, following=()):
        end = len(self.sources)
        for n in range(self.early, end):
            self.load(sp, n, self.sources[n])
        if following:
            for n in range(end, end + RING):
                self.load(sp, n, following[n % RING])
            for slot in range(RING):
                loads = len([n for n in range(self.early, end + RING) if n % RING == slot])
                sp.wait_ge(self.sems[slot], 16 * loads)


def panel_view(slot, kt, cols=None):
    v = slot.rearrange("p (k c) -> p k c", k=kt)
    return v if cols is None else v[:, :, 0:cols]


def weight(ap, layer, k0, kt, c0, cols):
    return ap[bass.ds(layer, 1), k0 * P:(k0 + kt) * P, c0:c0 + cols].rearrange("l (k p) c -> p (l k) c", p=P)


class Banks:

    def __init__(self, pe, banks, filled, read):
        self.pe, self.banks, self.filled, self.read, self.n = pe, banks, filled, read, 0

    def open(self):
        self.n += 1
        if self.n > len(self.banks):
            self.pe.wait_ge(self.read, self.n - len(self.banks))
        return self.banks[(self.n - 1) % len(self.banks)]

    def all_read(self):
        self.pe.wait_ge(self.read, self.n)


class Reader:

    def __init__(self, eng, banks, filled, read):
        self.eng, self.banks, self.filled, self.read, self.n = eng, banks, filled, read, 0

    def take(self):
        self.n += 1
        self.eng.wait_ge(self.filled, self.n)
        return self.banks[(self.n - 1) % len(self.banks)]

    def settle(self):
        self.eng.wait_ge(self.read, self.n)


def input_panels(io, layer, phase):
    cols = {"project": [COL_U] + [COL_ATT + n * PANEL for n in range(QKV_ATT // PANEL)],
            "deltanet": [COL_QKV + n * PANEL for n in range(4 * DN * P // PANEL)],
            "combine": [COL_GATES + br * D + n * PANEL for n in range(D // PANEL) for br in range(3)]}[phase]
    return [(weight(io.w_in, layer, 0, KD, c, PANEL), KD, PANEL) for c in cols]



def norm_scalar(m, s, act, step, ss, rms, h):
    for t in range(NT):
        step.step(m.nc.scalar.activation(h[:, t], m.x[:, t], ACT.Square, accum_out=ss[:, t:t + 1]))
        m.nc.scalar.activation(rms[:, t:t + 1], ss[:, t:t + 1], ACT.Sqrt, bias=m.c("eps"), scale=1.0 / D).then_inc(s.rms_ready, 1)


def norm_vector(m, s, v, step, rms, rstd, gain, h):
    for t in range(NT):
        v.wait_ge(s.rms_ready, t + 1)
        step.step(m.nc.vector.reciprocal(rstd[:, t:t + 1], rms[:, t:t + 1]))
        m.nc.vector.scalar_tensor_tensor(out=h[:, t], in0=m.x[:, t], scalar=rstd[:, t:t + 1], in1=gain,
                                         op0=ALU.mult, op1=ALU.mult).then_inc(s.h_ready, 1)


def norm_transposes(m, s, pe, to_act, to_vec, h):
    for t in range(NT):
        pe.wait_ge(s.h_ready, t + 1)
        for half, banks in ((0, to_act), (1, to_vec)):
            bank = banks.open()
            for k in range(4):
                kk = 4 * half + k
                ins = m.nc.tensor.transpose(bank[:, k * P:(k + 1) * P], h[:, t, kk * P:(kk + 1) * P], m.c("ident"))
            ins.then_inc(banks.filled, 1)
    to_act.all_read()
    to_vec.all_read()


def norm_copy(m, eng, reader, half):
    for t in range(NT):
        bank = reader.take()
        dst = m.hT[:, 4 * half:4 * half + 4, t * P:(t + 1) * P]
        src = bank[:, :].rearrange("p (k n) -> p k n", k=4)
        if half == 0:
            m.nc.scalar.activation(dst, src, ACT.Copy).then_inc(reader.read, 1)
        else:
            m.nc.vector.tensor_copy(dst, src).then_inc(reader.read, 1)



def phase_project(m, layer):
    nc, io = m.nc, m.io
    with ExitStack() as ctx:
        s = semaphores(nc, ctx, COMMON + " rms_ready h_ready s5_to_act s5_from_act gain_in seed_ready bb_placed qk_sq qk_ss qk_rms qk_ready")
        sb = lambda n, shape, dt=F32: ctx.enter_context(nc.sbuf_tensor(n, shape, dt))
        gain = sb("gain_mix", [P, D])
        qk_gain = sb("qk_gain", [P, QK_HEADS * HEAD])
        small = sb("small1", [P, 256])
        s5s = sb("s5_small", [P, 26, 8])
        s5i = sb("s5_int", [P, 8], I32)
        bmat = sb("s5_b", [P, 2, 8, 16])
        cmat = sb("s5_c", [P, 2, 8, 16])
        bb = sb("s5_bb", [P, 2, 8, 16])
        bbt = sb("s5_bbt", [P, 4, 8, 16])
        bbd = sb("s5_bbd", [P, 2, 8 * P])
        pool_t = sb("rot_tmp", [P, 2, 4 * 256])
        pool_w = sb("rot_w", [P, 6, 4])
        h = m.work_a[:, :].rearrange("p (t d) -> p t d", t=NT)
        ss, rms, rstd = small[:, 0:4], small[:, 4:8], small[:, 8:12]
        qss, qrms, qrstd = small[:, 16:80], small[:, 80:144], small[:, 144:208]
        panels = Panels(m, s, input_panels(io, layer, "project"))
        NPARAM = 16
        S5_AT = 2
        panel_count = {}

        block = ctx.enter_context(nc.Block())

        @block.tensor
        def _(pe):
            to_act = Banks(pe, m.banks[0:3], s.act_filled, s.act_read)
            to_vec = Banks(pe, m.banks[3:6], s.vec_filled, s.vec_read)
            norm_transposes(m, s, pe, to_act, to_vec, h)
            w = panel_view(panels.landed(pe, 0), KD)
            for mt in range(2):
                bank = to_act.open()
                for k in range(KD):
                    ins = nc.tensor.matmul(bank[:, :], w[:, k, mt * P:(mt + 1) * P], m.hT[:, k, :],
                                           start=(k == 0), stop=(k == KD - 1))
                ins.then_inc(s.act_filled, 1)
            panels.released.append((s.act_filled, to_act.n))
            for n in range(5):
                w = panel_view(panels.landed(pe, n + 1), KD)
                for r in range(4):
                    banks = (to_act, to_vec)[r % 2]
                    bank = banks.open()
                    for k in range(KD):
                        ins = nc.tensor.matmul(bank[:, 0:PANEL], m.hT[:, k, r::4], w[:, k, :],
                                               start=(k == 0), stop=(k == KD - 1))
                    ins.then_inc(banks.filled, 1)
                panels.released.append((s.vec_filled, to_vec.n))
                panel_count[n] = to_vec.n
                if n:
                    pe.wait_ge(s.qk_ready, n)
                    for b, banks in ((2 * n - 2, to_act), (2 * n - 1, to_vec)):
                        bank = banks.open()
                        for r in range(4):
                            ins = nc.tensor.transpose(bank[:, r * P:(r + 1) * P], m.att_qk[:, r, b * P:(b + 1) * P], m.c("ident"))
                        ins.then_inc(banks.filled, 1)
                if n == S5_AT:
                    pe.wait_ge(s.bb_placed, 1)
                    for part in range(2):
                        for half in range(2):
                            bank = to_act.open()
                            for b in range(4):
                                at = (4 * half + b) * P
                                ins = nc.tensor.transpose(bank[:, b * P:(b + 1) * P], bbd[:, part, at:at + P], m.c("ident"))
                            ins.then_inc(s.act_filled, 1)
            to_act.all_read()
            to_vec.all_read()

        @block.sync
        def _(sp):
            def load(dst, src):
                sp.dma_start(dst, src).then_inc(s.params_in, 16)
            sp.dma_start(gain[:, :], io.norm_mix[bass.ds(layer, 1), :].partition_broadcast(P).rearrange("p l d -> p (l d)")).then_inc(s.gain_in, 16)
            for n in range(2):
                src = (io.att_q_gain, io.att_k_gain)[n][bass.ds(layer, 1), :].partition_broadcast(P)
                load(qk_gain[:, n * HEAD:(n + 1) * HEAD], src.rearrange("p l d -> p (l d)"))
            load(s5s[:, 0], io.s5_a_re[bass.ds(layer, 1)].rearrange("l p b -> p (l b)"))
            load(s5s[:, 1], io.s5_a_im[bass.ds(layer, 1)].rearrange("l p b -> p (l b)"))
            for hh in range(2):
                src = io.s5_log_dt[bass.ds(layer, 1), hh, :].partition_broadcast(64)
                load(s5s[64 * hh:64 * hh + 64, 2], src.rearrange("p l b -> p (l b)"))
            for n, a in enumerate((io.s5_b_re, io.s5_b_im)):
                load(bmat[:, n], a[bass.ds(layer, 1)].rearrange("l (b p) c -> p (l b) c", p=P))
            for n, a in enumerate((io.s5_c_re, io.s5_c_im)):
                load(cmat[:, n], a[bass.ds(layer, 1)].rearrange("l (b p) c -> p (l b) c", p=P))
            load(m.s5_d[:, :], io.s5_d[bass.ds(layer, 1)].rearrange("l p c -> p (l c)"))
            load(m.conv_w[:, :, :], io.dn_conv[bass.ds(layer, 1)].rearrange("l p b k -> p (l b) k"))
            load(m.a_log[:, :], io.dn_a_log[bass.ds(layer, 1), :].partition_broadcast(P).rearrange("p l d -> p (l d)"))
            load(m.dt_bias[:, :], io.dn_dt_bias[bass.ds(layer, 1), :].partition_broadcast(P).rearrange("p l d -> p (l d)"))
            load(m.w_ba[:, :, :], weight(io.w_in, layer, 0, KD, COL_BA, 2 * DN))
            load(m.out_gain[:, :], io.dn_out_gain[bass.ds(layer, 1)].rearrange("l p c -> p (l c)"))
            panels.stream(sp)

        @block.scalar
        def _(act):
            step = Link(act, s.act_step)
            banks = Reader(act, m.banks[0:3], s.act_filled, s.act_read)
            norm_scalar(m, s, act, step, ss, rms, h)
            norm_copy(m, act, banks, 0)
            act.wait_ge(s.params_in, 16 * NPARAM)
            nc.scalar.activation(s5s[:, 3], s5s[:, 2], ACT.Exp).then_inc(s.s5_from_act, 1)
            act.wait_ge(s.s5_to_act, 1)
            nc.scalar.activation(m.mag[:, :], s5s[:, 4], ACT.Exp).then_inc(s.s5_from_act, 1)
            act.wait_ge(s.s5_to_act, 2)
            nc.scalar.activation(s5s[:, 8], s5s[:, 6], ACT.Sin).then_inc(s.s5_from_act, 1)
            nc.scalar.activation(s5s[:, 9], s5s[:, 7], ACT.Sin).then_inc(s.s5_from_act, 1)
            for mt in range(2):
                bank = banks.take()
                nc.scalar.activation(m.uT[:, mt, :], bank[:, :], ACT.Copy).then_inc(s.act_read, 1)
            for n in range(5):
                for r in (0, 2):
                    bank = banks.take()
                    dst = m.att_qk[:, r, n * PANEL:(n + 1) * PANEL] if n < 4 else m.att_v[:, r, :]
                    nc.scalar.activation(dst, bank[:, 0:PANEL], ACT.Copy).then_inc(s.act_read, 1)
                banks.settle()
                if n:
                    bank = banks.take()
                    nc.scalar.activation(m.qkT[:, 2 * n - 2, :], bank[:, :], ACT.Copy).then_inc(s.act_read, 1)
                if n == S5_AT:
                    for part in range(2):
                        for half in range(2):
                            bank = banks.take()
                            nc.scalar.activation(m.s5_in[:, part, half * 512:half * 512 + 512], bank[:, :], ACT.Copy).then_inc(s.act_read, 1)
                if n < 4:
                    act.wait_ge(s.vec_read, panel_count[n])
                    nc.scalar.activation(m.work_a[:, n * D:(n + 1) * D].rearrange("p (r c) -> p r c", r=4),
                                         m.att_qk[:, :, n * PANEL:(n + 1) * PANEL], ACT.Square).then_inc(s.qk_sq, 1)
                    act.wait_ge(s.qk_ss, n + 1)
                    nc.scalar.activation(qrms[:, 16 * n:16 * n + 16], qss[:, 16 * n:16 * n + 16], ACT.Sqrt,
                                         bias=m.c("eps"), scale=1.0 / HEAD).then_inc(s.qk_rms, 1)

        @block.vector
        def _(v):
            step = Link(v, s.vec_step)
            banks = Reader(v, m.banks[3:6], s.vec_filled, s.vec_read)
            tt, ts = nc.vector.tensor_tensor, nc.vector.tensor_scalar
            v.wait_ge(s.gain_in, 16)
            norm_vector(m, s, v, step, rms, rstd, gain[:, :], h)
            norm_copy(m, v, banks, 1)
            v.wait_ge(s.params_in, 16 * NPARAM)
            re, im, dt, ldt, th = s5s[:, 0], s5s[:, 1], s5s[:, 3], s5s[:, 4], s5s[:, 5]
            v.wait_ge(s.s5_from_act, 1)
            tt(ldt, re, dt, ALU.mult).then_inc(s.s5_to_act, 1)
            step.step(tt(th, im, dt, ALU.mult))
            step.step(ts(s5s[:, 6], th, 1.0 / (2 * PI), None, ALU.mult))
            step.step(nc.vector.tensor_copy(s5i[:, :], s5s[:, 6]))
            step.step(nc.vector.tensor_copy(s5s[:, 6], s5i[:, :]))
            step.step(nc.vector.scalar_tensor_tensor(out=s5s[:, 7], in0=s5s[:, 6], scalar=-TWO_PI_HI, in1=th, op0=ALU.mult, op1=ALU.add))
            step.step(nc.vector.scalar_tensor_tensor(out=s5s[:, 6], in0=s5s[:, 6], scalar=-TWO_PI_LO, in1=s5s[:, 7], op0=ALU.mult, op1=ALU.add))
            step.step(ts(s5s[:, 7], s5s[:, 6], PI / 2, None, ALU.add))
            for n in (6, 7):
                for cmp, bound, turn in ((ALU.is_gt, PI, -2 * PI), (ALU.is_lt, -PI, 2 * PI)):
                    step.step(ts(s5s[:, 10], s5s[:, n], bound, turn, cmp, ALU.mult))
                    step.step(tt(s5s[:, n], s5s[:, n], s5s[:, 10], ALU.add))
            step.step(ts(s5s[:, 6], s5s[:, 6], 3.1415925, -3.1415925, ALU.min, ALU.max))
            ts(s5s[:, 7], s5s[:, 7], 3.1415925, -3.1415925, ALU.min, ALU.max).then_inc(s.s5_to_act, 1)
            v.wait_ge(s.s5_from_act, 4)
            sin, cos = s5s[:, 8], s5s[:, 9]
            step.mark(nc.vector.tensor_copy(m.seed[:, 0], cos))
            nc.vector.tensor_copy(m.seed[:, 1], sin).then_inc(s.seed_ready, 1)
            g = [s5s[:, n] for n in range(11, 26)]
            step.mark(tt(g[0], m.mag[:, :], cos, ALU.mult))
            step.mark(tt(g[1], m.mag[:, :], sin, ALU.mult))
            step.mark(tt(g[2], re, re, ALU.mult))
            step.step(tt(g[3], im, im, ALU.mult))
            step.mark(ts(g[0], g[0], -1.0, None, ALU.add))
            step.step(tt(g[2], g[2], g[3], ALU.add))
            step.mark(nc.vector.reciprocal(g[4], g[2]))
            step.mark(tt(g[5], g[0], re, ALU.mult))
            step.mark(tt(g[6], g[1], im, ALU.mult))
            step.mark(tt(g[7], g[1], re, ALU.mult))
            step.step(tt(g[8], g[0], im, ALU.mult))
            step.mark(tt(g[5], g[5], g[6], ALU.add))
            step.step(tt(g[7], g[7], g[8], ALU.subtract))
            step.mark(tt(g[5], g[5], g[4], ALU.mult))
            step.step(tt(g[7], g[7], g[4], ALU.mult))
            cr = over(g[5].unsqueeze(2), (P, 8, 16))
            ci = over(g[7].unsqueeze(2), (P, 8, 16))
            step.mark(tt(bbt[:, 0], bmat[:, 0], cr, ALU.mult))
            step.mark(tt(bbt[:, 1], bmat[:, 1], ci, ALU.mult))
            step.mark(tt(bbt[:, 2], bmat[:, 1], cr, ALU.mult))
            step.step(tt(bbt[:, 3], bmat[:, 0], ci, ALU.mult))
            step.mark(tt(bb[:, 0], bbt[:, 0], bbt[:, 1], ALU.subtract))
            step.step(tt(bb[:, 1], bbt[:, 2], bbt[:, 3], ALU.add))
            for b in (bbd, m.s5_out):
                step.mark(nc.vector.memset(b[:, :, :], 0.0))
            step.settle()
            for part in range(2):
                for b in range(8):
                    for hh in range(2):
                        rows_ = slice(64 * hh, 64 * hh + 64)
                        at = b * P + 32 * (b % 4) + 16 * hh
                        step.mark(nc.vector.tensor_copy(bbd[rows_, part, at:at + 16], bb[rows_, part, b]))
                        step.mark(ts(m.s5_out[rows_, part, at:at + 16], cmat[rows_, part, b], (1.0, -1.0)[part], None, ALU.mult))
            step.settle()
            v.sem_inc(s.bb_placed, 1)
            step.mark(nc.vector.tensor_copy(qk_gain[:, 12 * HEAD:].rearrange("p (g c) -> p g c", g=4),
                                            over(qk_gain[:, HEAD:2 * HEAD].unsqueeze(1), (P, 4, HEAD))))
            step.step(ts(qk_gain[:, 0:HEAD], qk_gain[:, 0:HEAD], HEAD ** -0.5, None, ALU.mult))
            step.step(nc.vector.tensor_copy(qk_gain[:, HEAD:12 * HEAD].rearrange("p (g c) -> p g c", g=11),
                                            over(qk_gain[:, 0:HEAD].unsqueeze(1), (P, 11, HEAD))))
            for n in range(5):
                for r in (1, 3):
                    bank = banks.take()
                    dst = m.att_qk[:, r, n * PANEL:(n + 1) * PANEL] if n < 4 else m.att_v[:, r, :]
                    nc.vector.tensor_copy(dst, bank[:, 0:PANEL]).then_inc(s.vec_read, 1)
                banks.settle()
                if n:
                    bank = banks.take()
                    nc.vector.tensor_copy(m.qkT[:, 2 * n - 1, :], bank[:, :]).then_inc(s.vec_read, 1)
                if n < 4:
                    some = slice(16 * n, 16 * n + 16)
                    v.wait_ge(s.qk_sq, n + 1)
                    nc.vector.tensor_reduce(qss[:, some], m.work_a[:, n * D:(n + 1) * D].rearrange("p (g c) -> p g c", c=HEAD),
                                            AX_X, ALU.add).then_inc(s.qk_ss, 1)
                    v.wait_ge(s.qk_rms, n + 1)
                    step.step(nc.vector.reciprocal(qrstd[:, some], qrms[:, some]))
                    qk = m.att_qk[:, :, n * PANEL:(n + 1) * PANEL]
                    qk4 = qk.rearrange("p r (g c) -> p r g c", c=HEAD)
                    step.step(tt(qk4, qk4, over(qrstd[:, some].rearrange("p (r g) -> p r g", r=4).unsqueeze(3), (P, 4, 4, HEAD)), ALU.mult))
                    tt(qk, qk, over(qk_gain[:, n * PANEL:(n + 1) * PANEL].unsqueeze(1), (P, 4, PANEL)), ALU.mult).then_inc(s.qk_ready, 1)
        @block.gpsimd
        def _(pool):
            step = Link(pool, s.pool_step)
            tt = nc.gpsimd.tensor_tensor
            step.mark(nc.gpsimd.memset(m.rot[:, 0, :, 0:1], 1.0))
            step.mark(nc.gpsimd.memset(m.rot[:, 1, :, 0:1], 0.0))
            pool.wait_ge(s.seed_ready, 1)
            step.settle()
            for q in range(2):
                bl = slice(4 * q, 4 * q + 4)
                w = [m.seed[:, 0, bl], m.seed[:, 1, bl]]
                n = 1
                while n < T:
                    wr = over(w[0].unsqueeze(2), (P, 4, n))
                    wi = over(w[1].unsqueeze(2), (P, 4, n))
                    re, im = m.rot[:, 0, bl, 0:n], m.rot[:, 1, bl, 0:n]
                    t = [pool_t[:, k, 0:4 * n].rearrange("p (b n) -> p b n", b=4) for k in range(2)]
                    step.mark(tt(t[0], re, wr, ALU.mult))
                    step.step(tt(t[1], im, wi, ALU.mult))
                    step.step(tt(m.rot[:, 0, bl, n:2 * n], t[0], t[1], ALU.subtract))
                    step.mark(tt(t[0], re, wi, ALU.mult))
                    step.step(tt(t[1], im, wr, ALU.mult))
                    step.step(tt(m.rot[:, 1, bl, n:2 * n], t[0], t[1], ALU.add))
                    n *= 2
                    if n < T:
                        e = [pool_w[:, k] for k in range(6)]
                        new = (2, 3) if n.bit_length() % 2 == 0 else (4, 5)
                        step.mark(tt(e[0], w[0], w[0], ALU.mult))
                        step.step(tt(e[1], w[1], w[1], ALU.mult))
                        step.mark(tt(e[new[0]], e[0], e[1], ALU.subtract))
                        step.step(tt(e[new[1]], w[0], w[1], ALU.mult))
                        step.step(tt(e[new[1]], e[new[1]], e[new[1]], ALU.add))
                        w = [e[new[0]], e[new[1]]]
    clear(nc, s)



def phase_attend(m, layer):
    nc, io = m.nc, m.io
    with ExitStack() as ctx:
        s = semaphores(nc, ctx, COMMON + " soft_ready exp_done folded o_filled o_ready ur_ready scanned x_ready y_done y_read gelu_done")
        sb = lambda n, shape, dt=F32: ctx.enter_context(nc.sbuf_tensor(n, shape, dt))
        small = sb("small2", [P, 64])
        bu = sb("s5_bu", [P, 2, T])
        ptmp = sb("s5_ptmp", [P, 2, T])
        ur = sb("s5_ur", [P, 2, 2, T])
        z = sb("s5_z", [P, 2, T])
        vtmp = sb("s5_vtmp", [P, 2, T])
        xs = sb("s5_x", [P, 2, 2, T])
        wb = m.att_qk[:, :, :].rearrange("p r c -> p (r c)")
        e = [wb[:, k * 768:(k + 1) * 768] for k in range(3)]
        pt = [wb[:, 2304 + k * 512:2816 + k * 512] for k in range(2)]
        osb = [wb[:, 3328 + k * 256:3584 + k * 256] for k in range(2)]
        nmax, den, rden = small[:, 0:16], small[:, 16:32], small[:, 32:48]
        obanks, ybank = (m.banks[7], m.banks[2]), m.banks[6]
        N = 4 * SLOTS
        GATES_AT = (3, 7, 11, 15)
        pt_count, bu_count, at_count = {}, {}, {}

        def a_order(it):
            out = []
            if it >= 1:
                out.append(("pt", it - 1))
                if (it - 1) % 4 == 2 and it - 1 >= 4:
                    out.append(("at", (it - 1) // 4 - 1))
            if it % 2 == 0 and it // 2 < S5_BLOCKS:
                out.append(("bu", it // 2))
            return out

        block = ctx.enter_context(nc.Block())

        @block.tensor
        def _(pe):
            to_act = Banks(pe, m.banks[0:2], s.act_filled, s.act_read)
            to_vec = Banks(pe, m.banks[3:6], s.vec_filled, s.vec_read)

            def scores(it):
                r, sl = it // 4, it % 4
                rows = slice(64 * (sl % 2), 64 * (sl % 2) + 64)
                k = m.qkT[rows, (GROUPS * SLOTS + sl) // 2]
                q = [m.qkT[rows, (4 * g + sl) // 2, r * P:(r + 1) * P] for g in range(GROUPS)]
                bank = to_vec.open()
                nc.tensor.matmul(bank[:, :], q[0], k, start=True, stop=True).then_inc(s.vec_filled, 1)
                bank = to_vec.open()
                nc.tensor.matmul(bank[:, 0:P], q[1], k[:, r * P:(r + 1) * P], start=True, stop=True)
                nc.tensor.matmul(bank[:, P:2 * P], q[2], k[:, r * P:(r + 1) * P], start=True, stop=True).then_inc(s.vec_filled, 1)

            def transposed_probs(it):
                pe.wait_ge(s.folded, it + 1)
                bank = to_act.open()
                for r2 in range(4):
                    ins = nc.tensor.transpose(bank[:, r2 * P:(r2 + 1) * P], e[it % 3][:, r2 * P:(r2 + 1) * P], m.c("ident"))
                ins.then_inc(s.act_filled, 1)
                pt_count[it] = to_act.n

            def values(it):
                r, sl = it // 4, it % 4
                if sl == 0 and r >= 2:
                    pe.wait_ge(s.o_ready, r - 1)
                pe.wait_ge(s.act_read, pt_count[it])
                at = HEAD * sl
                for r2 in range(4):
                    ins = nc.tensor.matmul(obanks[r % 2][:, at:at + HEAD], pt[it % 2][:, r2 * P:(r2 + 1) * P],
                                           m.att_v[:, r2, sl * HEAD:(sl + 1) * HEAD], start=(r2 == 0), stop=(r2 == 3))
                ins.then_inc(s.o_filled, 1)

            def out_transpose(r):
                pe.wait_ge(s.o_ready, r + 1)
                bank = to_act.open()
                for k in range(2):
                    ins = nc.tensor.transpose(bank[:, k * P:(k + 1) * P], osb[r % 2][:, k * P:(k + 1) * P], m.c("ident"))
                ins.then_inc(s.act_filled, 1)
                at_count[r] = to_act.n

            def s5_input(b):
                for part in range(2):
                    bank = to_act.open()
                    nc.tensor.matmul(bank[:, :], m.s5_in[:, part, b * P:(b + 1) * P], m.uT[:, b // 4, :],
                                     start=True, stop=True).then_inc(s.act_filled, 1)
                bu_count[b] = to_act.n

            def s5_output(b):
                pe.wait_ge(s.x_ready, b + 1)
                if b == 4:
                    pe.wait_ge(s.y_read, 1)
                for part in range(2):
                    ins = nc.tensor.matmul(ybank[:, :], m.s5_out[:, part, b * P:(b + 1) * P], xs[:, b % 2, part, :],
                                           start=(b % 4 == 0 and part == 0), stop=(b % 4 == 3 and part == 1))
                ins.then_inc(s.y_done, 1)

            def beta_alpha(c):
                bank = to_vec.open()
                for k in range(KD):
                    ins = nc.tensor.matmul(bank[:, 0:2 * DN], m.hT[:, k, c * P:(c + 1) * P], m.w_ba[:, k, :],
                                           start=(k == 0), stop=(k == KD - 1))
                ins.then_inc(s.vec_filled, 1)

            scores(0)
            for it in range(N + 4):
                if it + 1 < N:
                    scores(it + 1)
                for what, n in a_order(it) if it <= N else ():
                    {"pt": transposed_probs, "at": out_transpose, "bu": s5_input}[what](n)
                if 2 <= it < N + 2:
                    values(it - 2)
                if it % 2 == 0 and 0 <= (it - 4) // 2 < S5_BLOCKS:
                    s5_output((it - 4) // 2)
                if it in GATES_AT:
                    beta_alpha(GATES_AT.index(it))
            out_transpose(3)

        @block.sync
        def _(sp):
            Panels(m, s, []).stream(sp, input_panels(io, layer, "deltanet"))

        @block.scalar
        def _(act):
            banks = Reader(act, m.banks[0:2], s.act_filled, s.act_read)

            def copy(what, n):
                bank = banks.take()
                if what == "pt":
                    if n >= 2:
                        act.wait_ge(s.o_filled, n - 1)
                    nc.scalar.activation(pt[n % 2], bank[:, :], ACT.Copy).then_inc(s.act_read, 1)
                elif what == "at":
                    nc.scalar.activation(m.aT[:, :, n::4], bank[:, 0:256].rearrange("p (k q) -> p k q", k=2),
                                         ACT.Copy).then_inc(s.act_read, 1)
                else:
                    if n >= 1:
                        act.wait_ge(s.ur_ready, n)
                    nc.scalar.activation(bu[:, 0, :], bank[:, :], ACT.Copy).then_inc(s.act_read, 1)
                    bank = banks.take()
                    nc.scalar.activation(bu[:, 1, :], bank[:, :], ACT.Copy).then_inc(s.act_read, 1)

            for it in range(N + 1):
                if it < N:
                    act.wait_ge(s.soft_ready, it + 1)
                    nc.scalar.activation(e[it % 3], e[it % 3], ACT.Exp, bias=nmax[:, it:it + 1],
                                         accum_out=den[:, it:it + 1]).then_inc(s.exp_done, 1)
                for what, n in a_order(it):
                    copy(what, n)
            copy("at", 3)
            for yt in range(2):
                act.wait_ge(s.y_read, yt + 1)
                nc.scalar.activation(m.sT[:, yt, :], m.sT[:, yt, :], ACT.Gelu_apprx_tanh).then_inc(s.gelu_done, 1)

        @block.vector
        def _(v):
            step = Link(v, s.vec_step)
            banks = Reader(v, m.banks[3:6], s.vec_filled, s.vec_read)
            tt, stt = nc.vector.tensor_tensor, nc.vector.scalar_tensor_tensor

            def soft(it):
                r, sl = it // 4, it % 4
                if it >= 3:
                    v.wait_ge(s.act_filled, pt_count[it - 3])
                bank = banks.take()
                stt(out=e[it % 3][:, 0:512], in0=m.c("dist_g0")[:, (3 - r) * P:(7 - r) * P], scalar=-float(SLOPES[sl]),
                    in1=bank[:, :], op0=ALU.mult, op1=ALU.add).then_inc(s.vec_read, 1)
                bank = banks.take()
                step.mark(stt(out=e[it % 3][:, 512:640], in0=m.c("dist_g1"), scalar=-float(SLOPES[SLOTS + sl]),
                              in1=bank[:, 0:P], op0=ALU.mult, op1=ALU.add))
                stt(out=e[it % 3][:, 640:768], in0=m.c("dist_g2"), scalar=-float(SLOPES[2 * SLOTS + sl]),
                    in1=bank[:, P:2 * P], op0=ALU.mult, op1=ALU.add).then_inc(s.vec_read, 1)
                banks.settle()
                step.settle()
                nc.vector.tensor_reduce(nmax[:, it:it + 1], e[it % 3], AX_X, ALU.max, negate=True).then_inc(s.soft_ready, 1)

            def fold(it):
                r = it // 4
                v.wait_ge(s.exp_done, it + 1)
                own = e[it % 3][:, r * P:(r + 1) * P]
                step.step(tt(own, own, e[it % 3][:, 512:640], ALU.add))
                tt(own, own, e[it % 3][:, 640:768], ALU.add).then_inc(s.folded, 1)

            def normalise(r):
                v.wait_ge(s.o_filled, 4 * r + 4)
                if r >= 2:
                    v.wait_ge(s.act_filled, at_count[r - 2])
                step.step(nc.vector.reciprocal(rden[:, 4 * r:4 * r + 4], den[:, 4 * r:4 * r + 4]))
                tt(osb[r % 2].rearrange("p (s c) -> p s c", s=4),
                   obanks[r % 2][:, 0:256].rearrange("p (s c) -> p s c", s=4),
                   over(rden[:, 4 * r:4 * r + 4].unsqueeze(2), (P, 4, HEAD)), ALU.mult).then_inc(s.o_ready, 1)

            def recur(b):
                v.wait_ge(s.ur_ready, b + 1)
                if b >= 1:
                    step.settle()
                for part in range(2):
                    nc.vector.tensor_tensor_scan(z[:, part, :], over(m.mag[:, b:b + 1], (P, T)), ur[:, b % 2, part, :],
                                                 0.0, ALU.mult, ALU.add).then_inc(s.scanned, 1)
                v.wait_ge(s.scanned, 2 * b + 2)
                cos, sin = m.rot[:, 0, b, :], m.rot[:, 1, b, :]
                if b >= 2:
                    v.wait_ge(s.y_done, b - 1)
                if b >= 1:
                    v.wait_ge(s.x_ready, b)
                step.mark(tt(vtmp[:, 0], z[:, 0], cos, ALU.mult))
                step.step(tt(vtmp[:, 1], z[:, 1], sin, ALU.mult))
                step.step(tt(xs[:, b % 2, 0], vtmp[:, 0], vtmp[:, 1], ALU.subtract))
                step.mark(tt(vtmp[:, 0], z[:, 0], sin, ALU.mult))
                step.step(tt(vtmp[:, 1], z[:, 1], cos, ALU.mult))
                tt(xs[:, b % 2, 1], vtmp[:, 0], vtmp[:, 1], ALU.add).then_inc(s.x_ready, 1)

            def skip(yt):
                v.wait_ge(s.y_done, 4 * yt + 4)
                stt(out=m.sT[:, yt, :], in0=m.uT[:, yt, :], scalar=m.s5_d[:, yt:yt + 1], in1=ybank[:, :],
                    op0=ALU.mult, op1=ALU.add).then_inc(s.y_read, 1)

            for it in range(N + 4):
                if it < N:
                    soft(it)
                if 1 <= it <= N:
                    fold(it - 1)
                if it >= 3 and (it - 3) % 4 == 3 and (it - 3) // 4 < 4:
                    normalise((it - 3) // 4)
                if it in (11, 19):
                    skip((it - 11) // 8)
                if it - 1 in GATES_AT:
                    bank = banks.take()
                    nc.vector.tensor_copy(m.ba[:, GATES_AT.index(it - 1), :], bank[:, 0:2 * DN]).then_inc(s.vec_read, 1)
                if it % 2 == 1 and 0 <= (it - 3) // 2 < S5_BLOCKS:
                    recur((it - 3) // 2)

        @block.gpsimd
        def _(pool):
            step = Link(pool, s.pool_step)
            tt = nc.gpsimd.tensor_tensor
            for b in range(S5_BLOCKS):
                cos, sin = m.rot[:, 0, b, :], m.rot[:, 1, b, :]
                pool.wait_ge(s.act_read, bu_count[b])
                if b >= 2:
                    pool.wait_ge(s.scanned, 2 * b - 2)
                if b >= 1:
                    pool.wait_ge(s.ur_ready, b)
                step.mark(tt(ptmp[:, 0], bu[:, 0], cos, ALU.mult))
                step.step(tt(ptmp[:, 1], bu[:, 1], sin, ALU.mult))
                step.step(tt(ur[:, b % 2, 0], ptmp[:, 0], ptmp[:, 1], ALU.add))
                step.mark(tt(ptmp[:, 0], bu[:, 1], cos, ALU.mult))
                step.step(tt(ptmp[:, 1], bu[:, 0], sin, ALU.mult))
                tt(ur[:, b % 2, 1], ptmp[:, 0], ptmp[:, 1], ALU.subtract).then_inc(s.ur_ready, 1)
    clear(nc, s)



JOINS = (2, 4, 8, 16, 32, 64)
CONVOLVED_AT = (0, 2, 5, 7)
VALUES_AT = 3


def phase_deltanet(m, layer):
    nc, io = m.nc, m.io
    with ExitStack() as ctx:
        s = semaphores(nc, ctx, COMMON + " conv_done silu_done sq_ready root_ready normed gate_a gate_v tri_ready expo_ready "
                       "decay_ready l_ready x_ready ct_ready vn_ready state_ready fill_filled fill_read")
        sb = lambda n, shape, dt=F32: ctx.enter_context(nc.sbuf_tensor(n, shape, dt))
        raw = sb("dn_raw", [P, 3 * DN, T + 3])
        cv = sb("dn_conv", [P, 2, T])
        sq = sb("dn_sq", [P, 2, T])
        rs = sb("dn_root", [P, 2, T])
        small = sb("small3", [P, 240])
        big = lambda n: sb(n, [P, NT, T])
        lm, at, er, xt, lt, kbg, kdec, vb = (big(n) for n in ("dn_l", "dn_at", "dn_er", "dn_xt", "dn_lt", "dn_kbg", "dn_kdec", "dn_vb"))
        ct = sb("dn_ct", [P, 2, T])
        yb = sb("dn_y", [P, 2, T])
        vn = sb("dn_vn", [P, T])
        state = sb("dn_state", [P, 2, T])
        x = lm
        heads = lambda a: a.rearrange("p (h n) -> p h n", h=DN)
        g16 = [small[:, 16 * k:16 * k + 16] for k in range(15)]
        beta, xg, na, lnp, g, gc, ngc, t3, ekd, eg, bg, gl = g16[0:12]
        ea = g16[12][:, 0:4]
        ch = lambda a: a.rearrange("p (c h) -> p c h", c=NT)
        panels = Panels(m, s, input_panels(io, layer, "deltanet"), early=RING)
        qt = lambda h, c: raw[:, h, 3 + c * P:3 + (c + 1) * P]
        kt = lambda h, c: raw[:, DN + h, 3 + c * P:3 + (c + 1) * P]
        vt = lambda h, c: raw[:, 2 * DN + h, 3 + c * P:3 + (c + 1) * P]
        hs = lambda h: slice(h * P, (h + 1) * P)
        blocks = lambda a, b, odd: a.rearrange("p (n two w) -> p n two w", two=2, w=b)[:, :, odd, :]
        raw_count, lt_count, y_count, z_count, out_count = ({} for _ in range(5))
        STEPS = len(JOINS) * NT
        BEFORE, BESIDE, IN_STEP = 2 * KD, 3, 2
        fill_end = [-(-((f + 1) * KD - BEFORE - BESIDE * NT) // IN_STEP) - 1 for f in range(2 * DN)]
        assert fill_end[2 * DN - 1] < STEPS and fill_end[DN - 1] < 2 * NT

        block = ctx.enter_context(nc.Block())

        @block.tensor
        def _(pe):
            to_act = Banks(pe, m.banks[0:3], s.act_filled, s.act_read)
            to_vec = Banks(pe, m.banks[3:6], s.vec_filled, s.vec_read)
            mm = nc.tensor.matmul

            def projection(n, mt, banks, w):
                bank = banks.open()
                for k in range(KD):
                    ins = mm(bank[:, :], w[:, k, mt * P:(mt + 1) * P], m.hT[:, k, :], start=(k == 0), stop=(k == KD - 1))
                ins.then_inc(banks.filled, 1)

            def sums(t, ready):
                pe.wait_ge(*ready)
                bank = to_act.open()
                mm(bank[:, :], m.c("ones"), sq[:, t % 2, :], start=True, stop=True).then_inc(s.act_filled, 1)

            def filling():
                for f in range(2 * DN):
                    n = 4 + f // 2
                    if f >= 2:
                        pe.wait_ge(s.fill_read, f - 1)
                    w = panel_view(panels.landed(pe, n), KD)
                    for k in range(KD):
                        ins = mm(m.banks[6 + f % 2][:, :], w[:, k, f % 2 * P:(f % 2 + 1) * P], m.hT[:, k, :], start=(k == 0), stop=(k == KD - 1))
                        if k == KD - 1:
                            ins.then_inc(s.fill_filled, 1)
                            if f % 2:
                                panels.released.append((s.fill_filled, f + 1))
                        yield

            pieces = filling()

            def fill(count):
                for _ in range(count):
                    next(pieces, None)

            for n in range(4):
                w = panel_view(panels.landed(pe, n), KD)
                projection(n, 0, to_act, w)
                raw_count[2 * n] = to_act.n
                if n == 0:
                    pe.wait_ge(s.gate_v, 2)
                    bank = to_act.open()
                    mm(bank[:, 0:16], m.c("triu"), g, start=True, stop=True).then_inc(s.act_filled, 1)
                else:
                    for t in (2 * n - 2, 2 * n - 1):
                        sums(t, (s.sq_ready, t + 1))
                projection(n, 1, to_vec, w)
                panels.released.append((s.vec_filled, to_vec.n))
                pe.wait_ge(s.tri_ready, n + 1)
                bank = to_vec.open()
                mm(bank[:, :], m.c("ones"), lt[:, n, :], start=True, stop=True).then_inc(s.vec_filled, 1)
            fill(BEFORE // 2)
            for t in (6, 7):
                sums(t, (s.sq_ready, t + 1))
            fill(BEFORE // 2)

            def transposed_l(c):
                pe.wait_ge(s.l_ready, c + 1)
                bank = to_act.open()
                for h in range(DN):
                    ins = nc.tensor.transpose(bank[:, hs(h)], lm[:, c, hs(h)], m.c("ident"))
                ins.then_inc(s.act_filled, 1)
                lt_count[c] = to_act.n

            for c in range(NT):
                pe.wait_ge(s.normed, 8)
                for a, b in ((kt, kt), (kt, qt)):
                    bank = to_vec.open()
                    for h in range(DN):
                        ins = mm(bank[:, hs(h)], a(h, c), b(h, c), start=True, stop=True)
                    ins.then_inc(s.vec_filled, 1)
                bank = to_vec.open()
                for h in range(DN):
                    ins = nc.tensor.transpose(bank[:, hs(h)], kt(h, c), m.c("ident"))
                ins.then_inc(s.vec_filled, 1)
                fill(BESIDE)
                if c:
                    transposed_l(c - 1)
            transposed_l(NT - 1)

            def join_tail(i):
                c, b = i % NT, JOINS[i // NT]
                compact = lambda bank, h: bank[:, h * P // 2:(h + 1) * P // 2].rearrange("p (n w) -> p n w", w=b)
                pe.wait_ge(s.act_read, y_count[i])
                if i < STEPS - NT:
                    bank = to_vec.open()
                    for h in range(DN):
                        ins = mm(compact(bank, h), xt[:, c, hs(h)], blocks(yb[:, i % 2, hs(h)], b, 0), start=True, stop=True)
                    ins.then_inc(s.vec_filled, 1)
                bank = to_vec.open()
                for h in range(DN):
                    ins = mm(compact(bank, h), yb[:, i % 2, hs(h)], blocks(xt[:, c, hs(h)], b, 1), start=True, stop=True)
                ins.then_inc(s.vec_filled, 1)
                z_count[i] = to_vec.n

            for i in range(STEPS):
                c = i % NT
                pe.wait_ge(s.ct_ready, i + 1)
                pe.wait_ge(s.x_ready, i + 1)
                bank = to_act.open()
                for h in range(DN):
                    ins = mm(bank[:, hs(h)], ct[:, i % 2, hs(h)], x[:, c, hs(h)], start=True, stop=True)
                ins.then_inc(s.act_filled, 1)
                y_count[i] = to_act.n
                fill(IN_STEP)
                if i:
                    join_tail(i - 1)
                if i // NT == VALUES_AT:
                    pe.wait_ge(s.silu_done, 3 * DN)
                    bank = to_act.open()
                    for h in range(DN):
                        ins = nc.tensor.transpose(bank[:, hs(h)], vt(h, c), m.c("ident"))
                    ins.then_inc(s.act_filled, 1)
            join_tail(STEPS - 1)
            for c in range(NT):
                pe.wait_ge(s.x_ready, STEPS + c + 1)
                bank = to_act.open()
                for h in range(DN):
                    ins = mm(bank[:, hs(h)], xt[:, c, hs(h)], vb[:, c, hs(h)], start=True, stop=True)
                ins.then_inc(s.act_filled, 1)
                bank = to_act.open()
                for h in range(DN):
                    ins = mm(bank[:, hs(h)], kbg[:, c, hs(h)], xt[:, c, hs(h)], start=True, stop=True)
                ins.then_inc(s.act_filled, 1)
            to_act.all_read()
            for c in range(NT):
                if c:
                    pe.wait_ge(s.state_ready, c)
                    bank = to_vec.open()
                    for h in range(DN):
                        ins = mm(bank[:, hs(h)], lt[:, c, hs(h)], state[:, (c - 1) % 2, hs(h)], start=True, stop=True)
                    ins.then_inc(s.vec_filled, 1)
                    if c == 2:
                        for o in (0, 1):
                            sums(o, (s.act_read, out_count[o]))
                    pe.wait_ge(s.vn_ready, c)
                src = lambda h: vn[:, hs(h)] if c else lm[:, 0, hs(h)]
                if c < NT - 1:
                    bank = to_vec.open()
                    for h in range(DN):
                        ins = mm(bank[:, hs(h)], kdec[:, c, hs(h)], src(h), start=True, stop=True)
                    ins.then_inc(s.vec_filled, 1)
                bank = to_act.open()
                for h in range(DN):
                    ins = mm(bank[:, hs(h)], src(h), at[:, c, hs(h)], start=True, stop=(c == 0))
                    if c:
                        ins = mm(bank[:, hs(h)], state[:, (c - 1) % 2, hs(h)], er[:, c, hs(h)], start=False, stop=True)
                ins.then_inc(s.act_filled, 1)
                out_count[c] = to_act.n
            for o in (2, 3):
                sums(o, (s.act_read, out_count[o]))

        @block.sync
        def _(sp):
            panels.stream(sp, input_panels(io, layer, "combine"))

        @block.scalar
        def _(act):
            step = Link(act, s.act_step)
            banks = Reader(act, m.banks[0:3], s.act_filled, s.act_read)
            f = nc.scalar.activation
            step.mark(f(ch(beta), m.ba[:, :, 0:DN], ACT.Sigmoid))
            act.wait_ge(s.gate_v, 1)
            step.mark(f(ea, m.a_log[:, :], ACT.Exp))
            step.step(f(lnp, na, ACT.Exp))
            f(lnp, lnp, ACT.Ln, bias=1.0).then_inc(s.gate_a, 1)

            def roots(us, scale=1.0):
                for u in us:
                    if u >= 2:
                        act.wait_ge(s.normed, u - 1)
                    bank = banks.take()
                    f(rs[:, u % 2, :], bank[:, :], ACT.Ln, bias=m.c("eps"), scale=scale).then_inc(s.act_read, 1)
                banks.settle()
                for u in us:
                    f(rs[:, u % 2, :], rs[:, u % 2, :], ACT.Exp, scale=-0.5).then_inc(s.root_ready, 1)

            def silu(t):
                act.wait_ge(s.conv_done, t + 1)
                f(raw[:, t, 3:], cv[:, t % 2, :], ACT.Silu).then_inc(s.silu_done, 1)

            def decays(c):
                act.wait_ge(s.expo_ready, c + 1)
                for h in range(DN):
                    n = 4 * c + h
                    step.mark(f(lm[:, c, hs(h)], lm[:, c, hs(h)], ACT.Exp, bias=gc[:, n:n + 1]))
                    step.mark(f(at[:, c, hs(h)], at[:, c, hs(h)], ACT.Exp, bias=ngc[:, n:n + 1]))
                step.mark(f(ekd[:, 4 * c:4 * c + 4], t3[:, 4 * c:4 * c + 4], ACT.Exp))
                f(er[:, c, :], er[:, c, :], ACT.Exp).then_inc(s.decay_ready, 1)

            def filled(k):
                act.wait_ge(s.fill_filled, k + 1)
                dst, kind = (raw[:, 2 * DN + k, 3:], ACT.Copy) if k < DN else (raw[:, k - DN, 3:], ACT.Silu)
                f(dst, m.banks[6 + k % 2][:, :], kind).then_inc(s.fill_read, 1)

            for n in range(4):
                bank = banks.take()
                f(raw[:, 2 * n, 3:], bank[:, :], ACT.Copy).then_inc(s.act_read, 1)
                if n == 0:
                    bank = banks.take()
                    step.mark(f(gc, bank[:, 0:16], ACT.Copy))
                    step.mark(f(ngc, bank[:, 0:16], ACT.Copy, scale=-1.0))
                    f(eg, bank[:, 0:16], ACT.Exp).then_inc(s.act_read, 1)
                    banks.settle()
                    step.settle()
                    act.sem_inc(s.gate_a, 1)
                else:
                    roots((2 * n - 2, 2 * n - 1))
                    decays(n - 1)
                for t in (2 * n, 2 * n + 1):
                    silu(t)
                    act.wait_ge(s.silu_done, t + 1)
                    f(sq[:, t % 2, :], raw[:, t, 3:], ACT.Square).then_inc(s.sq_ready, 1)
            filled(0)
            roots((6, 7))
            decays(3)
            filled(1)
            step.settle()
            done = 2
            for c in range(NT):
                if c:
                    bank = banks.take()
                    f(lt[:, c - 1, :], bank[:, :], ACT.Copy).then_inc(s.act_read, 1)
                if BEFORE + BESIDE * (c + 1) >= (done + 1) * KD:
                    filled(done)
                    done += 1
            bank = banks.take()
            f(lt[:, NT - 1, :], bank[:, :], ACT.Copy).then_inc(s.act_read, 1)
            for i in range(STEPS):
                lv, c = i // NT, i % NT
                bank = banks.take()
                if i >= 2:
                    act.wait_ge(s.vec_filled, z_count[i - 2])
                f(yb[:, i % 2, :], bank[:, :], ACT.Copy).then_inc(s.act_read, 1)
                if done < 2 * DN and i >= fill_end[done]:
                    filled(done)
                    done += 1
                if i - 2 in CONVOLVED_AT:
                    silu(2 * DN + CONVOLVED_AT.index(i - 2))
                if lv == VALUES_AT:
                    bank = banks.take()
                    for h in range(DN):
                        n = 4 * c + h
                        ins = f(vb[:, c, hs(h)], bank[:, hs(h)], ACT.Copy, scale=beta[:, n:n + 1])
                        if h < DN - 1:
                            step.mark(ins)
                    ins.then_inc(s.act_read, 1)
            step.settle()
            for c in range(NT):
                bank = banks.take()
                f(lm[:, c, :], bank[:, :], ACT.Copy).then_inc(s.act_read, 1)
                bank = banks.take()
                f(lt[:, c, :], bank[:, :], ACT.Copy).then_inc(s.act_read, 1)
            for c in range(NT):
                bank = banks.take()
                step.mark(f(m.bT[:, :, c * P:(c + 1) * P], heads(bank[:, :]), ACT.Copy))
                step.settle()
                f(sq[:, c % 2, :], bank[:, :], ACT.Square).then_inc(s.act_read, 1)
                if c == 1:
                    roots((8, 9), 1.0 / P)
            roots((10, 11), 1.0 / P)

        @block.vector
        def _(v):
            step = Link(v, s.vec_step)
            banks = Reader(v, m.banks[3:6], s.vec_filled, s.vec_read)
            tt, ts, stt = nc.vector.tensor_tensor, nc.vector.tensor_scalar, nc.vector.scalar_tensor_tensor
            step.mark(nc.vector.memset(raw[:, :, 0:3], 0.0))
            step.step(tt(ch(xg), m.ba[:, :, DN:2 * DN], over(m.dt_bias[:, :].unsqueeze(1), (P, NT, DN)), ALU.add))
            stt(out=na, in0=xg, scalar=-1.0, in1=xg, op0=ALU.mult, op1=ALU.min).then_inc(s.gate_v, 1)
            v.wait_ge(s.gate_a, 1)
            step.step(stt(out=xg, in0=xg, scalar=0.0, in1=lnp, op0=ALU.max, op1=ALU.add))
            stt(out=ch(g), in0=ch(xg), scalar=-1.0, in1=over(ea.unsqueeze(1), (P, NT, DN)), op0=ALU.mult, op1=ALU.mult).then_inc(s.gate_v, 1)
            v.wait_ge(s.gate_v, 2)
            for c in range(NT):
                tt(heads(lt[:, c, :]), over(m.c("triu").unsqueeze(1), (P, DN, P)),
                   over(g[:, 4 * c:4 * c + 4].unsqueeze(2), (P, DN, P)), ALU.mult).then_inc(s.tri_ready, 1)

            def conv(t):
                if t >= 2:
                    v.wait_ge(s.silu_done, t - 1)
                o = cv[:, t % 2, :]
                step.step(ts(o, raw[:, t, 0:T], m.conv_w[:, t, 0:1], None, ALU.mult))
                for k in (1, 2, 3):
                    ins = stt(out=o, in0=raw[:, t, k:k + T], scalar=m.conv_w[:, t, k:k + 1], in1=o, op0=ALU.mult, op1=ALU.add)
                    if k < 3:
                        step.step(ins)
                ins.then_inc(s.conv_done, 1)

            def exponents(c):
                bank = banks.take()
                step.mark(tt(heads(lm[:, c, :]), over(m.c("strict").unsqueeze(1), (P, DN, P)), heads(bank[:, :]), ALU.subtract))
                step.mark(tt(heads(at[:, c, :]), over(m.c("incl_t").unsqueeze(1), (P, DN, P)), heads(bank[:, :]), ALU.add))
                step.mark(tt(t3[:, 4 * c:4 * c + 4].unsqueeze(2), heads(bank[:, :])[:, :, P - 1:P], gc[:, 4 * c:4 * c + 4].unsqueeze(2), ALU.subtract))
                step.step(nc.vector.tensor_copy(er[:, c, :], bank[:, :]))
                v.sem_inc(s.vec_read, 1)
                v.sem_inc(s.expo_ready, 1)

            def unit_length(t):
                v.wait_ge(s.root_ready, t + 1)
                stt(out=raw[:, t, 3:], in0=raw[:, t, 3:], scalar=float(P) ** -0.5 if t < DN else 1.0, in1=rs[:, t % 2, :],
                    op0=ALU.mult, op1=ALU.mult).then_inc(s.normed, 1)

            for n in range(4):
                v.wait_ge(s.act_read, raw_count[2 * n])
                conv(2 * n)
                if n:
                    unit_length(2 * n - 2)
                    unit_length(2 * n - 1)
                bank = banks.take()
                nc.vector.tensor_copy(raw[:, 2 * n + 1, 3:], bank[:, :]).then_inc(s.vec_read, 1)
                banks.settle()
                conv(2 * n + 1)
                if n == 0:
                    v.wait_ge(s.gate_a, 2)
                    step.step(tt(bg, beta, eg, ALU.mult))
                exponents(n)
            unit_length(6)
            unit_length(7)

            def first_blocks(c):
                v.wait_ge(s.act_read, lt_count[c])
                step.mark(tt(heads(x[:, c, :]), heads(lm[:, c, :]), over(m.c("join1_low").unsqueeze(1), (P, DN, P)), ALU.mult))
                step.step(tt(heads(xt[:, c, :]), heads(lt[:, c, :]), over(m.c("join1").unsqueeze(1), (P, DN, P)), ALU.mult))
                step.mark(tt(heads(x[:, c, :]), over(m.c("ident").unsqueeze(1), (P, DN, P)), heads(x[:, c, :]), ALU.subtract))
                step.step(tt(heads(xt[:, c, :]), over(m.c("ident").unsqueeze(1), (P, DN, P)), heads(xt[:, c, :]), ALU.subtract))
                v.sem_inc(s.x_ready, 1)

            for c in range(NT):
                v.wait_ge(s.decay_ready, c + 1)
                bank = banks.take()
                for h in range(DN):
                    n = 4 * c + h
                    ins = stt(out=lm[:, c, hs(h)], in0=bank[:, hs(h)], scalar=beta[:, n:n + 1], in1=lm[:, c, hs(h)], op0=ALU.mult, op1=ALU.mult)
                    if h < DN - 1:
                        step.mark(ins)
                ins.then_inc(s.vec_read, 1)
                banks.settle()
                step.settle()
                v.sem_inc(s.l_ready, 1)
                step.step(nc.vector.tensor_copy(gl[:, 4 * c:4 * c + 4].unsqueeze(2), heads(er[:, c, :])[:, :, P - 1:P]))
                step.mark(tt(heads(er[:, c, :]), heads(er[:, c, :]), raw[:, 0:DN, 3 + c * P:3 + (c + 1) * P], ALU.mult))
                bank = banks.take()
                tt(at[:, c, :], at[:, c, :], bank[:, :], ALU.mult).then_inc(s.vec_read, 1)
                bank = banks.take()
                step.mark(tt(heads(kbg[:, c, :]), heads(bank[:, :]), over(bg[:, 4 * c:4 * c + 4].unsqueeze(2), (P, DN, P)), ALU.mult))
                tt(heads(kdec[:, c, :]), heads(bank[:, :]), over(ekd[:, 4 * c:4 * c + 4].unsqueeze(2), (P, DN, P)), ALU.mult).then_inc(s.vec_read, 1)
                if c:
                    first_blocks(c - 1)
            first_blocks(NT - 1)
            for i in range(STEPS):
                lv, c = i // NT, i % NT
                v.wait_ge(s.x_ready, i + 1)
                b = JOINS[lv]
                for dst in (blocks(x[:, c, :], b, 0), blocks(xt[:, c, :], b, 1))[lv == len(JOINS) - 1:]:
                    bank = banks.take()
                    tt(dst, dst, bank[:, 0:T // 2].rearrange("p (n w) -> p n w", w=b), ALU.subtract).then_inc(s.vec_read, 1)
                banks.settle()
                v.sem_inc(s.x_ready, 1)
                if i in CONVOLVED_AT:
                    t = 2 * DN + CONVOLVED_AT.index(i)
                    v.wait_ge(s.fill_read, t - 2 * DN + 1)
                    conv(t)

            def gated(c):
                u = 8 + c
                v.wait_ge(s.root_ready, u + 1)
                step.step(tt(heads(rs[:, u % 2, :]), heads(rs[:, u % 2, :]), raw[:, 0:DN, 3 + c * P:3 + (c + 1) * P], ALU.mult))
                out = m.bT[:, :, c * P:(c + 1) * P]
                stt(out=out, in0=out, scalar=m.out_gain[:, 0:1], in1=heads(rs[:, u % 2, :]), op0=ALU.mult, op1=ALU.mult).then_inc(s.normed, 1)

            v.wait_ge(s.fill_read, 2 * DN)
            for c in range(NT):
                if c:
                    bank = banks.take()
                    v.wait_ge(s.vec_read, banks.n - 1)
                    tt(vn[:, :], lm[:, c, :], bank[:, :], ALU.subtract).then_inc(s.vec_read, 1)
                    banks.settle()
                    v.sem_inc(s.vn_ready, 1)
                if c < NT - 1:
                    bank = banks.take()
                    if c == 0:
                        nc.vector.tensor_copy(state[:, 0, :], bank[:, :]).then_inc(s.vec_read, 1)
                    else:
                        for h in range(DN):
                            n = 4 * c + h
                            ins = stt(out=state[:, c % 2, hs(h)], in0=state[:, (c - 1) % 2, hs(h)], scalar=gl[:, n:n + 1], in1=bank[:, hs(h)], op0=ALU.mult, op1=ALU.add)
                            if h < DN - 1:
                                step.mark(ins)
                        ins.then_inc(s.vec_read, 1)
                    banks.settle()
                    step.settle()
                    v.sem_inc(s.state_ready, 1)
            for c in range(NT):
                gated(c)

        @block.gpsimd
        def _(pool):
            for i in range(STEPS):
                pool.wait_ge(s.act_read, lt_count[i % NT])
                if i >= 2:
                    pool.wait_ge(s.act_filled, y_count[i - 2])
                    pool.wait_ge(s.ct_ready, i - 1)
                nc.gpsimd.tensor_tensor(heads(ct[:, i % 2, :]), heads(lt[:, i % NT, :]), over(m.c(f"join{JOINS[i // NT]}").unsqueeze(1), (P, DN, P)),
                                        ALU.mult).then_inc(s.ct_ready, 1)
    clear(nc, s)



def phase_combine(m, layer):
    nc, io = m.nc, m.io
    with ExitStack() as ctx:
        s = semaphores(nc, ctx, COMMON + " out_w comb_ready")
        sb = lambda n, shape, dt=F32: ctx.enter_context(nc.sbuf_tensor(n, shape, dt))
        wa = sb("w_a", [P, 2, D])
        wb = sb("w_b", [P, 4, D])
        wv = sb("w_cv", [P, 2, D])
        wg = sb("w_cg", [P, 2, D])
        sig = sb("sig", [P, 4, 4, T])
        tmp = sb("comb_tmp", [P, 4, T])
        comb = sb("comb", [P, KD, T])
        rows = input_panels(io, layer, "combine")
        rows += [(weight(io.w_out, layer, 0, KD, n * PANEL, PANEL), KD, PANEL) for n in range(4)]
        panels = Panels(m, s, rows, early=RING)
        block = ctx.enter_context(nc.Block())

        @block.tensor
        def _(pe):
            to_act = Banks(pe, m.banks[0:3], s.act_filled, s.act_read)
            to_vec = Banks(pe, m.banks[3:6], s.vec_filled, s.vec_read)

            def product(banks, pairs, cols=slice(0, T)):
                bank = banks.open()
                for n, (a, b) in enumerate(pairs):
                    ins = nc.tensor.matmul(bank[:, cols], a, b, start=(n == 0), stop=(n == len(pairs) - 1))
                ins.then_inc(banks.filled, 1)

            for pair in range(KD // 2):
                for br in range(3):
                    w = panel_view(panels.landed(pe, 3 * pair + br), KD)
                    for half in range(2):
                        product(to_act, [(w[:, k, half * P:(half + 1) * P], m.hT[:, k, :]) for k in range(KD)])
                    panels.released.append((s.act_filled, to_act.n))
                if pair == 0:
                    pe.wait_ge(s.out_w, 16 * 4)
                for half in range(2):
                    mt = 2 * pair + half
                    cols = slice(mt * P, (mt + 1) * P)
                    product(to_act, [(wg[:, k, cols], m.sT[:, k, :]) for k in range(2)])
                    product(to_vec, [(wa[:, k, cols], m.aT[:, k, :]) for k in range(2)])
                    product(to_vec, [(wb[:, k, cols], m.bT[:, k, :]) for k in range(4)])
                    product(to_vec, [(wv[:, k, cols], m.sT[:, k, :]) for k in range(2)])
            pe.wait_ge(s.comb_ready, KD)
            for n in range(4):
                w = panel_view(panels.landed(pe, 3 * KD // 2 + n), KD)
                for t in range(NT):
                    product(to_vec, [(comb[:, k, t * P:(t + 1) * P], w[:, k, :]) for k in range(KD)], slice(0, PANEL))
                panels.released.append((s.vec_filled, to_vec.n))

        @block.sync
        def _(sp):
            panels.stream(sp)

        @block.scalar
        def _(act):
            for dst, src, kt in ((wg, io.w_c_gate, 2), (wa, io.w_a_out, 2), (wb, io.w_b_out, 4), (wv, io.w_c_val, 2)):
                act.dma_start(dst[:, :, :], weight(src, layer, 0, kt, 0, D)).then_inc(s.out_w, 16)
            banks = Reader(act, m.banks[0:3], s.act_filled, s.act_read)
            for pair in range(KD // 2):
                if pair >= 2:
                    act.wait_ge(s.comb_ready, 2 * pair - 2)
                for br, half in [(br, half) for br in range(3) for half in range(2)] + [(3, 0), (3, 1)]:
                    bank = banks.take()
                    nc.scalar.activation(sig[:, br, (2 * pair + half) % 4, :], bank[:, :], ACT.Sigmoid).then_inc(s.act_read, 1)

        @block.vector
        def _(v):
            step = Link(v, s.vec_step)
            banks = Reader(v, m.banks[3:6], s.vec_filled, s.vec_read)
            tt = nc.vector.tensor_tensor
            for mt in range(KD):
                v.wait_ge(s.act_read, 8 * (mt // 2) + 7 + mt % 2)
                if mt:
                    v.wait_ge(s.comb_ready, mt)
                for n, br in enumerate((0, 1, 3)):
                    bank = banks.take()
                    tt(tmp[:, n], sig[:, br, mt % 4, :], bank[:, :], ALU.mult).then_inc(s.vec_read, 1)
                banks.settle()
                step.mark(tt(tmp[:, 3], tmp[:, 2], sig[:, 2, mt % 4, :], ALU.mult))
                step.step(tt(tmp[:, 0], tmp[:, 0], tmp[:, 1], ALU.add))
                tt(comb[:, mt, :], tmp[:, 0], tmp[:, 3], ALU.add).then_inc(s.comb_ready, 1)
            for n in range(4):
                for t in range(NT):
                    bank = banks.take()
                    xs = m.x[:, t, n * PANEL:(n + 1) * PANEL]
                    tt(xs, xs, bank[:, 0:PANEL], ALU.add).then_inc(s.vec_read, 1)
    clear(nc, s)



RINGS = 8
PAIRS = PEER_HEADS // 2
TURN = 2 * TOPK
LEAST = -3e38


def phase_peer(m, layer):
    nc, io = m.nc, m.io
    with ExitStack() as ctx:
        s = semaphores(nc, ctx, COMMON + " rms_ready h_ready queries_in panel_in query_filled query_here score_filled scores_here paced_sp "
                       "ple_in p_here tile_done ple_rms ple_h turned ple_hT half_filled sig_ready ple_added "
                       "topped exp_done selected u_free v_free out_free tanh_in tanh_done w_ready dg_done idx_here paced paced_v")
        sb = lambda n, shape, dt=F32: ctx.enter_context(nc.sbuf_tensor(n, shape, dt))
        u = sb("u_rows", [P, RINGS, D])
        vr = sb("v_rows", [P, RINGS, D])
        dg = sb("dg", [P, RINGS, P])
        h = sb("h", [P, NT, D])
        first = sb("query_memory", [P, KD * T + KD * 4 * P + 4 * T])
        hT = first[:, 0:KD * T].rearrange("p (k n) -> p k n", k=KD)
        panel = first[:, KD * T:2 * KD * T].rearrange("p (k c) -> p k c", k=KD)
        qry = first[:, 2 * KD * T:].rearrange("p (c n) -> p c n", c=4)
        w_gate = first[:, 0:KD * D].rearrange("p (k d) -> p k d", k=KD)
        w_ple = first[:, KD * D:].rearrange("p (k d) -> p k d", k=2)
        m.hT = hT
        hcur = sb("h_tile", [P, D])
        small = sb("small5", [P, 16])
        ss, rms, rstd = small[:, 0:4], small[:, 4:8], small[:, 8:12]
        keys = sb("keys", [P, 4, KEYS])
        scores = sb("scores", [P, PAIRS * NT, 4, KEYS])
        sc = sb("sel_s", [P, 2, KEYS])
        sc2 = sb("sel_s2", [P, 2, KEYS])
        val = sb("sel_v", [P, 2, TOPK])
        vi = sb("sel_i", [P, 2, TOPK], U32)
        vif = sb("sel_if", [P, 2, TOPK])
        cand = sb("sel_c", [P, TOPK, TOPK])
        cand2 = sb("sel_c2", [P, TOPK, TOPK])
        top = sb("sel_top", [P, TOPK])
        pos = sb("sel_pos", [P, TOPK], U32)
        ab = sb("sel_ab", [P, 2, TOPK], U32)
        abf = sb("sel_abf", [P, 2, TOPK])
        hit = sb("sel_hit", [P, 2 * TOPK, TOPK])
        chosen = sb("sel_ch", [P, 2, TOPK])
        expo = sb("sel_e", [P, TOPK])
        one = sb("sel_one", [P, 8])
        idx_all = sb("idx_all", [P, NT * PEER_HEADS * TOPK], U32)
        gate_all = sb("gate_all", [P, NT * PEER_HEADS * TOPK])
        idx = [sb(f"idx{k}", [P, TOPK], U32) for k in range(2)]
        act_u = sb("act_u", [P, TURN])
        inner = sb("act_in", [P, TURN])
        th = sb("act_th", [P, TURN])
        w = sb("act_w", [P, TURN])
        gain = u[:, 0, :]
        by_turn = scores[:, :, :, :].rearrange("p b c k -> p (b c k)")
        pT = by_turn[:, 0:2 * T].rearrange("p (k n) -> p k n", k=2)
        ple_gain, ple_h, ple_hT, sig = (by_turn[:, k * D:(k + 1) * D] for k in range(1, 5))
        p_tile = by_turn[:, 5 * D:5 * D + 2 * P]
        assert 5 * D + 2 * P <= (PAIRS - 1) * NT * 4 * KEYS and 2 * T == D
        hflat = h[:, :, :].rearrange("p t d -> p (t d)")
        xflat = m.x[:, :, :].rearrange("p t d -> p (t d)")
        tables = io.peer_u.rearrange("l e d -> (l e) d"), io.peer_v.rearrange("l e d -> (l e) d")
        out_banks = [(m.banks[4], m.banks[5]), (m.banks[6], m.banks[7])]

        def turns(eng, turn):
            last = PAIRS - 1
            with eng.Fori(0, last) as pair:
                with eng.Fori(0, NT) as t:
                    turn(t, pair * NT + t, pair=pair, project=True)
            turn(0, last * NT)
            with eng.Fori(1, NT - 1) as t:
                turn(t, last * NT + t, embed=True)
            turn(NT - 1, PAIRS * NT - 1, choose_next=False, embed=True)

        def landed(eng, sems, b, n):
            uses = (layer * (NT * PAIRS) + b) * (TURN // RINGS) + (n // RINGS + 1)
            eng.wait_ge(sems[n % RINGS], uses * 16)

        block = ctx.enter_context(nc.Block())

        @block.gpsimd
        def _(pool):
            pool.sem_inc(s.u_free, RINGS)
            pool.sem_inc(s.v_free, RINGS)
            pool.sem_inc(s.out_free, 2)

            def paced():
                pool.sem_inc(s.paced, 1)

            def turn(t, b, pair=None, project=False, choose_next=True, embed=False):
                for hh in range(2):
                    pool.wait_ge(s.selected, b * 2 + (hh + 1))
                    paced()
                    nc.gpsimd.tensor_copy(idx[hh][:, :], idx_all[:, bass.ds((b * 2 + hh) * TOPK, TOPK)]).then_inc(s.idx_here, 1)
                    pool.wait_ge(s.idx_here, b * 2 + (hh + 1))
                    paced()
                    for g in range(TOPK // RINGS):
                        for free, rows, table, sems in ((s.u_free, u, tables[0], m.u_landed), (s.v_free, vr, tables[1], m.v_landed)):
                            for k in range(RINGS):
                                n = hh * TOPK + g * RINGS + k
                                pool.wait_ge(free, b * TURN + (n + 1))
                                paced()
                                nc.gpsimd.indirect_dma_start(
                                    out=rows[:, k, :], out_offset=None, in_=table,
                                    in_offset=bass.IndirectOffsetOnAxis(ap=idx[hh][:, g * RINGS + k:g * RINGS + k + 1], axis=0),
                                ).then_inc(sems[k], 16)

            turns(pool, turn)

        @block.sync
        def _(sp):
            sp.dma_start(gain, io.norm_ffn[bass.ds(layer, 1), :].partition_broadcast(P).rearrange("p l d -> p (l d)")).then_inc(s.params_in, 16)
            sp.dma_start(panel[:, :, :], weight(io.peer_w_query, layer, 0, KD, 0, 4 * P)).then_inc(s.queries_in, 16)
            for n, a in enumerate((io.peer_keys1, io.peer_keys2) * 2):
                sp.dma_start(keys[:, n, :], a[bass.ds(layer, 1)].rearrange("l d k -> d (l k)")).then_inc(s.queries_in, 16)
            sp.wait_ge(s.act_filled, NT + 1)
            sp.sem_inc(s.query_filled, 1)
            with sp.Fori(0, (PAIRS - 1) * NT) as b:
                sp.wait_ge(s.query_filled, b + 1)
                sp.sem_inc(s.paced_sp, 1)
                src = io.peer_w_query[bass.ds(layer, 1), :, bass.ds(b * P + 4 * P, P)].rearrange("l (k p) c -> p (l k) c", p=P)
                sp.dma_start(panel[:, :, 0:P], src).then_inc(s.panel_in, 16)
            chunks = (PAIRS - 1) * NT
            sp.wait_ge(s.query_filled, 1 + chunks)
            sp.dma_start(w_gate, weight(io.ple_w_gate, layer, 0, KD, 0, D)).then_inc(s.ple_in, 16)
            sp.wait_ge(s.score_filled, chunks)
            sp.dma_start(w_ple, weight(io.ple_w, layer, 0, 2, 0, D)).then_inc(s.ple_in, 16)
            sp.wait_ge(s.selected, 2 * chunks)
            sp.dma_start(pT, weight(io.p, layer, 0, 2, 0, T)).then_inc(s.ple_in, 16)
            sp.dma_start(ple_gain, io.ple_norm[bass.ds(layer, 1), :].partition_broadcast(P).rearrange("p l d -> p (l d)")).then_inc(s.ple_in, 16)

        @block.vector
        def _(v):
            step = Link(v, s.vec_step)
            banks = Reader(v, m.banks[2:4], s.vec_filled, s.vec_read)
            tt, ts, stt = nc.vector.tensor_tensor, nc.vector.tensor_scalar, nc.vector.scalar_tensor_tensor

            def choose(j):
                step.step(nc.vector.tensor_copy(sc[:, :, :].rearrange("p a k -> p (a k)"), by_turn[:, bass.ds(j * 2 * KEYS, 2 * KEYS)]))
                for half in range(2):
                    step.mark(nc.vector.max(val[:, half, 0:8], sc[:, half, :]))
                step.settle()
                for half in range(2):
                    step.mark(nc.vector.max_index(vi[:, half, 0:8], val[:, half, 0:8], sc[:, half, :]))
                    step.mark(nc.vector.match_replace(sc2[:, half, :], val[:, half, 0:8], sc[:, half, :], LEAST))
                step.settle()
                for half in range(2):
                    step.mark(nc.vector.max(val[:, half, 8:16], sc2[:, half, :]))
                step.settle()
                for half in range(2):
                    step.mark(nc.vector.max_index(vi[:, half, 8:16], val[:, half, 8:16], sc2[:, half, :]))
                step.mark(tt(cand[:, :, :], over(val[:, 0, :].unsqueeze(2), (P, TOPK, TOPK)), over(val[:, 1, :].unsqueeze(1), (P, TOPK, TOPK)), ALU.add))
                step.settle()
                cf, cf2 = (a[:, :, :].rearrange("p a b -> p (a b)") for a in (cand, cand2))
                step.mark(nc.vector.tensor_copy(vif[:, :, :], vi[:, :, :]))
                step.step(nc.vector.max(top[:, 0:8], cf))
                step.mark(ts(one[:, 0:1], top[:, 0:1], -1.0, None, ALU.mult))
                step.mark(nc.vector.max_index(pos[:, 0:8], top[:, 0:8], cf))
                step.step(nc.vector.match_replace(cf2, top[:, 0:8], cf, LEAST))
                nc.vector.max(top[:, 8:16], cf2).then_inc(s.topped, 1)
                v.wait_ge(s.topped, j + 1)
                v.sem_inc(s.paced_v, 1)
                step.step(nc.vector.max_index(pos[:, 8:16], top[:, 8:16], cf2))
                step.mark(ts(ab[:, 0, :], pos[:, :], 4, None, ALU.logical_shift_right))
                step.step(ts(ab[:, 1, :], pos[:, :], 15, None, ALU.bitwise_and))
                step.step(nc.vector.tensor_copy(abf[:, :, :], ab[:, :, :]))
                step.step(tt(hit[:, :, :], over(abf[:, :, :].rearrange("p a k -> p (a k)").unsqueeze(2), (P, 2 * TOPK, TOPK)),
                             over(m.c("iota").unsqueeze(1), (P, 2 * TOPK, TOPK)), ALU.is_equal))
                h4 = hit[:, :, :].rearrange("p (a k) n -> p a k n", a=2)
                step.step(tt(h4, h4, over(vif[:, :, :].unsqueeze(2), (P, 2, TOPK, TOPK)), ALU.mult))
                step.step(nc.vector.tensor_reduce(chosen[:, :, :].rearrange("p a k -> p (a k)"), hit[:, :, :], AX_X, ALU.add))
                step.step(stt(out=chosen[:, 0, :], in0=chosen[:, 0, :], scalar=float(KEYS), in1=chosen[:, 1, :], op0=ALU.mult, op1=ALU.add))
                step.mark(ts(idx_all[:, bass.ds(j * TOPK, TOPK)], chosen[:, 0, :], m.row_base[:, 0:1], None, ALU.add))
                v.wait_ge(s.exp_done, j + 1)
                step.step(nc.vector.reciprocal(one[:, 2:3], one[:, 1:2]))
                step.step(ts(gate_all[:, bass.ds(j * TOPK, TOPK)], expo[:, :], one[:, 2:3], None, ALU.mult))
                v.sem_inc(s.selected, 1)
                step.restart()

            def group(b, g):
                at = slice(g * RINGS, (g + 1) * RINGS)
                for k in range(RINGS):
                    n = g * RINGS + k
                    landed(v, m.u_landed, b, n)
                    nc.vector.tensor_tensor_reduce(out=u[:, k, :], in0=u[:, k, :], in1=hcur[:, :], scale=1.0, scalar=0.0,
                                                   op0=ALU.mult, op1=ALU.add, accum_out=act_u[:, n:n + 1]).then_inc(s.u_free, 1)
                v.wait_ge(s.u_free, b * TURN + ((g + 2) * RINGS))
                step.step(tt(inner[:, at], act_u[:, at], act_u[:, at], ALU.mult))
                step.step(ts(inner[:, at], inner[:, at], 0.044715, 1.0, ALU.mult, ALU.add))
                tt(inner[:, at], inner[:, at], act_u[:, at], ALU.mult).then_inc(s.tanh_in, 1)
                v.wait_ge(s.tanh_done, b * 4 + (g + 1))
                step.step(stt(out=th[:, at], in0=th[:, at], scalar=1.0, in1=act_u[:, at], op0=ALU.add, op1=ALU.mult))
                stt(out=w[:, at], in0=th[:, at], scalar=0.5, in1=gate_all[:, bass.ds((b * 4 + g) * RINGS, RINGS)],
                    op0=ALU.mult, op1=ALU.mult).then_inc(s.w_ready, 1)

            def add_out(t, b, hh):
                v.wait_ge(s.v_free, b * TURN + (RINGS + TOPK * (hh + 1)))
                v.sem_inc(s.paced_v, 1)
                for half in range(2):
                    xs = xflat[:, bass.ds(t * D + half * 512, 512)]
                    step.mark(tt(xs, xs, out_banks[hh][half][:, :], ALU.add))
                step.settle()
                v.sem_inc(s.out_free, 1)

            def turn(t, b, pair=None, project=False, choose_next=True, embed=False):
                step.step(nc.vector.tensor_copy(hcur[:, :], hflat[:, bass.ds(t * D, D)]))
                group(b, 0)
                if embed:
                    normalised(t - 1)
                group(b, 1)
                step.restart()
                if project:
                    v.wait_ge(s.scores_here, b + 1)
                    v.sem_inc(s.paced_v, 1)
                if choose_next:
                    choose(b * 2 + 2)
                group(b, 2)
                add_out(t, b, 0)
                group(b, 3)
                step.restart()
                if project:
                    v.wait_ge(s.scores_here, b + 2)
                    v.sem_inc(s.paced_v, 1)
                if choose_next:
                    choose(b * 2 + 3)
                if embed:
                    embedded(t - 1)
                add_out(t, b, 1)
                if not project:
                    v.sem_inc(s.tile_done, 1)
                step.restart()

            def normalised(e):
                v.wait_ge(s.ple_in, 16 * 4)
                v.wait_ge(s.ple_rms, e + 1)
                v.sem_inc(s.paced_v, 1)
                step.step(nc.vector.reciprocal(small[:, 14:15], small[:, 13:14]))
                stt(out=ple_h, in0=xflat[:, bass.ds(e * D, D)], scalar=small[:, 14:15], in1=ple_gain,
                    op0=ALU.mult, op1=ALU.mult).then_inc(s.ple_h, 1)

            def embedded(e):
                for half in range(2):
                    v.wait_ge(s.sig_ready, e * 2 + (half + 2))
                    v.sem_inc(s.paced_v, 1)
                    part = sig[:, half * 512:half * 512 + 512]
                    step.step(tt(part, part, m.banks[2 + half][:, :], ALU.mult))
                    xs = xflat[:, bass.ds(e * D + half * 512, 512)]
                    step.step(tt(xs, xs, part, ALU.add))
                    v.sem_inc(s.ple_added, 1)

            v.sem_inc(s.ple_added, 1)
            v.wait_ge(s.params_in, 16)
            norm_vector(m, s, v, step, rms, rstd, gain, h)
            norm_copy(m, v, banks, 1)
            for head in range(2):
                c = 2 * head + 1
                bank = banks.take()
                nc.vector.tensor_copy(qry[:, c, :], bank[:, :]).then_inc(s.vec_read, 1)
                bank = banks.take()
                nc.vector.tensor_copy(scores[:, 0:NT, c, :], bank[:, :].rearrange("p (t k) -> p t k", t=NT)).then_inc(s.vec_read, 1)
                banks.settle()
                v.wait_ge(s.act_read, banks.n)
                step.restart()
                choose(head)
            turns(v, turn)
            normalised(NT - 1)
            embedded(NT - 1)
            step.step(ts(m.row_base[:, :], m.row_base[:, :], float(EXPERTS), None, ALU.add))

        @block.scalar
        def _(act):
            def weigh(j):
                act.wait_ge(s.topped, j + 1)
                nc.scalar.activation(expo[:, :], top[:, :], ACT.Exp, bias=one[:, 0:1], accum_out=one[:, 1:2]).then_inc(s.exp_done, 1)

            def group(b, g):
                at = slice(g * RINGS, (g + 1) * RINGS)
                act.wait_ge(s.tanh_in, b * 4 + (g + 1))
                nc.scalar.activation(th[:, at], inner[:, at], ACT.Tanh, scale=0.7978845608028654).then_inc(s.tanh_done, 1)
                act.wait_ge(s.w_ready, b * 4 + (g + 1))
                for k in range(RINGS):
                    n = g * RINGS + k
                    act.wait_ge(s.v_free, b * TURN + (n + 1))
                    nc.scalar.activation(dg[:, k, :], m.c("ident"), ACT.Copy, scale=w[:, n:n + 1]).then_inc(s.dg_done, 1)

            def turn(t, b, pair=None, project=False, choose_next=True, embed=False):
                if project:
                    act.wait_ge(s.query_filled, b + 2)
                    nc.scalar.activation(qry[:, 0, :], m.banks[0][:, :], ACT.Copy).then_inc(s.query_here, 1)
                if embed:
                    squares(t - 1)
                group(b, 0)
                if embed:
                    turned(t - 1)
                group(b, 1)
                if project:
                    act.wait_ge(s.score_filled, b + 1)
                    nc.scalar.activation(scores[:, bass.ds(pair * NT + NT, NT), bass.ds(t, 1), :].rearrange("p b c k -> p b (c k)"),
                                         m.banks[2][:, :].rearrange("p (t k) -> p t k", t=NT), ACT.Copy).then_inc(s.scores_here, 1)
                if choose_next:
                    weigh(b * 2 + 2)
                group(b, 2)
                if embed:
                    gated(t - 1, 0)
                group(b, 3)
                if choose_next:
                    weigh(b * 2 + 3)
                if embed:
                    gated(t - 1, 1)

            def squares(e):
                act.wait_ge(s.ple_in, 16 * 4)
                nc.scalar.activation(p_tile.rearrange("p (k n) -> p k n", k=2), pT[:, :, bass.ds(e * P, P)], ACT.Copy).then_inc(s.p_here, 1)
                act.wait_ge(s.tile_done, e + 1)
                nc.scalar.activation(ple_h, xflat[:, bass.ds(e * D, D)], ACT.Square, accum_out=small[:, 12:13]).then_inc(s.act_step, 1)
                act.wait_ge(s.act_step, 1)
                act.sem_clear(s.act_step)
                nc.scalar.activation(small[:, 13:14], small[:, 12:13], ACT.Sqrt, bias=m.c("eps"), scale=1.0 / D).then_inc(s.ple_rms, 1)

            def turned(e):
                act.wait_ge(s.turned, e + 1)
                for half in range(2):
                    nc.scalar.activation(ple_hT[:, half * 512:half * 512 + 512], m.banks[half][:, :], ACT.Copy).then_inc(s.ple_hT, 1)

            def gated(e, half):
                act.wait_ge(s.half_filled, e * 2 + (half + 1))
                nc.scalar.activation(sig[:, half * 512:half * 512 + 512], m.banks[half][:, :], ACT.Sigmoid).then_inc(s.sig_ready, 1)

            step = Link(act, s.act_step)
            banks = Reader(act, m.banks[0:2], s.act_filled, s.act_read)
            norm_scalar(m, s, act, step, ss, rms, h)
            norm_copy(m, act, banks, 0)
            for head in range(2):
                c = 2 * head
                bank = banks.take()
                nc.scalar.activation(qry[:, c, :], bank[:, :], ACT.Copy).then_inc(s.act_read, 1)
                bank = banks.take()
                nc.scalar.activation(scores[:, 0:NT, c, :], bank[:, :].rearrange("p (t k) -> p t k", t=NT), ACT.Copy).then_inc(s.act_read, 1)
                if head:
                    banks.settle()
                    act.sem_inc(s.scores_here, 1)
                weigh(head)
            step.restart()
            act.sem_inc(s.sig_ready, 1)
            turns(act, turn)
            squares(NT - 1)
            turned(NT - 1)
            gated(NT - 1, 0)
            gated(NT - 1, 1)

        @block.tensor
        def _(pe):
            to_act = Banks(pe, m.banks[0:2], s.act_filled, s.act_read)
            to_vec = Banks(pe, m.banks[2:4], s.vec_filled, s.vec_read)
            norm_transposes(m, s, pe, to_act, to_vec, h)
            pe.wait_ge(s.queries_in, 16 * 5)
            for head in range(2):
                chunks = ((2 * head, to_act), (2 * head + 1, to_vec))
                for c, banks in chunks:
                    bank = banks.open()
                    for k in range(KD):
                        ins = nc.tensor.matmul(bank[:, :], panel[:, k, c * P:(c + 1) * P], hT[:, k, :], start=(k == 0), stop=(k == KD - 1))
                    ins.then_inc(banks.filled, 1)
                for c, banks in chunks:
                    banks.all_read()
                    bank = banks.open()
                    for t in range(NT):
                        ins = nc.tensor.matmul(bank[:, t * KEYS:(t + 1) * KEYS], qry[:, c, t * P:(t + 1) * P], keys[:, c, :], start=True, stop=True)
                    ins.then_inc(banks.filled, 1)
            to_act.all_read()
            to_vec.all_read()

            def queries(b):
                pe.wait_ge(s.panel_in, b * 16 + 16)
                pe.wait_ge(s.scores_here, b + 1)
                for k in range(KD):
                    ins = nc.tensor.matmul(m.banks[0][:, :], panel[:, k, 0:P], hT[:, k, :], start=(k == 0), stop=(k == KD - 1))
                ins.then_inc(s.query_filled, 1)

            def score(b, t_chunk):
                pe.wait_ge(s.query_here, b + 1)
                half_keys = keys[:, :, :].rearrange("p c k -> p (c k)")[:, bass.ds(t_chunk * KEYS, KEYS)]
                for t in range(NT):
                    ins = nc.tensor.matmul(m.banks[2][:, t * KEYS:(t + 1) * KEYS], qry[:, 0, t * P:(t + 1) * P], half_keys, start=True, stop=True)
                ins.then_inc(s.score_filled, 1)

            def turn(t, b, pair=None, project=False, choose_next=True, embed=False):
                if project:
                    queries(b)
                for hh in range(2):
                    pe.wait_ge(s.out_free, b * 2 + (hh + 1))
                    for i in range(TOPK):
                        n = hh * TOPK + i
                        if project and n == RINGS:
                            score(b, t)
                        if embed and n == RINGS:
                            turn_over(t - 1)
                        if embed and n in (2 * RINGS, 3 * RINGS):
                            gate(t - 1, n // RINGS - 2)
                        landed(pe, m.v_landed, b, n)
                        pe.wait_ge(s.dg_done, b * TURN + (n + 1))
                        for half in range(2):
                            ins = nc.tensor.matmul(out_banks[hh][half][:, :], dg[:, n % RINGS, :], vr[:, n % RINGS, half * 512:half * 512 + 512],
                                                   start=(i == 0), stop=(i == TOPK - 1))
                        ins.then_inc(s.v_free, 1)

            def turn_over(e):
                pe.wait_ge(s.ple_in, 16 * 4)
                pe.wait_ge(s.ple_added, e * 2 + 1)
                pe.wait_ge(s.p_here, e + 1)
                for half in range(2):
                    for k in range(2):
                        nc.tensor.matmul(m.banks[2 + half][:, :], p_tile[:, k * P:(k + 1) * P], w_ple[:, k, half * 512:half * 512 + 512],
                                         start=(k == 0), stop=(k == 1))
                pe.wait_ge(s.ple_h, e + 1)
                pe.wait_ge(s.sig_ready, e * 2 + 1)
                for k in range(KD):
                    ins = nc.tensor.transpose(m.banks[k // 4][:, k % 4 * P:(k % 4 + 1) * P], ple_h[:, k * P:(k + 1) * P], m.c("ident"))
                ins.then_inc(s.turned, 1)

            def gate(e, half):
                pe.wait_ge(s.ple_hT, e * 2 + 2)
                cols = slice(half * 512, half * 512 + 512)
                for k in range(KD):
                    ins = nc.tensor.matmul(m.banks[half][:, :], ple_hT[:, k * P:(k + 1) * P], w_gate[:, k, cols], start=(k == 0), stop=(k == KD - 1))
                ins.then_inc(s.half_filled, 1)

            turns(pe, turn)
            turn_over(NT - 1)
            gate(NT - 1, 0)
            gate(NT - 1, 1)
    clear(nc, s)


def decoder_trunk(nc, io):
    with ExitStack() as ctx:
        sb = lambda n, shape, dt=F32: ctx.enter_context(nc.sbuf_tensor(n, shape, dt))
        once = semaphores(nc, ctx, "loaded stored")
        swdge = [ctx.enter_context(nc.semaphore(f"{n}_landed{k}")) for n in "uv" for k in range(RINGS)]
        m = Machine()
        m.nc, m.io, m.u_landed, m.v_landed = nc, io, swdge[:RINGS], swdge[RINGS:]
        m.banks = [ctx.enter_context(nc.psum_tensor(f"bank{k}", [P, 512], F32)) for k in range(8)]
        consts = sb("consts", [P, CONSTS.shape[1]])
        m.c = lambda name: consts[:, WHERE[name][0]:WHERE[name][0] + WHERE[name][1]]
        m.x = sb("x", [P, NT, D])
        m.row_base = sb("row_base", [P, 1])

        with nc.Block() as block:
            @block.sync
            def _(sp):
                sp.dma_start(consts[:, :], io.consts).then_inc(once.loaded, 16)
                sp.dma_start(m.x[:, :, :], io.x.rearrange("b (t p) d -> p (b t) d", p=P)).then_inc(once.loaded, 16)
                sp.wait_ge(once.loaded, 32)

            @block.vector
            def _(v):
                nc.vector.memset(m.row_base[:, :], 0.0)

        with nc.Fori(0, DEPTH) as layer:
            with ExitStack() as mix:
                sm = lambda n, shape, dt=F32: mix.enter_context(nc.sbuf_tensor(n, shape, dt))
                m.hT = sm("hT", [P, KD, T])
                ring = sm("ring", [P, RING, KD * PANEL])
                m.ring = ring
                m.aT = sm("aT", [P, 2, T])
                m.sT = sm("sT", [P, 2, T])
                m.ba = sm("ba", [P, NT, 2 * DN])
                m.w_ba = sm("w_ba", [P, KD, 2 * DN])
                m.conv_w = sm("conv_w", [P, 3 * DN, 4])
                m.a_log = sm("a_log", [P, DN])
                m.dt_bias = sm("dt_bias", [P, DN])
                m.out_gain = sm("out_gain", [P, 1])
                with ExitStack() as front:
                    sf = lambda n, shape, dt=F32: front.enter_context(nc.sbuf_tensor(n, shape, dt))
                    m.work_a = sf("work_a", [P, NT * D])
                    m.qkT = m.work_a[:, :].rearrange("p (b n) -> p b n", b=8)
                    m.att_qk = sf("att_qk", [P, 4, QK_HEADS * HEAD])
                    m.att_v = sf("att_v", [P, 4, SLOTS * HEAD])
                    m.uT = sf("uT", [P, 2, T])
                    m.rot = sf("rot", [P, 2, 8, T])
                    m.s5_in = sf("s5_in", [P, 2, 8 * P])
                    m.s5_out = sf("s5_out", [P, 2, 8 * P])
                    m.s5_d = sf("s5_d", [P, 2])
                    m.mag = sf("mag", [P, 8])
                    m.seed = sf("seed", [P, 2, 8])
                    phase_project(m, layer)
                    phase_attend(m, layer)
                m.bT = sm("bT", [P, DN, T])
                phase_deltanet(m, layer)
                phase_combine(m, layer)
            phase_peer(m, layer)
        with nc.Block() as block:
            @block.sync
            def _(sp):
                sp.dma_start(io.out.rearrange("b (t p) d -> p (b t) d", p=P), m.x[:, :, :]).then_inc(once.stored, 16)
                sp.wait_ge(once.stored, 16)


def kernel(**inputs):
    import concourse.bacc as bacc
    from concourse.bass_utils import run_bass_kernel_spmd

    a = {k: np.asarray(v) for k, v in inputs.items()}
    n = DEPTH
    swap = lambda t: np.ascontiguousarray(np.swapaxes(t, -1, -2))
    a["dn_conv"] = np.ascontiguousarray(a["dn_conv"].reshape(n, 4, 3 * DN, P).transpose(0, 3, 2, 1))
    a["s5_a_re"] = swap(a["s5_a_re"].reshape(n, S5_BLOCKS, P))
    a["s5_a_im"] = swap(a["s5_a_im"].reshape(n, S5_BLOCKS, P))
    a["s5_b_re"] = a["s5_b_re"].reshape(n, S5_BLOCKS * P, 16)
    a["s5_b_im"] = a["s5_b_im"].reshape(n, S5_BLOCKS * P, 16)
    a["s5_c_re"] = swap(a["s5_c_re"]).reshape(n, S5_BLOCKS * P, 16)
    a["s5_c_im"] = swap(a["s5_c_im"]).reshape(n, S5_BLOCKS * P, 16)
    a["s5_d"] = swap(a["s5_d"].reshape(n, 2, P))
    a["s5_log_dt"] = swap(a["s5_log_dt"].reshape(n, S5_BLOCKS, 2))
    a["dn_out_gain"] = a["dn_out_gain"].reshape(n, P, 1)
    a["peer_keys1"] = swap(a["peer_keys1"])
    a["peer_keys2"] = swap(a["peer_keys2"])
    a["p"] = swap(a["p"].reshape(n, T, PLE))
    a["consts"] = CONSTS
    nc = bacc.Bacc("TRN2", target_bir_lowering=False, num_devices=1)
    arrays, aps = {}, {}
    for name, t in a.items():
        t = np.ascontiguousarray(t)
        arrays[f"in_{name}"] = t
        aps[name] = nc.dram_tensor(f"in_{name}", t.shape, mybir.dt.from_np(t.dtype), kind="ExternalInput").ap()
    aps["out"] = nc.dram_tensor("out_x", (1, T, D), F32, kind="ExternalOutput").ap()
    io = namedtuple("Arrays", list(aps))(*aps.values())
    decoder_trunk(nc, io)
    got = run_bass_kernel_spmd(nc, [arrays], core_ids=[0])
    return got.results[0]["out_x"]
```
